# Optimizing a Trainium2 kernel written in Bass

```python
import jax, jax.numpy as jnp
from jax import lax
import numpy as np
import jax
import jax.numpy as jnp

D_MODEL = 1024
BATCH = 1
SEQ = 256
DEPTH = 2

CONV_DIM = 512
CONV_WIDTH = 3
RET_HEADS = 4
RET_HEAD_DIM = 128
RET_DIM = RET_HEADS * RET_HEAD_DIM
GLA_HEADS = 4
GLA_KEY_HEAD_DIM = 64
GLA_VAL_HEAD_DIM = 128
GLA_KEY_DIM = GLA_HEADS * GLA_KEY_HEAD_DIM
GLA_VAL_DIM = GLA_HEADS * GLA_VAL_HEAD_DIM
GLA_GATE_RANK = 16
GLA_GATE_TAU = 16.0
N_BRANCHES = 3
CHUNK = 64
D_FF = (((8 * D_MODEL + 2) // 3 + 255) // 256) * 256
ROPE_BASE = 10000.0
EPS = 1e-6
IN_COLS = 3 * CONV_DIM + 4 * RET_DIM + 2 * GLA_KEY_DIM + 2 * GLA_VAL_DIM + GLA_GATE_RANK + N_BRANCHES * D_MODEL


def rms_norm(x, w):
    xf = x.astype(jnp.float32)
    y = xf * lax.rsqrt(jnp.mean(xf * xf, axis=-1, keepdims=True) + EPS)
    return (y * w.astype(jnp.float32)).astype(x.dtype)

def head_norm(y, w, center):
    b, t, h, d = y.shape
    if center:
        y = y - jnp.mean(y, axis=-1, keepdims=True)
    y = y * lax.rsqrt(jnp.mean(y * y, axis=-1, keepdims=True) + EPS)
    return y.reshape(b, t, h * d) * w.astype(jnp.float32)

def rotary(x, positions):
    half = x.shape[-1] // 2
    inv_freq = ROPE_BASE ** (-jnp.arange(half, dtype=jnp.float32) / half)
    ang = positions.astype(jnp.float32)[..., None] * inv_freq
    cos = jnp.cos(ang)[:, :, None, :]
    sin = jnp.sin(ang)[:, :, None, :]
    x1, x2 = x[..., :half], x[..., half:]
    return jnp.concatenate([x1 * cos - x2 * sin, x2 * cos + x1 * sin], axis=-1)

def to_chunks(x):
    b, t, h, d = x.shape
    return x.reshape(b, t // CHUNK, CHUNK, h, d).transpose(1, 0, 3, 2, 4)

def from_chunks(x):
    nc, b, h, c, d = x.shape
    return x.transpose(1, 0, 3, 2, 4).reshape(b, nc * c, h, d)

def short_conv(u, b_gate, c_gate, conv_w):
    z = c_gate * u
    t = z.shape[1]
    zp = jnp.pad(z, ((0, 0), (CONV_WIDTH - 1, 0), (0, 0)))
    y = sum(conv_w[i] * zp[:, i:i + t, :] for i in range(CONV_WIDTH))
    return b_gate * y

def retention(q, k, v):
    b, t, h, dk = q.shape
    dv = v.shape[-1]
    log_g = jnp.log(1.0 - 2.0 ** (-5.0 - jnp.arange(h, dtype=jnp.float32)))
    idx = jnp.arange(CHUNK, dtype=jnp.float32)
    diff = idx[:, None] - idx[None, :]
    causal = diff >= 0
    decay_mask = jnp.where(causal, jnp.exp(log_g[:, None, None] * jnp.maximum(diff, 0.0)), 0.0)
    q_decay = jnp.exp(log_g[:, None] * (idx + 1.0))[None, :, :, None]
    k_decay = jnp.exp(log_g[:, None] * (CHUNK - 1.0 - idx))[None, :, :, None]
    chunk_decay = jnp.exp(log_g * CHUNK)[None, :, None, None]
    q = q * (dk ** -0.5)

    def step(state, inp):
        qi, ki, vi = inp
        s = jnp.einsum('bhid,bhjd->bhij', qi, ki) * decay_mask
        intra = jnp.einsum('bhij,bhjv->bhiv', s, vi)
        inter = jnp.einsum('bhid,bhdv->bhiv', qi * q_decay, state)
        new_state = state * chunk_decay + jnp.einsum('bhjd,bhjv->bhdv', ki * k_decay, vi)
        return new_state, intra + inter

    state0 = jnp.zeros((b, h, dk, dv), jnp.float32)
    _, out = lax.scan(step, state0, (to_chunks(q), to_chunks(k), to_chunks(v)))
    return from_chunks(out)

def gated_linear_attention(q, k, v, log_a):
    b, t, h, dk = q.shape
    dv = v.shape[-1]
    q = q * (dk ** -0.5)
    tril = jnp.tril(jnp.ones((CHUNK, CHUNK), dtype=bool))[None, None, :, :, None]

    def step(state, inp):
        qi, ki, vi, gi = inp
        cum = jnp.cumsum(gi, axis=2)
        rel = cum[:, :, :, None, :] - cum[:, :, None, :, :]
        pair_decay = jnp.where(tril, jnp.exp(jnp.where(tril, rel, 0.0)), 0.0)
        s = jnp.einsum('bhid,bhjd,bhijd->bhij', qi, ki, pair_decay)
        intra = jnp.einsum('bhij,bhjv->bhiv', s, vi)
        inter = jnp.einsum('bhid,bhdv->bhiv', qi * jnp.exp(cum), state)
        last = cum[:, :, -1:, :]
        new_state = state * jnp.exp(last)[:, :, 0, :, None] + jnp.einsum(
            'bhjd,bhjv->bhdv', ki * jnp.exp(last - cum), vi)
        return new_state, intra + inter

    state0 = jnp.zeros((b, h, dk, dv), jnp.float32)
    _, out = lax.scan(step, state0, (to_chunks(q), to_chunks(k), to_chunks(v), to_chunks(log_a)))
    return from_chunks(out)

def split_columns(proj):
    sizes = ([CONV_DIM] * 3 + [RET_DIM] * 4
             + [GLA_KEY_DIM, GLA_KEY_DIM, GLA_VAL_DIM, GLA_VAL_DIM, GLA_GATE_RANK]
             + [D_MODEL] * N_BRANCHES)
    offsets = [int(o) for o in np.cumsum(sizes)[:-1]]
    return jnp.split(proj, offsets, axis=-1)

def mixer_block(h, positions, w_in, conv_w, ret_gn_w, gla_w_a2, gla_b_a, gla_gn_w,
                w_branch_a, w_branch_b, w_branch_c, w_out):
    bsz, t, _ = h.shape
    proj = (h @ w_in).astype(jnp.float32)
    (cu, cb, cc, rq, rk, rv, rg, gq, gk, gv, gr, ga_down,
     gate_a, gate_b, gate_c) = split_columns(proj)

    y_a = short_conv(cu, cb, cc, conv_w.astype(jnp.float32))

    rq = rotary(rq.reshape(bsz, t, RET_HEADS, RET_HEAD_DIM), positions)
    rk = rotary(rk.reshape(bsz, t, RET_HEADS, RET_HEAD_DIM), positions)
    rv = rv.reshape(bsz, t, RET_HEADS, RET_HEAD_DIM)
    y_b = head_norm(retention(rq, rk, rv), ret_gn_w, center=True) * jax.nn.silu(rg)

    gate_logits = ga_down @ gla_w_a2.astype(jnp.float32) + gla_b_a.astype(jnp.float32)
    log_a = (jax.nn.log_sigmoid(gate_logits) / GLA_GATE_TAU).reshape(bsz, t, GLA_HEADS, GLA_KEY_HEAD_DIM)
    gq = gq.reshape(bsz, t, GLA_HEADS, GLA_KEY_HEAD_DIM)
    gk = gk.reshape(bsz, t, GLA_HEADS, GLA_KEY_HEAD_DIM)
    gv = gv.reshape(bsz, t, GLA_HEADS, GLA_VAL_HEAD_DIM)
    y_c = head_norm(gated_linear_attention(gq, gk, gv, log_a), gla_gn_w, center=False) * jax.nn.silu(gr)

    merged = (jax.nn.sigmoid(gate_a) * (y_a @ w_branch_a.astype(jnp.float32))
              + jax.nn.sigmoid(gate_b) * (y_b @ w_branch_b.astype(jnp.float32))
              + jax.nn.sigmoid(gate_c) * (y_c @ w_branch_c.astype(jnp.float32)))
    return (merged @ w_out.astype(jnp.float32)).astype(h.dtype)

def swiglu(h, w_gate, w_up, w_down):
    return (jax.nn.silu(h @ w_gate) * (h @ w_up)) @ w_down

def first_inputs(seed: int = 0) -> dict:
    key = jax.random.key(seed)
    ks = jax.random.split(key, 20)
    f32 = jnp.float32

    def normal(k, shape, scale):
        return jax.random.normal(k, shape, f32) * scale

    def gain(k, shape):
        return 1.0 + 0.1 * jax.random.normal(k, shape, f32)

    return {
        "x": normal(ks[0], (BATCH, SEQ, D_MODEL), 1.0),
        "positions": jnp.broadcast_to(jnp.arange(SEQ, dtype=jnp.int32), (BATCH, SEQ)),
        "norm_mix_pre": gain(ks[1], (DEPTH, D_MODEL)),
        "w_in": normal(ks[2], (DEPTH, D_MODEL, IN_COLS), D_MODEL ** -0.5),
        "conv_w": normal(ks[3], (DEPTH, CONV_WIDTH, CONV_DIM), CONV_WIDTH ** -0.5),
        "ret_gn_w": gain(ks[4], (DEPTH, RET_DIM)),
        "gla_w_a2": normal(ks[5], (DEPTH, GLA_GATE_RANK, GLA_KEY_DIM), GLA_GATE_RANK ** -0.5),
        "gla_b_a": normal(ks[6], (DEPTH, GLA_KEY_DIM), 0.1),
        "gla_gn_w": gain(ks[7], (DEPTH, GLA_VAL_DIM)),
        "w_branch_a": normal(ks[8], (DEPTH, CONV_DIM, D_MODEL), CONV_DIM ** -0.5),
        "w_branch_b": normal(ks[9], (DEPTH, RET_DIM, D_MODEL), RET_DIM ** -0.5),
        "w_branch_c": normal(ks[10], (DEPTH, GLA_VAL_DIM, D_MODEL), GLA_VAL_DIM ** -0.5),
        "w_out": normal(ks[11], (DEPTH, D_MODEL, D_MODEL), D_MODEL ** -0.5),
        "norm_mix_post": gain(ks[12], (DEPTH, D_MODEL)),
        "norm_ffn_pre": gain(ks[13], (DEPTH, D_MODEL)),
        "w_ffn_gate": normal(ks[14], (DEPTH, D_MODEL, D_FF), D_MODEL ** -0.5),
        "w_ffn_up": normal(ks[15], (DEPTH, D_MODEL, D_FF), D_MODEL ** -0.5),
        "w_ffn_down": normal(ks[16], (DEPTH, D_FF, D_MODEL), D_FF ** -0.5),
        "norm_ffn_post": gain(ks[17], (DEPTH, D_MODEL)),
    }

def first_block(x, positions, norm_mix_pre, w_in, conv_w, ret_gn_w, gla_w_a2, gla_b_a, gla_gn_w,
              w_branch_a, w_branch_b, w_branch_c, w_out, norm_mix_post, norm_ffn_pre,
              w_ffn_gate, w_ffn_up, w_ffn_down, norm_ffn_post):
    for layer in range(DEPTH):
        h = rms_norm(x, norm_mix_pre[layer])
        m = mixer_block(h, positions, w_in[layer], conv_w[layer], ret_gn_w[layer], gla_w_a2[layer],
                        gla_b_a[layer], gla_gn_w[layer], w_branch_a[layer], w_branch_b[layer],
                        w_branch_c[layer], w_out[layer])
        x = x + rms_norm(m, norm_mix_post[layer]).astype(x.dtype)
        h = rms_norm(x, norm_ffn_pre[layer])
        f = swiglu(h, w_ffn_gate[layer], w_ffn_up[layer], w_ffn_down[layer])
        x = x + rms_norm(f, norm_ffn_post[layer]).astype(x.dtype)
    return x


GRID_W = 64
CTX_LEN = 256
CONV_K = 31
MLSTM_HEADS = 4
MLSTM_DIM = 1024
MLSTM_HEAD_DIM = MLSTM_DIM // MLSTM_HEADS
MLSTM_CHUNK = 64
M_INIT = -1e30
ATTN_HEADS = 8
ATTN_KV_HEADS = 2
ATTN_GROUP = ATTN_HEADS // ATTN_KV_HEADS
ATTN_HEAD_DIM = 64
ATTN_DIM = ATTN_HEADS * ATTN_HEAD_DIM
KV_DIM = ATTN_KV_HEADS * ATTN_HEAD_DIM
Q_BLOCK = 128
ROPE_THETA = 10000.0
D_FF_2 = 2816
FFN_CONV_K = 3
N_BRANCH = 3
IN_SIZES = (2 * CONV_DIM, 3 * MLSTM_DIM, MLSTM_DIM, 4 * MLSTM_HEADS, ATTN_DIM, KV_DIM, KV_DIM, N_BRANCH * D_MODEL)
N_IN = sum(IN_SIZES)


def rmsnorm(x, w):
    xf = x.astype(jnp.float32)
    y = xf * lax.rsqrt(jnp.mean(xf * xf, axis=-1, keepdims=True) + EPS)
    return (y * w.astype(jnp.float32)).astype(x.dtype)

def layernorm(x, w, b):
    xf = x.astype(jnp.float32)
    xc = xf - jnp.mean(xf, axis=-1, keepdims=True)
    y = xc * lax.rsqrt(jnp.mean(xc * xc, axis=-1, keepdims=True) + EPS)
    return (y * w.astype(jnp.float32) + b.astype(jnp.float32)).astype(x.dtype)

def dwconv(x, w, b):
    k = w.shape[0]
    y = lax.conv_general_dilated(x, w[:, None, :].astype(x.dtype), window_strides=(1,),
                                 padding=((k // 2, k // 2),), dimension_numbers=("NWC", "WIO", "NWC"),
                                 feature_group_count=x.shape[-1])
    return y + b.astype(x.dtype)

def axial_rope_tables(rows):
    row = jnp.broadcast_to(jnp.arange(rows, dtype=jnp.float32)[:, None], (rows, GRID_W)).reshape(-1)
    col = jnp.broadcast_to(jnp.arange(GRID_W, dtype=jnp.float32)[None, :], (rows, GRID_W)).reshape(-1)
    n_freq = ATTN_HEAD_DIM // 4
    inv_freq = ROPE_THETA ** (-jnp.arange(n_freq, dtype=jnp.float32) / n_freq)
    ang = jnp.concatenate([row[:, None] * inv_freq, col[:, None] * inv_freq], axis=-1)
    return jnp.cos(ang), jnp.sin(ang)

def apply_rope(x, cos, sin):
    half = x.shape[-1] // 2
    x1, x2 = x[..., :half], x[..., half:]
    c = cos[None, :, None, :]
    s = sin[None, :, None, :]
    return jnp.concatenate([x1 * c - x2 * s, x1 * s + x2 * c], axis=-1).astype(x.dtype)

def mlstm_chunked(q, k, v, log_i, log_f, state):
    b, h, n_tok, d = q.shape
    n_chunks = n_tok // MLSTM_CHUNK

    def to_chunks(a):
        return jnp.moveaxis(a.reshape(b, h, n_chunks, MLSTM_CHUNK, *a.shape[3:]), 2, 0)

    xs = (to_chunks(q), to_chunks(k), to_chunks(v), to_chunks(log_i), to_chunks(log_f))
    lower = jnp.tril(jnp.ones((MLSTM_CHUNK, MLSTM_CHUNK), dtype=bool))

    def step(carry, inp):
        c_mat, n_vec, m = carry
        qc, kc, vc, li, lf = inp
        cum = jnp.cumsum(lf, axis=-1)
        d_mat = jnp.where(lower, cum[..., :, None] - cum[..., None, :] + li[..., None, :], -jnp.inf)
        inter = cum + m[..., None]
        m_t = jnp.maximum(inter, jnp.max(d_mat, axis=-1))
        w_intra = jnp.exp(d_mat - m_t[..., None])
        w_inter = jnp.exp(inter - m_t)
        s = jnp.einsum("bhtd,bhsd->bhts", qc, kc) * w_intra
        num = w_inter[..., None] * jnp.einsum("bhtd,bhde->bhte", qc, c_mat) + jnp.einsum("bhts,bhse->bhte", s, vc)
        den = w_inter * jnp.einsum("bhtd,bhd->bht", qc, n_vec) + jnp.sum(s, axis=-1)
        h_out = num / jnp.maximum(jnp.abs(den), jnp.exp(-m_t))[..., None]
        cum_last = cum[..., -1]
        g = cum_last[..., None] - cum + li
        m_new = jnp.maximum(cum_last + m, jnp.max(g, axis=-1))
        decay = jnp.exp(cum_last + m - m_new)
        wk = jnp.exp(g - m_new[..., None])[..., None] * kc
        c_new = decay[..., None, None] * c_mat + jnp.einsum("bhsd,bhse->bhde", wk, vc)
        n_new = decay[..., None] * n_vec + jnp.sum(wk, axis=-2)
        return (c_new, n_new, m_new), h_out

    state, hs = lax.scan(step, state, xs)
    return jnp.moveaxis(hs, 0, 2).reshape(b, h, n_tok, d), state

def mlstm_prepare(qkv, gate_pre, gate_b):
    b, n, _ = qkv.shape
    q, k, v = jnp.split(qkv.astype(jnp.float32), 3, axis=-1)

    def to_heads(a):
        return a.reshape(b, n, MLSTM_HEADS, MLSTM_HEAD_DIM).transpose(0, 2, 1, 3)

    pre = (gate_pre.astype(jnp.float32) + gate_b.astype(jnp.float32)).reshape(b, n, 4, MLSTM_HEADS).transpose(2, 0, 3, 1)
    return to_heads(q), to_heads(k) * MLSTM_HEAD_DIM ** -0.5, to_heads(v), pre

def mlstm_bidirectional(qx, kx, vx, pre_x, qc, kc, vc, pre_c):
    b = qx.shape[0]
    zero = (jnp.zeros((b, MLSTM_HEADS, MLSTM_HEAD_DIM, MLSTM_HEAD_DIM), jnp.float32),
            jnp.zeros((b, MLSTM_HEADS, MLSTM_HEAD_DIM), jnp.float32),
            jnp.full((b, MLSTM_HEADS), M_INIT, jnp.float32))

    def flip(a):
        return jnp.flip(a, axis=2)

    lsig = jax.nn.log_sigmoid
    hc_f, st_f = mlstm_chunked(qc, kc, vc, pre_c[0], lsig(pre_c[1]), zero)
    hx_f, _ = mlstm_chunked(qx, kx, vx, pre_x[0], lsig(pre_x[1]), st_f)
    hc_b, st_b = mlstm_chunked(flip(qc), flip(kc), flip(vc), flip(pre_c[2]), flip(lsig(pre_c[3])), zero)
    hx_b, _ = mlstm_chunked(flip(qx), flip(kx), flip(vx), flip(pre_x[2]), flip(lsig(pre_x[3])), st_b)
    return hx_f + flip(hx_b), hc_f + flip(hc_b)

def mlstm_readout(h, o_pre, norm_w, w_o):
    b, _, n, _ = h.shape
    hn = rmsnorm(h.transpose(0, 2, 1, 3), norm_w.reshape(MLSTM_HEADS, MLSTM_HEAD_DIM)).reshape(b, n, MLSTM_DIM)
    return (hn.astype(o_pre.dtype) * jax.nn.sigmoid(o_pre)) @ w_o

def attn_heads(a, n_heads, norm_w):
    b, n, _ = a.shape
    return rmsnorm(a.reshape(b, n, n_heads, ATTN_HEAD_DIM), norm_w)

def attend(q, k, v):
    s = jnp.einsum("bqhgd,bkhd->bhgqk", q, k).astype(jnp.float32) * ATTN_HEAD_DIM ** -0.5
    p = jax.nn.softmax(s, axis=-1).astype(v.dtype)
    return jnp.einsum("bhgqk,bkhd->bqhgd", p, v)

def latent_attention(q, k, v):
    b, n = q.shape[:2]
    n_blocks = n // Q_BLOCK
    qb = jnp.moveaxis(q.reshape(b, n_blocks, Q_BLOCK, ATTN_KV_HEADS, ATTN_GROUP, ATTN_HEAD_DIM), 1, 0)
    o = lax.map(lambda qi: attend(qi, k, v), qb)
    return jnp.moveaxis(o, 0, 1).reshape(b, n, ATTN_DIM)

def conformer_conv(u, dw_w, dw_b, ln_w, ln_b, w_o):
    a, g = jnp.split(u, 2, axis=-1)
    h = dwconv(a * jax.nn.sigmoid(g), dw_w, dw_b)
    return jax.nn.silu(layernorm(h, ln_w, ln_b)) @ w_o

def conv_ffn(h, w_up, dw_w, dw_b, w_down):
    u = dwconv(h @ w_up, dw_w, dw_b)
    a, g = jnp.split(u, 2, axis=-1)
    return (a * jax.nn.silu(g)) @ w_down

def token_mixers(hx, hc, cos, sin, want_ctx, w_in, branch_gate_b, conv_dw_w, conv_dw_b, conv_ln_w, conv_ln_b,
                 w_conv_out, mlstm_gate_b, mlstm_norm_w, w_mlstm_out, q_norm_w, k_norm_w, w_attn_out, w_out):
    offsets = [int(o) for o in np.cumsum(IN_SIZES)[:-1]]
    cu_x, mqkv_x, mo_x, mg_x, aq_x, ak_x, av_x, bg_x = jnp.split(hx @ w_in, offsets, axis=-1)
    cu_c, mqkv_c, mo_c, mg_c, aq_c, ak_c, av_c, bg_c = jnp.split(hc @ w_in, offsets, axis=-1)
    b, n, _ = hx.shape
    n_ctx = hc.shape[1]

    conv_x = conformer_conv(cu_x, conv_dw_w, conv_dw_b, conv_ln_w, conv_ln_b, w_conv_out)

    h_x, h_c = mlstm_bidirectional(*mlstm_prepare(mqkv_x, mg_x, mlstm_gate_b), *mlstm_prepare(mqkv_c, mg_c, mlstm_gate_b))
    mlstm_x = mlstm_readout(h_x, mo_x, mlstm_norm_w, w_mlstm_out)

    k_c = attn_heads(ak_c, ATTN_KV_HEADS, k_norm_w)
    v_c = av_c.reshape(b, n_ctx, ATTN_KV_HEADS, ATTN_HEAD_DIM)
    k_x = apply_rope(attn_heads(ak_x, ATTN_KV_HEADS, k_norm_w), cos, sin)
    v_x = av_x.reshape(b, n, ATTN_KV_HEADS, ATTN_HEAD_DIM)
    q_x = apply_rope(attn_heads(aq_x, ATTN_HEADS, q_norm_w), cos, sin).reshape(b, n, ATTN_KV_HEADS, ATTN_GROUP, ATTN_HEAD_DIM)
    attn_x = latent_attention(q_x, jnp.concatenate([k_c, k_x], axis=1), jnp.concatenate([v_c, v_x], axis=1)) @ w_attn_out

    def merge(conv_o, mlstm_o, attn_o, gate_pre):
        g_conv, g_mlstm, g_attn = jnp.split(jax.nn.sigmoid(gate_pre + branch_gate_b), N_BRANCH, axis=-1)
        return (g_conv * conv_o + g_mlstm * mlstm_o + g_attn * attn_o) @ w_out

    out_x = merge(conv_x, mlstm_x, attn_x, bg_x)
    if not want_ctx:
        return out_x, None
    conv_c = conformer_conv(cu_c, conv_dw_w, conv_dw_b, conv_ln_w, conv_ln_b, w_conv_out)
    mlstm_c = mlstm_readout(h_c, mo_c, mlstm_norm_w, w_mlstm_out)
    q_c = attn_heads(aq_c, ATTN_HEADS, q_norm_w).reshape(b, n_ctx, ATTN_KV_HEADS, ATTN_GROUP, ATTN_HEAD_DIM)
    attn_c = attend(q_c, k_c, v_c).reshape(b, n_ctx, ATTN_DIM) @ w_attn_out
    return out_x, merge(conv_c, mlstm_c, attn_c, bg_c)

def second_inputs(seed: int = 0) -> dict:
    key = jax.random.key(seed)
    ks = jax.random.split(key, 32)
    f32 = jnp.float32
    D = D_MODEL
    L = DEPTH

    def nrm(i, shape, scale):
        return jax.random.normal(ks[i], shape, f32) * scale

    fb = jnp.linspace(3.0, 6.0, MLSTM_HEADS, dtype=f32)
    zh = jnp.zeros((MLSTM_HEADS,), f32)
    gate_base = jnp.concatenate([zh, fb, zh, fb])
    return {
        "x": nrm(0, (BATCH, SEQ, D), 1.0),
        "c": nrm(1, (BATCH, D), 1.0),
        "ctx": nrm(2, (BATCH, CTX_LEN, D), 1.0),
        "c_ctx": nrm(3, (D,), 1.0),
        "ada_w": nrm(4, (L, D, 6 * D), 0.5 * D ** -0.5),
        "ada_b": nrm(5, (L, 6 * D), 0.02),
        "norm1_w": 1.0 + nrm(6, (L, D), 0.02),
        "norm2_w": 1.0 + nrm(7, (L, D), 0.02),
        "w_in": nrm(8, (L, D, N_IN), D ** -0.5),
        "branch_gate_b": nrm(9, (L, N_BRANCH * D), 0.02),
        "conv_dw_w": nrm(10, (L, CONV_K, CONV_DIM), CONV_K ** -0.5),
        "conv_dw_b": nrm(11, (L, CONV_DIM), 0.02),
        "conv_ln_w": 1.0 + nrm(12, (L, CONV_DIM), 0.02),
        "conv_ln_b": nrm(13, (L, CONV_DIM), 0.02),
        "w_conv_out": nrm(14, (L, CONV_DIM, D), CONV_DIM ** -0.5),
        "mlstm_gate_b": gate_base + nrm(15, (L, 4 * MLSTM_HEADS), 0.1),
        "mlstm_norm_w": 1.0 + nrm(16, (L, MLSTM_DIM), 0.02),
        "w_mlstm_out": nrm(17, (L, MLSTM_DIM, D), MLSTM_DIM ** -0.5),
        "q_norm_w": 1.0 + nrm(18, (L, ATTN_HEAD_DIM), 0.02),
        "k_norm_w": 1.0 + nrm(19, (L, ATTN_HEAD_DIM), 0.02),
        "w_attn_out": nrm(20, (L, ATTN_DIM, D), ATTN_DIM ** -0.5),
        "w_out": nrm(21, (L, D, D), D ** -0.5),
        "ffn_w_up": nrm(22, (L, D, 2 * D_FF_2), D ** -0.5),
        "ffn_conv_w": nrm(23, (L, FFN_CONV_K, 2 * D_FF_2), FFN_CONV_K ** -0.5),
        "ffn_conv_b": nrm(24, (L, 2 * D_FF_2), 0.02),
        "ffn_w_down": nrm(25, (L, D_FF_2, D), D_FF_2 ** -0.5),
    }

def second_block(x, c, ctx, c_ctx, ada_w, ada_b, norm1_w, norm2_w, w_in, branch_gate_b, conv_dw_w, conv_dw_b,
              conv_ln_w, conv_ln_b, w_conv_out, mlstm_gate_b, mlstm_norm_w, w_mlstm_out, q_norm_w, k_norm_w,
              w_attn_out, w_out, ffn_w_up, ffn_conv_w, ffn_conv_b, ffn_w_down):
    rows = x.shape[1] // GRID_W
    cos, sin = axial_rope_tables(rows)
    xc = ctx
    for l in range(DEPTH):
        want_ctx = l < DEPTH - 1
        mod_x = jax.nn.silu(c) @ ada_w[l] + ada_b[l]
        mod_c = jax.nn.silu(c_ctx) @ ada_w[l] + ada_b[l]
        sh1, sc1, g1, sh2, sc2, g2 = jnp.split(mod_x[:, None, :], 6, axis=-1)
        sh1c, sc1c, g1c, sh2c, sc2c, g2c = jnp.split(mod_c, 6, axis=-1)

        hx = rmsnorm(x, norm1_w[l]) * (1.0 + sc1) + sh1
        hc = rmsnorm(xc, norm1_w[l]) * (1.0 + sc1c) + sh1c
        mix_x, mix_c = token_mixers(hx, hc, cos, sin, want_ctx, w_in[l], branch_gate_b[l], conv_dw_w[l],
                                    conv_dw_b[l], conv_ln_w[l], conv_ln_b[l], w_conv_out[l], mlstm_gate_b[l],
                                    mlstm_norm_w[l], w_mlstm_out[l], q_norm_w[l], k_norm_w[l], w_attn_out[l], w_out[l])
        x = x + g1 * mix_x
        hx = rmsnorm(x, norm2_w[l]) * (1.0 + sc2) + sh2
        x = x + g2 * conv_ffn(hx, ffn_w_up[l], ffn_conv_w[l], ffn_conv_b[l], ffn_w_down[l])
        if want_ctx:
            xc = xc + g1c * mix_c
            hc = rmsnorm(xc, norm2_w[l]) * (1.0 + sc2c) + sh2c
            xc = xc + g2c * conv_ffn(hc, ffn_w_up[l], ffn_conv_w[l], ffn_conv_b[l], ffn_w_down[l])
    return x


def setup_inputs(seed=0):
    out = dict(first_inputs(seed))
    for name, value in second_inputs(seed + 1).items():
        if name != "x":
            out[name + "_2"] = value
    return out


def reference(
    x, positions, norm_mix_pre, w_in, conv_w, ret_gn_w, gla_w_a2, gla_b_a, gla_gn_w, w_branch_a,
    w_branch_b, w_branch_c, w_out, norm_mix_post, norm_ffn_pre, w_ffn_gate, w_ffn_up,
    w_ffn_down, norm_ffn_post, c_2, ctx_2, c_ctx_2, ada_w_2, ada_b_2, norm1_w_2, norm2_w_2,
    w_in_2, branch_gate_b_2, conv_dw_w_2, conv_dw_b_2, conv_ln_w_2, conv_ln_b_2, w_conv_out_2,
    mlstm_gate_b_2, mlstm_norm_w_2, w_mlstm_out_2, q_norm_w_2, k_norm_w_2, w_attn_out_2,
    w_out_2, ffn_w_up_2, ffn_conv_w_2, ffn_conv_b_2, ffn_w_down_2,
):
    x = first_block(
        x, positions, norm_mix_pre, w_in, conv_w, ret_gn_w, gla_w_a2, gla_b_a, gla_gn_w,
        w_branch_a, w_branch_b, w_branch_c, w_out, norm_mix_post, norm_ffn_pre, w_ffn_gate,
        w_ffn_up, w_ffn_down, norm_ffn_post,
    )
    return second_block(
        x, c_2, ctx_2, c_ctx_2, ada_w_2, ada_b_2, norm1_w_2, norm2_w_2, w_in_2, branch_gate_b_2,
        conv_dw_w_2, conv_dw_b_2, conv_ln_w_2, conv_ln_b_2, w_conv_out_2, mlstm_gate_b_2,
        mlstm_norm_w_2, w_mlstm_out_2, q_norm_w_2, k_norm_w_2, w_attn_out_2, w_out_2,
        ffn_w_up_2, ffn_conv_w_2, ffn_conv_b_2, ffn_w_down_2,
    )


_drawn_inputs = setup_inputs


def setup_inputs(seed=0):
    import zlib

    import numpy as np

    out = dict(_drawn_inputs(seed))
    spreads = {}
    factors = {'ada_b_2': 4.141,
     'norm1_w_2': 8.0,
     'norm2_w_2': 8.0,
     'branch_gate_b_2': 8.0,
     'conv_dw_b_2': 8.0,
     'conv_ln_w_2': 8.0,
     'conv_ln_b_2': 8.0,
     'mlstm_norm_w_2': 8.0,
     'q_norm_w_2': 8.0,
     'k_norm_w_2': 8.0,
     'ffn_conv_b_2': 8.0}
    for name, (base, spread) in spreads.items():
        noise = np.random.default_rng([zlib.crc32(name.encode()), seed]).standard_normal(out[name].shape)
        drawn = base * np.exp(spread * noise) if base else spread * noise
        out[name] = jnp.asarray(drawn.astype(out[name].dtype))
    for name, factor in factors.items():
        out[name] = (out[name] * factor).astype(out[name].dtype)
    return out
```

```python
import numpy as np

import concourse.bass as bass
from concourse import mybir
from concourse.alu_op_type import AluOpType as ALU

F32 = mybir.dt.float32
F32R = mybir.dt.float32r
I32 = mybir.dt.int32
ACT = mybir.ActivationFunctionType
AX_X = mybir.AxisListType.X

P = 128
D = 1024
KD = D // P
SEQ = 256
T2 = 2 * SEQ
CTX, LAT = (0, SEQ), (SEQ, T2)
DEPTH = 2
EPS = 1e-6

CONV = 512
RH, RD = 4, 128
GH, GK, GV = 4, 64, 128
GTAU = 16.0
RANK = 16
FF = 2816
NFF = FF // P
FF_HALF = NFF // 2
CONV_K = 31
PAD = CONV_K // 2
MH, MD = 4, 256
AH, AKV, AD = 8, 2, 64
AG = AH // AKV
GRID_W = 64
M_INIT = -1e30
GLA_LEVELS = [64, 32, 16, 8, 4, 2, 1]

UNIT = 8
RAW, SPLIT = 3, 4
ADA_COLS = 256
N_ADA = DEPTH * (6 * D // ADA_COLS)
ADA_UNITS = N_ADA * KD * (ADA_COLS // P) // UNIT


class Tile:

    def __init__(self, name, array, layer, rows, cols):
        self.name, self.array, self.layer, self.rows, self.cols = name, array, layer, rows, cols
        self.k = len(rows)
        self.wide = len(cols) // P


def span(start, n=P):
    return list(range(start, start + n))


def stream_tiles():
    full = list(range(KD))
    out = []

    def put(name, array, layer, cols, rows=None):
        out.append(Tile(name, array, layer, full if rows is None else rows, cols))

    cu, cb, cc, rq, rk, rv, rg, gq, gk, gv, gr, ga, gates = np.cumsum(
        [0, CONV, CONV, CONV, 512, 512, 512, 512, 256, 256, 512, 512, RANK]).tolist()
    for l in range(DEPTH):
        for h in range(RH):
            put("rq", "w_in", l, span(rq + h * P))
            put("rk", "w_in", l, span(rk + h * P))
        for v in range(2):
            put("rv", "w_in", l, span(rv + 256 * v, 256))
        for i in range(2):
            put("gq", "w_in", l, span(gq + i * P))
            put("gk", "w_in", l, span(gk + i * P))
        put("ga", "w_in", l, span(ga, RANK) + [-1] * (P - RANK))
        for v in range(2):
            put("gv", "w_in", l, span(gv + 256 * v, 256))
        for i in range(4):
            put("cu", "w_in", l, span(cu + i * P))
            put("cc", "w_in", l, span(cc + i * P))
            put("cb", "w_in", l, span(cb + i * P))
        for i in range(4):
            put("rg", "w_in", l, span(rg + i * P))
        for i in range(4):
            put("gr", "w_in", l, span(gr + i * P))
        for b, name in enumerate(("w_branch_a", "w_branch_b", "w_branch_c")):
            for f in range(KD):
                put("gate", "w_in", l, span(gates + b * D + f * P))
                put("branch", name, l, span(f * P), list(range(4)))
        for f in range(KD):
            put("out", "w_out", l, span(f * P))
        for t in range(NFF):
            put("ffg", "w_ffn_gate", l, span(t * P))
            put("ffu", "w_ffn_up", l, span(t * P))
        for f in range(KD):
            put("ffd", "w_ffn_down", l, span(f * P), list(range(NFF)))

    cu, mq, mk, mv, mo, mg, aq, ak, av, bg = np.cumsum([0, 2 * CONV, D, D, D, D, 16, 512, 128, 128]).tolist()
    pair = [span(j * AD, AD) + span((j + AG) * AD, AD) for j in range(AG)]
    for l in range(DEPTH):
        for i in range(4):
            put("ca", "w_in_2", l, span(cu + i * P))
            put("cg", "w_in_2", l, span(cu + CONV + i * P))
        for j in range(AG):
            put("aq", "w_in_2", l, [aq + c for c in pair[j]])
        put("ak", "w_in_2", l, span(ak))
        put("av", "w_in_2", l, span(av))
        put("mg", "w_in_2", l, span(mg, 16) + [-1] * (P - 16))
        for b, (name, rows) in enumerate((("w_conv_out_2", 4), ("w_attn_out_2", 4))):
            for f in range(KD):
                put("gate", "w_in_2", l, span(bg + (0, 2)[b] * D + f * P))
                put("branch", name, l, span(f * P), list(range(rows)))
        for h in range(MH):
            for i in range(2):
                put("mq", "w_in_2", l, span(mq + h * MD + i * P))
            for i in range(2):
                put("mk", "w_in_2", l, span(mk + h * MD + i * P))
            put("mv", "w_in_2", l, span(mv + h * MD, MD))
            for i in range(2):
                put("mo", "w_in_2", l, span(mo + h * MD + i * P))
        for f in range(KD):
            put("gate", "w_in_2", l, span(bg + D + f * P))
            put("branch", "w_mlstm_out_2", l, span(f * P))
        for f in range(KD):
            put("out", "w_out_2", l, span(f * P))
        for half in range(2):
            for t in range(half * FF_HALF, (half + 1) * FF_HALF):
                put("fa", "ffn_w_up_2", l, span(t * P))
                put("fg", "ffn_w_up_2", l, span(FF + t * P))
            for f in range(KD):
                put("fd", "ffn_w_down_2", l, span(f * P), span(half * FF_HALF, FF_HALF))
    return out


TILES = stream_tiles()
N_BLOCKS = sum(t.k * t.wide for t in TILES)
N_UNITS = N_BLOCKS // UNIT
assert N_BLOCKS % UNIT == 0 and N_UNITS % RAW == 0


def pack_weights(inputs):
    stream = np.zeros((ADA_UNITS + N_UNITS, P, UNIT * P), np.float32)
    blocks = stream.reshape(-1, P, UNIT, P)
    n = 0

    def put(block):
        nonlocal n
        blocks[n // UNIT, :, n % UNIT, :block.shape[1]] = block
        n += 1

    for l in range(DEPTH):
        w = inputs["ada_w_2"][l]
        for c in range(0, 6 * D, P * 2):
            for k in range(KD):
                for j in range(2):
                    put(w[k * P:(k + 1) * P, c + j * P:c + (j + 1) * P])
    for t in TILES:
        w = inputs[t.array][t.layer]
        if t.array == "w_attn_out_2":
            order = [r for j in range(AG) for r in span(j * AD, AD) + span((j + AG) * AD, AD)]
            w = w[order]
        for k in t.rows:
            for j in range(t.wide):
                cols = [c for c in t.cols[j * P:(j + 1) * P] if c >= 0]
                put(w[k * P:(k + 1) * P, cols])
    assert n == N_BLOCKS + ADA_UNITS * UNIT
    return stream


def vector_layout():
    at, out = 0, {}

    def put(name, n):
        nonlocal at
        out[name] = (at, n)
        at += n

    for l in range(DEPTH):
        for name in ("norm_mix_pre", "norm_mix_post", "norm_ffn_pre", "norm_ffn_post"):
            put((name, l), KD)
        put(("conv_w", l), 3 * 4)
        put(("ret_gn_w", l), RH)
        put(("gla_gn_w", l), GH)
        put(("gla_b_a", l), 2)
        put(("gla_w_a2", l), GH * GK)
    for l in range(DEPTH):
        put(("norm1_w_2", l), KD)
        put(("norm2_w_2", l), KD)
        put(("branch_gate_b_2", l), 3 * KD)
        put(("conv_dw_w_2", l), CONV_K * 4)
        put(("conv_dw_b_2", l), 4)
        put(("conv_ln_w_2", l), 4)
        put(("conv_ln_b_2", l), 4)
        put(("mlstm_gate_b_2", l), 16)
        put(("mlstm_norm_w_2", l), KD)
        put(("q_norm_w_2", l), 1)
        put(("k_norm_w_2", l), 1)
        put(("ffn_conv_w_2", l), 3 * 2 * NFF)
        put(("ffn_conv_b_2", l), 2 * NFF)
        put(("ada_b_2", l), 6 * KD)
    put("c", 2 * KD)
    return out, at


VEC, N_VEC = vector_layout()


def pack_vectors(inputs):
    vec = np.zeros((P, N_VEC), np.float32)

    def columns(a):
        return np.ascontiguousarray(a.reshape(-1, P).T)

    for key, (at, n) in VEC.items():
        if key == "c":
            both = np.stack([inputs["c_ctx_2"], inputs["c_2"][0]])
            vec[:, at:at + n] = both.reshape(2, KD, P).transpose(2, 1, 0).reshape(P, n)
            continue
        name, l = key
        a = inputs[name][l]
        if name == "gla_w_a2":
            vec[:RANK, at:at + n] = a
        elif name == "mlstm_gate_b_2":
            vec[:, at:at + n] = np.broadcast_to(a, (P, n))
        elif name in ("q_norm_w_2", "k_norm_w_2"):
            vec[:, at] = np.concatenate([a, a])
        else:
            vec[:, at:at + n] = columns(a)
    return vec


CONST_PARTS = [("ident", P), ("rot_ret", P), ("rot_att", P), ("upto", P), ("from", P), ("ones", P),
               ("one64", P), ("cos_ax", SEQ), ("sin_ax", SEQ), ("head_row", MH * P), ("inv_freq", 1)]
CONST = {}
for _name, _n in CONST_PARTS:
    CONST[_name] = (sum(n for _, n in CONST_PARTS[:len(CONST)]), _n)
N_CONST = sum(n for _, n in CONST_PARTS)
N_DECAY = RH * 3 * P


def constants():
    c = np.zeros((P, N_CONST), np.float32)

    def at(name):
        return c[:, CONST[name][0]:CONST[name][0] + CONST[name][1]]

    p, n = np.arange(P)[:, None], np.arange(P)[None, :]
    at("ident")[:] = p == n

    def rotation(half):
        r = np.zeros((P, P), np.float32)
        for base in range(0, P, 2 * half):
            for i in range(half):
                r[base + half + i, base + i] = -1.0
                r[base + i, base + half + i] = 1.0
        return r

    at("rot_ret")[:] = rotation(RD // 2)
    at("rot_att")[:] = rotation(AD // 2)
    at("upto")[:] = p <= n
    at("from")[:] = p >= n
    at("ones")[:] = 1.0
    at("one64")[:] = p // AD == n // AD
    n_freq = AD // 4
    inv = (10000.0 ** (-np.arange(n_freq, dtype=np.float32) / n_freq)).astype(np.float32)
    tok = np.arange(SEQ)
    ang = np.concatenate([(tok // GRID_W).astype(np.float32)[:, None] * inv,
                          (tok % GRID_W).astype(np.float32)[:, None] * inv], axis=-1)
    at("cos_ax")[:] = np.tile(np.cos(ang).T, (4, 1))
    at("sin_ax")[:] = np.tile(np.sin(ang).T, (4, 1))
    for h in range(MH):
        at("head_row")[h, h * P:(h + 1) * P] = 1.0
    half = RD // 2
    at("inv_freq")[:, 0] = np.tile((10000.0 ** (-np.arange(half, dtype=np.float32) / half)).astype(np.float32), 2)
    decay = np.zeros((P, RH, 3, P), np.float32)
    for h in range(RH):
        log_g = np.log(1.0 - 2.0 ** (-5.0 - h))
        for b, off in enumerate((0, P, 0)):
            diff = n + off - p
            decay[:, h, b, :] = np.where(diff >= 0, np.exp(log_g * np.maximum(diff, 0)), 0.0)
    masks = np.zeros((P, len(GLA_LEVELS) + 1, P), np.int32)
    for i, m in enumerate(GLA_LEVELS):
        masks[:, i, :] = (p // (2 * m) == n // (2 * m)) & (p % (2 * m) < m) & (n % (2 * m) >= m)
    masks[:, -1, :] = p == n
    return c, decay.reshape(P, N_DECAY), masks.reshape(P, -1)


class Expect:

    def __init__(self, engine):
        self.engine, self.seen = engine, {}

    def need(self, sem, more=1):
        self.seen[sem.name] = self.seen.get(sem.name, 0) + more
        self.engine.wait_ge(sem, self.seen[sem.name])


class Chain:

    def __init__(self, engine, sem):
        self.engine, self.sem, self.n = engine, sem, 0

    def do(self, instruction):
        instruction.then_inc(self.sem, 1)
        self.n += 1

    def settle(self):
        self.engine.wait_ge(self.sem, self.n)


class Place:

    def __init__(self):
        self.first_out, self.first_block, self.outs = [], [], []
        out = block = 0
        for t in TILES:
            self.first_out.append(out)
            self.first_block.append(block)
            n = 1
            if t.wide == 2:
                n = 2 if t.array == "w_in" else T2 // P
            self.outs.append(n)
            out += n
            block += t.k * t.wide
        self.free, ends = [None] * N_UNITS, 0
        for i, t in enumerate(TILES):
            b0, b1 = self.first_block[i], self.first_block[i] + t.k * t.wide
            for u in range(b0 // UNIT, (b1 - 1) // UNIT + 1):
                last = UNIT * (u + 1) - 1
                if b0 <= last < b1:
                    if t.wide == 2 or last == b1 - 1:
                        self.free[u] = ("tile", self.first_out[i] + self.outs[i])
                    else:
                        ends += 1
                        self.free[u] = ("unit", ends)


PLACE = Place()


def mixer_stack_kernel(nc, stream, vectors, consts, decay, gla_masks, positions, x_in, ctx_in, out):
    names = set()

    class Region:
        def __init__(self, start, size):
            self.at, self.end = start, start + size

        def put(self, name, shape, dtype=F32):
            size = 4 * int(np.prod(shape[1:]))
            size += -size % 32
            assert self.at + size <= self.end, (name, self.at + size - self.end)
            assert name not in names
            names.add(name)
            t = nc.alloc_sbuf_tensor_at(name, shape, dtype, offset=self.at)
            self.at += size
            return t

        def view(self):
            return Region(self.at, self.end - self.at)

        def part(self, size):
            self.at += size
            assert self.at <= self.end
            return Region(self.at - size, size)

    base = nc.sbuf_base + (-nc.sbuf_base % 64)
    sbuf = Region(base, nc.sbuf_usable_end - base)

    cst = sbuf.put("cst", [P, N_CONST])
    vec = sbuf.put("vec", [P, N_VEC])
    mod = sbuf.put("mod", [P, DEPTH, 6 * KD, 2])
    gain = sbuf.put("gain", [P, 2, KD, 2])
    silu_c = sbuf.put("silu_c", [P, KD, 2])
    eps = sbuf.put("eps", [P, 1])
    raw = sbuf.put("raw", [P, RAW, UNIT * P])
    w_hi = sbuf.put("w_hi", [P, SPLIT, UNIT * P], F32R)
    w_lo = sbuf.put("w_lo", [P, SPLIT, UNIT * P], F32R)
    xs = sbuf.put("xs", [P, KD, T2])
    h_hi = sbuf.put("h_hi", [P, KD, T2], F32R)
    h_lo = sbuf.put("h_lo", [P, KD, T2], F32R)
    sd = sbuf.put("sd", [P, T2])
    R0 = sbuf.part(4 * KD * T2)
    R1 = sbuf.part(4 * KD * T2)
    RY = sbuf.part(8 * NFF * SEQ)
    RE = sbuf.view()
    work = R0.view().put("work", [P, KD, T2])
    mix = R1.view().put("mix", [P, KD, T2])

    e = RE.view()
    dec = e.put("dec", [P, RH, 3 * P])
    gmask = e.put("gmask", [P, len(GLA_LEVELS) + 1, P], I32)
    cos1 = e.put("cos1", [P, SEQ])
    sin1 = e.put("sin1", [P, SEQ])
    ret_a = e.put("ret_a", [P, 3 * P])
    ga_t = e.put("ga_t", [RANK, SEQ])
    logit = e.put("logit", [P, 2, SEQ])
    gdec = e.put("gdec", [P, 2, SEQ])
    q_dec = e.put("q_dec", [P, 2, SEQ])
    k_dec = e.put("k_dec", [P, 2, SEQ])
    zrow = e.put("zrow", [P, SEQ + 2])
    r = R0.view()
    rq_raw = r.put("rq_raw", [P, RH, 2, SEQ])
    rqk = r.put("rqk", [P, RH, 2, SEQ])
    r = R0.view()
    g_acc = r.put("g_acc", [P, GH, 3, P])
    g_cum = r.put("g_cum", [P, 2, SEQ])
    o_sq = r.put("o_sq", [P, 2, 2 * SEQ])
    r = R0.view()
    gate_sb = r.put("gate_sb", [P, 2, T2])
    branch_sb = r.put("branch_sb", [P, 2, T2])
    prod_sb = r.put("prod_sb", [P, 2, T2])
    r = R0.view()
    ff_g = r.put("ff_g", [P, 2, SEQ])
    ff_u = r.put("ff_u", [P, 2, SEQ])
    ff_p = r.put("ff_p", [P, 2, SEQ])
    r = R1.view()
    silu_r = r.put("silu_r", [P, RH, SEQ])
    silu_g = r.put("silu_g", [P, GH, SEQ])
    conv_in = r.put("conv_in", [P, 2, 3, SEQ])
    conv_y = r.put("conv_y", [P, 2, SEQ])
    r = RY.view()
    y1_hi = r.put("y1_hi", [P, 12, SEQ], F32R)
    y1_lo = r.put("y1_lo", [P, 12, SEQ], F32R)
    rv = r.put("rv", [P, 2, RH * RD])
    gv = r.put("gv", [P, 2, GH * GV])
    o_ret = r.put("o_ret", [P, RH, SEQ])
    o_gla = r.put("o_gla", [P, GH, SEQ])
    gqk = r.put("gqk", [P, 2, 2, SEQ])
    r = RY.view()
    hid_hi = r.put("hid_hi", [P, NFF, SEQ], F32R)
    hid_lo = r.put("hid_lo", [P, NFF, SEQ], F32R)
    r = R0.view()
    pos_i = r.put("pos_i", [P, SEQ], I32)
    ang = r.put("ang", [P, SEQ])
    turns = r.put("turns", [P, SEQ])
    turns_i = r.put("turns_i", [P, SEQ], I32)
    ang2 = r.put("ang2", [P, SEQ])
    mod_rows = RY.view().put("mod_rows", [2, 6 * D])

    e = RE.view()
    z2 = e.put("z2", [P, 2, 2, SEQ + 2 * PAD])
    a_sq = e.put("a_sq", [P, T2])
    p_sb = e.put("p_sb", [P, 2, T2])
    pt_sb = e.put("pt_sb", [P, 2, T2])
    a_stat = e.put("a_stat", [P, 2, 4])
    a_rot = e.put("a_rot", [P, SEQ])
    e = RE.view()
    g_row = e.put("g_row", [MH, 2, T2])
    mx_row = e.put("mx_row", [MH, 2, T2])
    wgt = e.put("wgt", [P, 3, T2])
    em = e.put("em", [P, T2])
    nt = e.put("nt", [P, T2])
    pre = e.put("pre", [P, 4, 16])
    lsg = e.put("lsg", [P, 4, 16])
    fsum = e.put("fsum", [P, 4, 2, MH])
    gcol = e.put("gcol", [P, 4, 2, MH])
    r = R1.view()
    cin = r.put("cin", [P, 2, 2, T2])
    cy = r.put("cy", [P, 4, T2])
    r = R0.view()
    aq = r.put("aq", [P, AG + 1, T2])
    av_t = r.put("av_t", [P, T2])
    av = r.put("av", [P, 4, P])
    mg_t = r.put("mg_t", [16, T2])
    r = R0.view()
    s_sb = r.put("s_sb", [P, 4, T2])
    hacc = r.put("hacc", [P, 2, T2])
    smo = r.put("smo", [P, 2, T2])
    r = R0.view()
    up = r.put("up", [P, 2, 2, 2, SEQ + 2])
    e = RE.view()
    fc = e.put("fc", [P, 2, 2, T2])
    fh = e.put("fh", [P, 2, T2])
    r = RY.view()
    y2_hi = r.put("y2_hi", [P, KD, T2], F32R)
    y2_lo = r.put("y2_lo", [P, KD, T2], F32R)
    mqk = r.put("mqk", [P, 4, T2])
    mv = r.put("mv", [P, 4, MD])
    r = RY.view()
    hid2_hi = r.put("hid2_hi", [P, FF_HALF, T2], F32R)
    hid2_lo = r.put("hid2_lo", [P, FF_HALF, T2], F32R)

    def c_(name):
        return cst[:, CONST[name][0]:CONST[name][0] + CONST[name][1]]

    def v_(name, l, i=0, n=1):
        return vec[:, VEC[name, l][0] + i:VEC[name, l][0] + i + n]

    ident, ones = c_("ident"), c_("ones")

    banks = [nc.alloc_psum_tensor(f"bank{i}", [P, T2], F32) for i in range(8)]
    LIN, STAT, X = banks[0:2], banks[2], banks[3:8]


    def sem(name):
        return nc.alloc_semaphore(name)

    raw_loaded = [sem(f"raw_loaded{i}") for i in range(RAW)]
    ada_used = sem("ada_used")
    ada_out = sem("ada_out")
    mod_turned = sem("mod_turned")
    mod_ready = sem("mod_ready")
    hi_ready = sem("hi_ready")
    lo_ready = sem("lo_ready")
    unit_used = sem("unit_used")
    tile_done = sem("tile_done")
    tile_out = sem("tile_out")
    params_in, x_in_sem, stored = sem("params_in"), sem("x_loaded"), sem("stored")
    trig_args, trig_done = sem("trig_args"), sem("trig_done")
    silu_c_ready = sem("silu_c_ready")
    x_ready, sq_ready, stat_ready, std_ready = sem("x_ready"), sem("sq_ready"), sem("stat_ready"), sem("std_ready")
    norm_rows, hi_done, h_ready = sem("norm_rows"), sem("hi_done"), sem("h_ready")
    rot_done, qk_ready = sem("rot_done"), sem("qk_ready")
    score_done, ret_a_ready, ret_o_done, ret_o_out = (sem("ret_score_done"), sem("ret_a_ready"),
                                                      sem("ret_o_done"), sem("ret_o_out"))
    logit_done, logit_out, logit_ln = sem("logit_done"), sem("logit_out"), sem("logit_ln")
    lev_diff, lev_exp, lev_rows, lev_done, lev_taken = (sem("lev_diff"), sem("lev_exp"), sem("lev_rows"),
                                                        sem("lev_done"), sem("lev_taken"))
    gla_o_done, gla_o_out = sem("gla_o_done"), sem("gla_o_out")
    conv_used, conv_ready = sem("conv_used"), sem("conv_ready")
    mean_done, centred = sem("mean_done"), sem("centred")
    y_rows, y_hi_done, y_ready = sem("y_rows"), sem("y_hi_done"), sem("y_ready")
    merge_used, merged_rows, merged_hi, merged_ready = (sem("merge_used"), sem("merged_rows"), sem("merged_hi"),
                                                        sem("merged_ready"))
    ff_used, ff_rows, ff_hi, ff_ready = sem("ff_used"), sem("ff_rows"), sem("ff_hi"), sem("ff_ready")
    down_used = sem("down_used")
    av_turned, av_out = sem("av_turned"), sem("av_out")
    aq_scaled, aq_rot = sem("aq_scaled"), sem("aq_rot")
    a_score, a_neg, a_exp, a_prob, a_turned, a_pt, a_o_done, a_o_out = [
        sem(n) for n in ("a_score", "a_neg", "a_exp", "a_prob", "a_turned", "a_pt", "a_o_done", "a_o_out")]
    mg_turned, lsg_abs, lsg_ln, lsg_ready, fsum_done, gcol_ready, rows_turned, rows_ready = [
        sem(n) for n in ("mg_turned", "lsg_abs", "lsg_ln", "lsg_ready", "fsum_done", "gcol_ready",
                         "rows_turned", "rows_ready")]
    m_score, m_score_out, mx_done, w_arg, w_exp, w_ready, m_acc, em_in, em_out, m_taken, head_done = [
        sem(n) for n in ("m_score", "m_score_out", "mx_done", "w_arg", "w_exp", "w_ready", "m_acc", "em_in",
                         "em_out", "m_taken", "m_head_done")]
    cin_used, cy_ready, ln_rows, aq_ready, a_o_hi, pre_ready, merge2_used, den_abs = [
        sem(n) for n in ("cin_used", "cy_ready", "ln_rows", "aq_ready", "a_o_hi", "pre_ready", "merge2_used", "den_abs")]
    up_zero, fc_rows, fc_gate, ff2_rows, ff2_hi, ff2_ready = [
        sem(n) for n in ("up_zero", "fc_rows", "fc_gate", "ff2_rows", "ff2_hi", "ff2_ready")]
    dve_chain, act_chain = sem("dve_chain"), sem("act_chain")

    def spans(direction, tile, c0):
        own = tile * P
        if direction == 0:
            lo = max(own, c0)
            return [(lo, T2)], own if own >= c0 else None
        if tile < 2:
            if c0:
                return [(SEQ, T2)], None
            return ([(0, T2)] if tile == 1 else [(0, P), (SEQ, T2)]), own
        return [(SEQ, own + P)], own

    ORDER = {0: [0, 1, 2, 3], 1: [1, 0, 3, 2]}

    def hull(ranges):
        return ranges[0][0], ranges[-1][1]

    def att_steps(l):
        return [(q, j, g, T2 if q >= 2 else SEQ) for q in range(0 if l < DEPTH - 1 else 2, 4)
                for j in range(AG) for g in range(AKV)]

    def att_before(l):
        return sum(len(att_steps(i)) for i in range(l))

    with nc.Block() as block:

        @block.sync
        def _(sp):
            sp.dma_start(vec[:, :], vectors).then_inc(params_in, 16)
            sp.dma_start(cst[:, :], consts).then_inc(params_in, 16)

            def load(slot, unit):
                sp.dma_start(raw[:, slot, :], stream[unit]).then_inc(raw_loaded[slot], 16)

            for slot in range(RAW):
                load(slot, slot)
            sp.dma_start(dec[:, :, :], decay.rearrange("p (h n) -> p h n", h=RH)).then_inc(params_in, 16)
            sp.dma_start(gmask[:, :, :], gla_masks.rearrange("p (h n) -> p h n", n=P)).then_inc(params_in, 16)
            sp.dma_start(pos_i[:, :], positions).then_inc(params_in, 16)
            sp.dma_start(xs[:, :, SEQ:T2], x_in).then_inc(x_in_sem, 16)
            sp.dma_start(xs[:, :, 0:SEQ], ctx_in).then_inc(x_in_sem, 16)
            with sp.Fori(1, ADA_UNITS // RAW) as i:
                for slot in range(RAW):
                    sp.wait_ge(ada_used, i * RAW + (slot - RAW + 1))
                    load(slot, i * RAW + slot)
            for slot in range(RAW):
                sp.wait_ge(ada_used, ADA_UNITS - RAW + slot + 1)
                load(slot, ADA_UNITS + slot)
            with sp.Fori(1, N_UNITS // RAW) as i:
                for slot in range(RAW):
                    sp.wait_ge(lo_ready, i * RAW + (slot - RAW + 1))
                    load(slot, i * RAW + (ADA_UNITS + slot))
            for unit in range(N_UNITS // RAW * RAW, N_UNITS):
                sp.wait_ge(lo_ready, unit - RAW + 1)
                load(unit % RAW, ADA_UNITS + unit)
            sp.wait_ge(x_ready, 4 * DEPTH)
            sp.dma_start(out, xs[:, :, SEQ:T2]).then_inc(stored, 16)
            sp.wait_ge(stored, 16)

        @block.gpsimd
        def _(pool):
            step = RAW * SPLIT

            def low_part(unit, ordinal):
                pool.wait_ge(hi_ready, ordinal)
                nc.gpsimd.tensor_tensor(w_lo[:, unit % SPLIT, :], raw[:, unit % RAW, :], w_hi[:, unit % SPLIT, :],
                                        ALU.subtract).then_inc(lo_ready, 1)

            with pool.Fori(0, N_UNITS // step) as i:
                for j in range(step):
                    low_part(j, i * step + (j + 1))
            for unit in range(N_UNITS // step * step, N_UNITS):
                low_part(unit, unit + 1)

        @block.tensor
        def _(pe):
            E = Expect(pe)
            at = {"tile": 0, "unit": -1, "stat": 0}

            def wait_unit(u):
                if u > at["unit"]:
                    pe.wait_ge(lo_ready, u + 1)
                    at["unit"] = u

            def bank_of(n):
                if n >= len(LIN):
                    pe.wait_ge(tile_out, n - len(LIN) + 1)
                return LIN[n % len(LIN)]

            def product(x_hi, x_lo, c0, c1, count=1):
                for _ in range(count):
                    t, n, b = TILES[at["tile"]], PLACE.first_out[at["tile"]], PLACE.first_block[at["tile"]]
                    acc = bank_of(n)[:, c0:c1]
                    for k in range(t.k):
                        wait_unit((b + k) // UNIT)
                        slot, i = (b + k) // UNIT % SPLIT, (b + k) % UNIT
                        wh, wl = w_hi[:, slot, i * P:(i + 1) * P], w_lo[:, slot, i * P:(i + 1) * P]
                        nc.tensor.matmul(acc, wh, x_hi[:, k, c0:c1], start=k == 0, stop=False)
                        nc.tensor.matmul(acc, wh, x_lo[:, k, c0:c1], start=False, stop=False)
                        last = nc.tensor.matmul(acc, wl, x_hi[:, k, c0:c1], start=False, stop=k == t.k - 1)
                        if k == t.k - 1:
                            last.then_inc(tile_done, 1)
                        elif i == UNIT - 1:
                            last.then_inc(unit_used, 1)
                    at["tile"] += 1

            def values(first, count=1):
                for _ in range(count):
                    t, n, b = TILES[at["tile"]], PLACE.first_out[at["tile"]], PLACE.first_block[at["tile"]]
                    for i in range(PLACE.outs[at["tile"]]):
                        acc = bank_of(n + i)[:, 0:2 * P]
                        c = first + i * P
                        for k in range(t.k):
                            u, j = (b + 2 * k) // UNIT, (b + 2 * k) % UNIT
                            wait_unit(u)
                            wh, wl = w_hi[:, u % SPLIT, j * P:(j + 2) * P], w_lo[:, u % SPLIT, j * P:(j + 2) * P]
                            nc.tensor.matmul(acc, h_hi[:, k, c:c + P], wh, start=k == 0, stop=False)
                            nc.tensor.matmul(acc, h_hi[:, k, c:c + P], wl, start=False, stop=False)
                            last = nc.tensor.matmul(acc, h_lo[:, k, c:c + P], wh, start=False, stop=k == t.k - 1)
                        last.then_inc(tile_done, 1)
                    at["tile"] += 1

            def row_sums(rows, c0, c1, weights=ones):
                E.need(sq_ready)
                if at["stat"]:
                    E.need(std_ready)
                at["stat"] += 1
                for i, row in enumerate(rows):
                    last = nc.tensor.matmul(STAT[:, c0:c1], weights, row, start=i == 0, stop=i == len(rows) - 1)
                last.then_inc(stat_ready, 1)

            def norm_sums(c0, c1):
                row_sums([work[:, k, c0:c1] for k in range(KD)], c0, c1)

            E.need(silu_c_ready)
            for n in range(N_ADA):
                if n >= len(LIN):
                    pe.wait_ge(ada_out, n - len(LIN) + 1)
                for k in range(KD):
                    u = 2 * n + k // 4
                    if k % 4 == 0:
                        pe.wait_ge(raw_loaded[u % RAW], 16 * (u // RAW + 1))
                    last = nc.tensor.matmul(LIN[n % len(LIN)][0:2, 0:ADA_COLS], silu_c[:, k, :],
                                            raw[:, u % RAW, (k % 4) * ADA_COLS:(k % 4 + 1) * ADA_COLS],
                                            start=k == 0, stop=k == KD - 1)
                    if k % 4 == 3:
                        last.then_inc(ada_used, 1)
                if (n + 1) % (N_ADA // DEPTH) == 0:
                    l = n // (N_ADA // DEPTH)
                    pe.wait_ge(ada_out, n + 1)
                    for i in range(6 * KD):
                        last = nc.tensor.transpose(X[l][:, 2 * i:2 * i + 2], mod_rows[0:2, i * P:(i + 1) * P],
                                                   ident[0:2, 0:2])
                    last.then_inc(mod_turned, 1)

            c0, c1 = LAT
            for l in range(DEPTH):
                norm_sums(c0, c1)
                E.need(h_ready)
                if l == 0:
                    E.need(mod_ready, 2)
                product(h_hi, h_lo, c0, c1, 2 * RH)
                values(c0, 2)
                for h in range(RH):
                    pe.wait_ge(tile_out, PLACE.first_out[at["tile"] - 2])
                    if h >= 2:
                        E.need(qk_ready)
                    nc.tensor.matmul(X[h % 2][:, :], c_("rot_ret"), rq_raw[:, h, :, :], start=True, stop=True)\
                        .then_inc(rot_done, 1)
                product(h_hi, h_lo, c0, c1, 5)

                E.need(qk_ready, 2)

                def ret_scores(h):
                    q, k = rqk[:, h, 0, :], rqk[:, h, 1, :]
                    b = X[2 + h % 2]
                    if h >= 2:
                        E.need(ret_a_ready)
                    nc.tensor.matmul(b[:, 0:SEQ], k[:, 0:P], q, start=True, stop=True)
                    nc.tensor.matmul(b[:, SEQ:SEQ + P], k[:, P:SEQ], q[:, P:SEQ], start=True, stop=True)\
                        .then_inc(score_done, 1)

                ret_scores(0)
                pe.wait_ge(tile_out, PLACE.first_out[at["tile"] - 5])
                for h in range(RH):
                    if h + 1 < RH:
                        ret_scores(h + 1)
                    if h >= 2:
                        pe.wait_ge(ret_o_out, RH * l + h - 1)
                    pe.wait_ge(ret_a_ready, RH * l + h + 1)
                    o = X[4 * (1 - h % 2)][:, 0:SEQ]
                    nc.tensor.matmul(o, rv[:, 0, h * P:(h + 1) * P], ret_a[:, 0:SEQ], start=True, stop=False)
                    nc.tensor.matmul(o[:, P:SEQ], rv[:, 1, h * P:(h + 1) * P], ret_a[:, SEQ:SEQ + P],
                                     start=False, stop=True).then_inc(ret_o_done, 1)
                E.need(ret_a_ready, 2)
                values(c0, 2)
                pe.wait_ge(tile_out, PLACE.first_out[at["tile"] - 2])
                for i in range(2):
                    last = nc.tensor.matmul(X[0][:, i * SEQ:(i + 1) * SEQ],
                                            v_("gla_w_a2", l, i * P, P)[0:RANK, :], ga_t[:, :],
                                            start=True, stop=True)
                last.then_inc(logit_done, 1)
                for i in range(len(GLA_LEVELS) + 2):
                    diagonal = i == len(GLA_LEVELS) + 1
                    if not diagonal:
                        E.need(lev_rows)
                    if i:
                        E.need(lev_taken)
                    for h in range(GH):
                        rows = slice(GK * (h % 2), GK * (h % 2) + GK)
                        q = gqk[rows, 0, h // 2, :] if diagonal else q_dec[rows, h // 2, :]
                        k = gqk[rows, 1, h // 2, :] if diagonal else k_dec[rows, h // 2, :]
                        if i == 0:
                            last = nc.tensor.matmul(X[1 + h % 2][:, h // 2 * P:(h // 2 + 1) * P], k[:, 0:P],
                                                    q[:, P:SEQ], start=True, stop=True)
                            continue
                        for j in range(2):
                            c = (h // 2 * 2 + j) * P
                            last = nc.tensor.matmul(X[1 + h % 2][:, c:c + P], k[:, j * P:(j + 1) * P],
                                                    q[:, j * P:(j + 1) * P], start=True, stop=True)
                    last.then_inc(lev_done, 1)
                product(h_hi, h_lo, c0, c1, 12)
                E.need(lev_taken)
                for h in range(GH):
                    pe.wait_ge(ret_o_out, RH * (l + 1))
                    if h >= 2:
                        pe.wait_ge(gla_o_out, GH * l + h - 1)
                    o = X[4 * (1 - h % 2)][:, 0:SEQ]
                    nc.tensor.matmul(o, gv[:, 0, h * P:(h + 1) * P], g_acc[:, h, 0:2, :], start=True, stop=False)
                    nc.tensor.matmul(o[:, P:SEQ], gv[:, 1, h * P:(h + 1) * P], g_acc[:, h, 2, :],
                                     start=False, stop=True).then_inc(gla_o_done, 1)
                product(h_hi, h_lo, c0, c1, 8)
                for i in range(2):
                    pe.wait_ge(gla_o_out, GH * (l + 1))
                    nc.tensor.matmul(X[i][:, :], ones, o_ret[:, 2 * i:2 * i + 2, :], start=True, stop=True)\
                        .then_inc(mean_done, 1)
                for i in range(2):
                    row_sums([o_sq[:, i, :]], 0, T2)
                for i in range(2):
                    row_sums([o_sq[:, i, :]], 0, T2)
                for b in range(3):
                    E.need(y_ready)
                    for f in range(KD):
                        product(h_hi, h_lo, c0, c1)
                        product(y1_hi[:, 4 * b:4 * b + 4, :], y1_lo[:, 4 * b:4 * b + 4, :], 0, SEQ)
                E.need(merged_ready)
                product(y1_hi, y1_lo, 0, SEQ, KD)
                norm_sums(c0, c1)
                norm_sums(c0, c1)
                E.need(h_ready)
                product(h_hi, h_lo, c0, c1, 2 * NFF)
                E.need(ff_ready, NFF)
                product(hid_hi, hid_lo, 0, SEQ, KD)
                norm_sums(c0, c1)

            for l in range(DEPTH):
                c0 = 0 if l < DEPTH - 1 else SEQ
                cols = slice(c0, T2)
                norm_sums(0, T2)
                E.need(h_ready)
                product(h_hi, h_lo, c0, T2, 8)
                product(h_hi, h_lo, c0, T2, AG)
                product(h_hi, h_lo, 0, T2, 3)
                for j in range(AG + 2):
                    if j <= AG:
                        row_sums([a_sq[:, c0 if j < AG else 0:T2]], c0 if j < AG else 0, T2, c_("one64"))
                    if j:
                        E.need(aq_scaled)
                        if j > 2:
                            E.need(aq_ready)
                        nc.tensor.matmul(X[j % 2][:, 0:SEQ], c_("rot_att"), aq[:, j - 1, SEQ:T2], start=True,
                                         stop=True).then_inc(aq_rot, 1)
                pe.wait_ge(tile_out, PLACE.first_out[at["tile"] - 1])
                for i in range(4):
                    last = nc.tensor.transpose(X[2][:, i * P:(i + 1) * P], av_t[:, i * P:(i + 1) * P], ident)
                last.then_inc(av_turned, 1)
                E.need(aq_ready, 2)
                steps = att_steps(l)
                before = att_before(l)
                for i in range(len(steps) + 2):
                    if i < len(steps):
                        q, j, g, keys = steps[i]
                        rows = slice(AD * g, AD * g + AD)
                        if i >= 2:
                            pe.wait_ge(a_exp, before + i - 1)
                        nc.tensor.matmul(X[i % 2][:, 0:keys], aq[rows, j, q * P:(q + 1) * P], aq[rows, AG, 0:keys],
                                         start=True, stop=True).then_inc(a_score, 1)
                    if 1 <= i <= len(steps):
                        keys = steps[i - 1][3]
                        E.need(a_prob)
                        if i == 1:
                            E.need(av_out)
                        for t in range(keys // P):
                            last = nc.tensor.transpose(X[2 + (i - 1) % 2][:, t * P:(t + 1) * P],
                                                       p_sb[:, (i - 1) % 2, t * P:(t + 1) * P], ident)
                        last.then_inc(a_turned, 1)
                    if i >= 2:
                        q, j, g, keys = steps[i - 2]
                        E.need(a_pt)
                        if g == 0 and i > 2:
                            pe.wait_ge(a_o_out, (before + i - 2) // 2)
                        for t in range(keys // P):
                            last = nc.tensor.matmul(X[4][AD * g:AD * g + AD, 0:P], av[:, t, AD * g:AD * g + AD],
                                                    pt_sb[:, i % 2, t * P:(t + 1) * P], start=t == 0,
                                                    stop=t == keys // P - 1)
                        last.then_inc(a_o_done, 1)
                E.need(cy_ready)
                pe.wait_ge(a_exp, att_before(l + 1))
                for i in range(4):
                    last = nc.tensor.matmul(X[0][:, cols], ones, cy[:, i, cols], start=i == 0, stop=i == 3)
                last.then_inc(mean_done, 1)
                row_sums([cin[:, i // 2, i % 2, cols] for i in range(4)], c0, T2)
                for i in range(4):
                    last = nc.tensor.transpose(X[0][:, i * 16:(i + 1) * 16], mg_t[:, i * P:(i + 1) * P], ident[0:16, 0:16])
                last.then_inc(mg_turned, 1)
                E.need(lsg_ready)
                for i in range(4):
                    for d in range(2):
                        if d == 0:
                            parts = [(t, "ones") for t in range(i)] + [(i, "upto")]
                        elif i < 2:
                            parts = [(t, "ones") for t in range(i + 1, 2)] + [(i, "from")]
                        else:
                            parts = [(0, "ones"), (1, "ones")] + [(t, "ones") for t in range(i + 1, 4)] + [(i, "from")]
                        for n, (t, name) in enumerate(parts):
                            last = nc.tensor.matmul(X[1][:, (2 * i + d) * MH:(2 * i + d + 1) * MH], c_(name),
                                                    lsg[:, t, 8 * d + MH:8 * d + 2 * MH], start=n == 0,
                                                    stop=n == len(parts) - 1)
                last.then_inc(fsum_done, 1)
                E.need(gcol_ready)
                pe.wait_ge(a_o_out, att_before(l + 1) // 2)
                for d in range(2):
                    for i in range(4):
                        nc.tensor.transpose(X[2 + d][0:MH, i * P:(i + 1) * P], gcol[:, i, d, :], ident)
                        last = nc.tensor.transpose(X[4 * d][0:MH, i * P:(i + 1) * P], fsum[:, i, d, :], ident)
                last.then_inc(rows_turned, 1)
                for b in range(2):
                    E.need(y_ready)
                    for f in range(KD):
                        product(h_hi, h_lo, c0, T2)
                        product(y2_hi[:, 4 * b:4 * b + 4, :], y2_lo[:, 4 * b:4 * b + 4, :], c0, T2)
                E.need(rows_ready)

                def queries_keys():
                    product(h_hi, h_lo, c0, T2, 2)
                    product(h_hi, h_lo, 0, T2, 2)

                queries_keys()
                for h in range(MH):
                    n_head = l * MH + h
                    pe.wait_ge(tile_out, PLACE.first_out[at["tile"]])
                    for t in range(4):
                        if t >= 2:
                            pe.wait_ge(m_score_out, 4 * n_head + t - 1)
                        for i in range(2):
                            last = nc.tensor.matmul(X[t % 2][:, cols], mqk[:, 2 + i, t * P:(t + 1) * P],
                                                    mqk[:, i, cols], start=i == 0, stop=i == 1)
                        last.then_inc(m_score, 1)
                    head = c_("head_row")[0:MH, h * P:(h + 1) * P]
                    for d in range(2):
                        def running_max():
                            nc.tensor.matmul(X[2][:, cols], head, mx_row[:, d, cols], start=True, stop=True)\
                                .then_inc(mx_done, 1)
                            nc.tensor.matmul(X[4][:, cols], head, g_row[:, d, cols], start=True, stop=True)\
                                .then_inc(em_in, 1)

                        if d == 0:
                            running_max()
                            values(0)
                            product(h_hi, h_lo, c0, T2, 2)
                            pe.wait_ge(tile_out, PLACE.first_out[at["tile"] - 2])
                            pe.wait_ge(m_score_out, 4 * n_head + 4)
                        else:
                            pe.wait_ge(w_arg, 8 * n_head + 4)
                            pe.wait_ge(em_out, 2 * n_head + 1)
                            running_max()
                            pe.wait_ge(m_taken, 2 * n_head + 1)
                        for n, t in enumerate(ORDER[d]):
                            E.need(w_ready)
                            ranges = spans(d, t, c0)[0]
                            for i in range(3):
                                acc = X[3] if i == 0 else X[i - 1]
                                for a, b in ranges:
                                    w = wgt[:, (4 * d + n) % 3, a:b]
                                    left = ones if i == 0 else mv[:, t, (i - 1) * P:i * P]
                                    last = nc.tensor.matmul(acc[:, a:b], left, w, start=n == 0, stop=n == 3,
                                                            skip_group_check=True)
                            last.then_inc(m_acc, 1)
                    if h + 1 < MH:
                        queries_keys()
                    row_sums([s_sb[:, i, cols] for i in range(2)], c0, T2)
                E.need(y_ready)
                for f in range(KD):
                    product(h_hi, h_lo, c0, T2)
                    product(y2_hi, y2_lo, c0, T2)
                E.need(merged_ready)
                product(h_hi, h_lo, c0, T2, KD)
                norm_sums(c0, T2)
                E.need(h_ready)
                for half in range(2):
                    product(h_hi, h_lo, c0, T2, 2 * FF_HALF)
                    E.need(ff2_ready, FF_HALF)
                    product(hid2_hi, hid2_lo, c0, T2, KD)

        @block.scalar
        def _(act):
            E = Expect(act)
            C = Chain(act, act_chain)
            at = {"tile": 0, "unit": 0}

            def split_through(u):
                while at["unit"] <= min(u, N_UNITS - 1):
                    n = at["unit"]
                    act.wait_ge(raw_loaded[n % RAW], 16 * ((n + ADA_UNITS) // RAW + 1))
                    if n >= SPLIT:
                        kind, count = PLACE.free[n - SPLIT]
                        act.wait_ge(tile_done if kind == "tile" else unit_used, count)
                    nc.scalar.activation(w_hi[:, n % SPLIT, :], raw[:, n % RAW, :], ACT.Copy).then_inc(hi_ready, 1)
                    at["unit"] += 1

            def next_tile():
                i = at["tile"]
                first, t = PLACE.first_block[i], TILES[i]
                split_through(max((first + t.k * t.wide - 1) // UNIT, first // UNIT + SPLIT - 1))
                at["tile"] += 1
                return PLACE.first_out[i]

            def take(dst, c0, c1, func=ACT.Copy, scale=1.0, bias=0.0):
                n = next_tile()
                E.need(tile_done)
                src = LIN[n % len(LIN)][:dst.shape[0], c0:c1]
                if len(dst.shape) == 3:
                    src = src.rearrange("p (s n) -> p s n", n=SEQ)
                nc.scalar.activation(dst, src, func, bias=bias, scale=scale).then_inc(tile_out, 1)

            def take_values(dst, v):
                n = next_tile()
                for i in range(PLACE.outs[at["tile"] - 1]):
                    E.need(tile_done)
                    nc.scalar.activation(dst[:, i, v * 2 * P:(v + 1) * 2 * P], LIN[(n + i) % len(LIN)][:, 0:2 * P],
                                         ACT.Copy).then_inc(tile_out, 1)

            def square_rows(src, c0, c1):
                for i in range(2):
                    half = slice(i * KD // 2, (i + 1) * KD // 2)
                    last = nc.scalar.activation(work[:, half, c0:c1], src[:, half, c0:c1], ACT.Square)
                last.then_inc(sq_ready, 1)

            def root(c0, c1, n):
                E.need(stat_ready)
                nc.scalar.activation(sd[:, c0:c1], STAT[:, c0:c1], ACT.Sqrt, bias=eps[:, 0:1], scale=1.0 / n)\
                    .then_inc(std_ready, 1)

            def split_norm(c0, c1):
                for k in range(KD):
                    E.need(norm_rows)
                    nc.scalar.activation(h_hi[:, k, c0:c1], work[:, k, c0:c1], ACT.Copy).then_inc(hi_done, 1)

            act.wait_ge(params_in, 16 * 5)
            at_c = VEC["c"][0]
            nc.scalar.activation(silu_c[:, :, :], vec[:, at_c:at_c + 2 * KD], ACT.Silu).then_inc(silu_c_ready, 1)
            E.need(trig_args)
            nc.scalar.activation(sin1[:, :], ang[:, :], ACT.Sin)
            nc.scalar.activation(cos1[:, :], ang2[:, :], ACT.Sin).then_inc(trig_done, 1)
            for n in range(N_ADA):
                act.wait_ge(ada_used, 2 * n + 2)
                l, c = n // (N_ADA // DEPTH), n % (N_ADA // DEPTH)
                if c == 0 and l:
                    E.need(mod_turned)
                nc.scalar.activation(mod_rows[0:2, c * ADA_COLS:(c + 1) * ADA_COLS],
                                     LIN[n % len(LIN)][0:2, 0:ADA_COLS], ACT.Copy).then_inc(ada_out, 1)

            act.wait_ge(x_in_sem, 32)
            c0, c1 = LAT
            for l in range(DEPTH):
                if l:
                    E.need(x_ready)
                square_rows(xs, c0, c1)
                root(c0, c1, D)
                split_through(SPLIT - 1)
                split_norm(c0, c1)
                for h in range(RH):
                    take(rq_raw[:, h, 0, :], c0, c1, scale=RD ** -0.5)
                    take(rq_raw[:, h, 1, :], c0, c1)
                for v in range(2):
                    take_values(rv, v)
                for i in range(2):
                    take(gqk[:, 0, i, :], c0, c1, scale=GK ** -0.5)
                    take(gqk[:, 1, i, :], c0, c1)
                take(ga_t[:, :], c0, c1)

                def ret_out(h):
                    E.need(ret_o_done)
                    nc.scalar.activation(o_ret[:, h, :], X[4 * (1 - h % 2)][:, 0:SEQ], ACT.Copy)\
                        .then_inc(ret_o_out, 1)

                for h in range(RH):
                    ret_out(h)
                for v in range(2):
                    take_values(gv, v)
                E.need(logit_done)
                for i in range(2):
                    last = nc.scalar.activation(logit[:, i, :], X[0][:, i * SEQ:(i + 1) * SEQ], ACT.Identity,
                                                bias=v_("gla_b_a", l, i))
                last.then_inc(logit_out, 1)
                act.wait_ge(logit_out, l + 1)
                C.do(nc.scalar.activation(gdec[:, :, :], logit[:, :, :], ACT.Abs))
                C.settle()
                C.do(nc.scalar.activation(gdec[:, :, :], gdec[:, :, :], ACT.Exp, scale=-1.0))
                C.settle()
                nc.scalar.activation(gdec[:, :, :], gdec[:, :, :], ACT.Ln, bias=1.0).then_inc(logit_ln, 1)
                for i in range(len(GLA_LEVELS) + 1):
                    E.need(lev_diff)
                    C.do(nc.scalar.activation(gdec[:, :, :], gdec[:, :, :], ACT.Abs))
                    C.settle()
                    nc.scalar.activation(gdec[:, :, :], gdec[:, :, :], ACT.Exp, scale=-1.0 / GTAU).then_inc(lev_exp, 1)
                for i in range(4):
                    if i >= 2:
                        act.wait_ge(conv_used, 4 * l + i - 1)
                    for j in range(3):
                        take(conv_in[:, i % 2, j, :], c0, c1)

                def split_y(b, rows):
                    E.need(y_rows)
                    nc.scalar.activation(y1_hi[:, b, :], rows, ACT.Copy).then_inc(y_hi_done, 1)

                for h in range(GH):
                    E.need(gla_o_done)
                    nc.scalar.activation(o_gla[:, h, :], X[4 * (1 - h % 2)][:, 0:SEQ], ACT.Copy)\
                        .then_inc(gla_o_out, 1)
                for i in range(RH):
                    take(silu_r[:, i, :], c0, c1, ACT.Silu)
                for i in range(GH):
                    take(silu_g[:, i, :], c0, c1, ACT.Silu)
                for b, (o, dim) in enumerate(((o_ret, RD), (o_gla, GV))):
                    for i in range(2):
                        if b == 0:
                            E.need(centred)
                        else:
                            act.wait_ge(gla_o_out, GH * (l + 1))
                        nc.scalar.activation(o_sq[:, i, :], o[:, 2 * i:2 * i + 2, :], ACT.Square).then_inc(sq_ready, 1)
                        root(0, T2, dim)
                        for j in range(2):
                            split_y(4 + 4 * b + 2 * i + j, o[:, 2 * i + j, :])
                for b in range(3):
                    for f in range(KD):
                        if b or f >= 2:
                            act.wait_ge(merge_used, 3 * KD * l + KD * b + f - 1)
                        take(gate_sb[:, f % 2, 0:SEQ], c0, c1, ACT.Sigmoid)
                        take(branch_sb[:, f % 2, 0:SEQ], 0, SEQ)
                for f in range(KD):
                    E.need(merged_rows)
                    nc.scalar.activation(y1_hi[:, f, :], mix[:, f, 0:SEQ], ACT.Copy).then_inc(merged_hi, 1)
                for f in range(KD):
                    take(mix[:, f, c0:c1], 0, SEQ)
                act.wait_ge(tile_out, E.seen[tile_done.name])
                square_rows(mix, c0, c1)
                root(c0, c1, D)
                E.need(x_ready)
                square_rows(xs, c0, c1)
                root(c0, c1, D)
                split_norm(c0, c1)
                for t in range(NFF):
                    take(ff_g[:, t % 2, :], c0, c1, ACT.Silu)
                    take(ff_u[:, t % 2, :], c0, c1)
                    if t >= 1:
                        E.need(ff_rows)
                        nc.scalar.activation(hid_hi[:, t - 1, :], ff_p[:, (t - 1) % 2, :], ACT.Copy).then_inc(ff_hi, 1)
                E.need(ff_rows)
                nc.scalar.activation(hid_hi[:, NFF - 1, :], ff_p[:, (NFF - 1) % 2, :], ACT.Copy).then_inc(ff_hi, 1)
                for f in range(KD):
                    take(mix[:, f, c0:c1], 0, SEQ)
                act.wait_ge(tile_out, E.seen[tile_done.name])
                square_rows(mix, c0, c1)
                root(c0, c1, D)

            for l in range(DEPTH):
                c0 = 0 if l < DEPTH - 1 else SEQ
                cols = slice(c0, T2)
                E.need(x_ready)
                square_rows(xs, 0, T2)
                root(0, T2, D)
                split_norm(0, T2)
                for i in range(4):
                    if i >= 2:
                        act.wait_ge(cin_used, 4 * l + i - 1)
                    take(cin[:, i % 2, 0, cols], c0, T2)
                    take(cin[:, i % 2, 1, cols], c0, T2, ACT.Sigmoid)
                for j in range(AG):
                    take(aq[:, j, cols], c0, T2)
                take(aq[:, AG, :], 0, T2)
                take(av_t[:, :], 0, T2)
                take(mg_t[:, :], 0, T2)
                act.wait_ge(tile_out, E.seen[tile_done.name])
                for j in range(AG + 1):
                    a = c0 if j < AG else 0
                    nc.scalar.activation(a_sq[:, a:T2], aq[:, j, a:T2], ACT.Square).then_inc(sq_ready, 1)
                    if j:
                        E.need(aq_scaled)
                    root(a, T2, AD)
                E.need(aq_scaled)
                E.need(av_turned)
                nc.scalar.activation(av[:, :, :], X[2][:, :].rearrange("p (t n) -> p t n", n=P), ACT.Copy)\
                    .then_inc(av_out, 1)
                steps, before = att_steps(l), att_before(l)
                for i in range(len(steps) + 2):
                    if i < len(steps):
                        keys = steps[i][3]
                        E.need(a_neg)
                        nc.scalar.activation(p_sb[:, i % 2, 0:keys], X[i % 2][:, 0:keys], ACT.Exp,
                                             bias=a_stat[:, i % 2, 1:2], scale=AD ** -0.5,
                                             accum_out=a_stat[:, i % 2, 2:3]).then_inc(a_exp, 1)
                    if 1 <= i <= len(steps):
                        keys, b = steps[i - 1][3], (i - 1) % 2
                        E.need(a_turned)
                        if i > 2:
                            act.wait_ge(a_o_done, before + i - 2)
                        nc.scalar.activation(pt_sb[:, b, 0:keys], X[2 + b][:, 0:keys], ACT.Copy).then_inc(a_pt, 1)
                    if i >= 2 and steps[i - 2][2] == 1:
                        q, j, _, _ = steps[i - 2]
                        act.wait_ge(a_o_done, before + i - 1)
                        nc.scalar.activation(y2_hi[:, 4 + j, q * P:(q + 1) * P], X[4][:, 0:P], ACT.Copy)\
                            .then_inc(a_o_hi, 1)
                E.need(centred)
                nc.scalar.activation(cin[:, :, :, cols].rearrange("p a b n -> p (a b) n"), cy[:, :, cols], ACT.Square)\
                    .then_inc(sq_ready, 1)
                root(c0, T2, CONV)
                for i in range(4):
                    E.need(ln_rows)
                    C.do(nc.scalar.activation(cy[:, i, cols], cy[:, i, cols], ACT.Silu, bias=v_("conv_ln_b_2", l, i),
                                              scale=v_("conv_ln_w_2", l, i)))
                for i in range(4):
                    if i == 0:
                        C.settle()
                    nc.scalar.activation(y2_hi[:, i, cols], cy[:, i, cols], ACT.Copy).then_inc(y_hi_done, 1)
                E.need(pre_ready)
                C.do(nc.scalar.activation(lsg[:, :, :], pre[:, :, :], ACT.Abs))
                C.settle()
                C.do(nc.scalar.activation(lsg[:, :, :], lsg[:, :, :], ACT.Exp, scale=-1.0))
                C.settle()
                nc.scalar.activation(lsg[:, :, :], lsg[:, :, :], ACT.Ln, bias=1.0).then_inc(lsg_ln, 1)

                def take_merge(b, gate):
                    for f in range(KD):
                        if b % 3 or f >= 2:
                            act.wait_ge(merge2_used, KD * b + f - 1)
                        take(gate_sb[:, f % 2, cols], c0, T2, ACT.Sigmoid, bias=v_("branch_gate_b_2", l, gate * KD + f))
                        take(branch_sb[:, f % 2, cols], c0, T2)

                take_merge(3 * l, 0)
                take_merge(3 * l + 1, 2)

                def take_queries_keys():
                    for i in range(2):
                        take(mqk[:, i, cols], c0, T2)
                    for i in range(2):
                        take(mqk[:, 2 + i, :], 0, T2, scale=MD ** -0.5)

                take_queries_keys()
                act.wait_ge(merge2_used, KD * (3 * l + 2))
                for h in range(MH):
                    n_head = l * MH + h
                    for t in range(4):
                        E.need(m_score)
                        nc.scalar.activation(s_sb[:, t, cols], X[t % 2][:, cols], ACT.Copy).then_inc(m_score_out, 1)
                    for d in range(2):
                        if d == 0:
                            take_values(mv, 0)
                            for i in range(2):
                                take(smo[:, i, cols], c0, T2, ACT.Sigmoid)
                        E.need(em_in)
                        if d:
                            act.wait_ge(m_taken, 2 * n_head + 1)
                        nc.scalar.activation(em[:, cols], X[4][:, cols], ACT.Exp, scale=-1.0).then_inc(em_out, 1)
                        for n, t in enumerate(ORDER[d]):
                            E.need(w_arg)
                            a, b = hull(spans(d, t, c0)[0])
                            w = wgt[:, (4 * d + n) % 3, a:b]
                            nc.scalar.activation(w, w, ACT.Exp, scale=-1.0).then_inc(w_exp, 1)
                        act.wait_ge(m_acc, 8 * n_head + 4 * d + 4)
                        nc.scalar.activation(nt[:, cols], X[3][:, cols], ACT.Abs).then_inc(den_abs, 1)
                    if h + 1 < MH:
                        take_queries_keys()
                    E.need(head_done)
                    nc.scalar.activation(s_sb[:, 0:2, cols], hacc[:, :, cols], ACT.Square).then_inc(sq_ready, 1)
                    root(c0, T2, MD)
                    for i in range(2):
                        E.need(y_rows)
                        nc.scalar.activation(y2_hi[:, 2 * h + i, cols], hacc[:, i, cols], ACT.Copy).then_inc(y_hi_done, 1)
                take_merge(3 * l + 2, 1)
                for f in range(KD):
                    E.need(merged_rows)
                    nc.scalar.activation(h_hi[:, f, cols], mix[:, f, cols], ACT.Copy).then_inc(merged_hi, 1)
                for f in range(KD):
                    take(mix[:, f, cols], c0, T2)
                E.need(x_ready)
                square_rows(xs, c0, T2)
                root(c0, T2, D)
                split_norm(c0, T2)
                E.need(up_zero)
                first = c0 // SEQ
                for half in range(2):
                    n0 = NFF * l + FF_HALF * half
                    for t in range(FF_HALF + 2):
                        if t < FF_HALF:
                            if t >= 2:
                                act.wait_ge(fc_rows, n0 + t - 1)
                            for j in range(2):
                                take(up[:, t % 2, j, first:2, 1:SEQ + 1], c0, T2)
                        if 1 <= t <= FF_HALF:
                            E.need(fc_rows)
                            g = fc[:, (t - 1) % 2, 1, cols]
                            nc.scalar.activation(g, g, ACT.Silu).then_inc(fc_gate, 1)
                        if t >= 2:
                            E.need(ff2_rows)
                            nc.scalar.activation(hid2_hi[:, t - 2, cols], fh[:, t % 2, cols], ACT.Copy).then_inc(ff2_hi, 1)
                    for f in range(KD):
                        take(mix[:, f, cols], c0, T2)

        @block.vector
        def _(dve):
            E = Expect(dve)
            C = Chain(dve, dve_chain)
            V = nc.vector
            MUL, ADD, SUB = ALU.mult, ALU.add, ALU.subtract

            def inverse_root(c0, c1):
                E.need(std_ready)
                C.do(V.reciprocal(sd[:, c0:c1], sd[:, c0:c1]))
                C.settle()

            def split_low_norm(c0, c1):
                for k in range(KD):
                    E.need(hi_done)
                    last = V.tensor_tensor(h_lo[:, k, c0:c1], work[:, k, c0:c1], h_hi[:, k, c0:c1], SUB)
                last.then_inc(h_ready, 1)

            def norm1(name, l):
                c0, c1 = LAT
                inverse_root(c0, c1)
                for k in range(KD):
                    V.scalar_tensor_tensor(work[:, k, c0:c1], xs[:, k, c0:c1], v_(name, l, k), sd[:, c0:c1],
                                           MUL, MUL).then_inc(norm_rows, 1)
                split_low_norm(c0, c1)

            def add_normed(name, l):
                c0, c1 = LAT
                inverse_root(c0, c1)
                for k in range(KD):
                    C.do(V.scalar_tensor_tensor(work[:, k, c0:c1], mix[:, k, c0:c1], v_(name, l, k), sd[:, c0:c1],
                                                MUL, MUL))
                C.settle()
                last = V.tensor_tensor(xs[:, :, c0:c1], xs[:, :, c0:c1], work[:, :, c0:c1], ADD)
                last.then_inc(x_ready, 1)

            dve.wait_ge(params_in, 16 * 5)
            C.do(V.memset(eps[:, :], EPS))
            C.do(V.tensor_copy(ang[:, :], pos_i[:, :]))
            C.settle()
            C.do(V.tensor_scalar(ang[:, :], ang[:, :], c_("inv_freq"), None, MUL))
            C.settle()
            ROUND = 1.5 * 2.0 ** 23
            T1 = 6.28125
            T2_ = 0.0019350051879882812
            T3 = 2 * np.pi - T1 - T2_
            for dst, quarter in ((ang2, 0.25), (ang, 0.0)):
                C.do(V.tensor_scalar(turns[:, :], ang[:, :], float(1 / (2 * np.pi)), quarter, MUL, ADD))
                C.settle()
                C.do(V.tensor_scalar(turns[:, :], turns[:, :], ROUND, ROUND, ADD, SUB))
                C.settle()
                src = ang
                for part in (T1, T2_, T3):
                    C.do(V.scalar_tensor_tensor(dst[:, :], turns[:, :], -float(part), src[:, :], MUL, ADD))
                    C.settle()
                    src = dst
                if quarter:
                    C.do(V.tensor_scalar(dst[:, :], dst[:, :], float(np.pi / 2), None, ADD))
                    C.settle()
                last = V.tensor_scalar(dst[:, :], dst[:, :], 3.1415925, -3.1415925, ALU.min, ALU.max)
                if quarter:
                    C.do(last)
            last.then_inc(trig_args, 1)
            for l in range(DEPTH):
                E.need(mod_turned)
                turned = X[l][:, 0:2 * 6 * KD].rearrange("p (i s) -> p i s", s=2)
                V.tensor_tensor(mod[:, l, :, :], turned,
                                v_("ada_b_2", l, 0, 6 * KD).unsqueeze(2).to_broadcast([P, 6 * KD, 2]), ADD)\
                    .then_inc(mod_ready, 1)
            E.need(trig_done)

            dve.wait_ge(x_in_sem, 32)
            c0, c1 = LAT
            for l in range(DEPTH):
                norm1("norm_mix_pre", l)
                E.need(tile_out, 2 * RH + 4)
                both = [P, 2, SEQ]
                for h in range(RH):
                    E.need(rot_done)
                    C.do(V.tensor_tensor(rqk[:, h, :, :], rq_raw[:, h, :, :], cos1[:, :].unsqueeze(1).to_broadcast(both), MUL))
                    C.settle()
                    C.do(V.tensor_tensor(rq_raw[:, h, :, :], X[h % 2][:, :].rearrange("p (a n) -> p a n", a=2),
                                         sin1[:, :].unsqueeze(1).to_broadcast(both), MUL))
                    C.settle()
                    V.tensor_tensor(rqk[:, h, :, :], rqk[:, h, :, :], rq_raw[:, h, :, :], ADD).then_inc(qk_ready, 1)
                for h in range(RH):
                    E.need(score_done)
                    if h or l:
                        E.need(ret_o_done)
                    V.tensor_tensor(ret_a[:, :], X[2 + h % 2][:, 0:3 * P], dec[:, h, :], MUL).then_inc(ret_a_ready, 1)
                E.need(tile_out, 5 + 4)
                E.need(logit_out)
                E.need(logit_ln)
                C.do(V.tensor_scalar(logit[:, :, :], logit[:, :, :], 0.0, None, ALU.min))
                C.settle()
                C.do(V.tensor_tensor(logit[:, :, :], logit[:, :, :], gdec[:, :, :], SUB))
                C.do(V.memset(k_dec[:, 0, :], 1.0))
                C.do(V.memset(g_acc[:, :, :, :], 0.0))
                C.settle()
                for i in range(2):
                    C.do(V.tensor_tensor_scan(g_cum[:, i, :], k_dec[:, 0, :], logit[:, i, :], 0.0, MUL, ADD))
                C.settle()

                def pairs(level):
                    return gmask[:, level, :].unsqueeze(1).unsqueeze(1).to_broadcast([P, 2, 2, P])

                def blocks_of(bank):
                    return bank[:, :].rearrange("p (h j n) -> p h j n", h=2, j=2)

                for i, m in enumerate([P] + GLA_LEVELS):
                    blocks = g_cum[:, :, :].rearrange("p a (b t) -> p (a b) t", t=2 * m)
                    middle = blocks[:, :, m - 1:m].to_broadcast([P, 2 * SEQ // (2 * m), 2 * m])
                    V.tensor_tensor(gdec[:, :, :].rearrange("p a (b t) -> p (a b) t", t=2 * m), blocks, middle, SUB)\
                        .then_inc(lev_diff, 1)
                    E.need(lev_exp)
                    C.do(V.tensor_tensor(q_dec[:, :, :], gqk[:, 0, :, :], gdec[:, :, :], MUL))
                    V.tensor_tensor(k_dec[:, :, :], gqk[:, 1, :, :], gdec[:, :, :], MUL).then_inc(lev_rows, 1)
                    dve.wait_ge(lev_done, (len(GLA_LEVELS) + 2) * l + i + 1)
                    for odd in range(2):
                        if i == 0:
                            last = V.tensor_copy(g_acc[:, odd::2, 1, :],
                                                 X[1 + odd][:, 0:2 * P].rearrange("p (h n) -> p h n", n=P))
                        else:
                            last = V.copy_predicated(g_acc[:, odd::2, 0::2, :], pairs(i - 1), blocks_of(X[1 + odd]))
                    last.then_inc(lev_taken, 1)
                dve.wait_ge(lev_done, (len(GLA_LEVELS) + 2) * (l + 1))
                for odd in range(2):
                    last = V.copy_predicated(g_acc[:, odd::2, 0::2, :], pairs(len(GLA_LEVELS)), blocks_of(X[1 + odd]))
                last.then_inc(lev_taken, 1)
                C.do(V.memset(zrow[:, 0:2], 0.0))
                for i in range(4):
                    E.need(tile_out, 3)
                    u, g, b = (conv_in[:, i % 2, j, :] for j in range(3))
                    C.do(V.tensor_tensor(zrow[:, 2:], u, g, MUL))
                    C.settle()
                    y = conv_y[:, i % 2, :]
                    C.do(V.tensor_scalar(y, zrow[:, 0:SEQ], v_("conv_w", l, i), None, MUL))
                    for j in (1, 2):
                        C.settle()
                        C.do(V.scalar_tensor_tensor(y, zrow[:, j:j + SEQ], v_("conv_w", l, 4 * j + i), y, MUL, ADD))
                    C.settle()
                    C.do(V.tensor_tensor(y, y, b, MUL))
                    C.settle()
                    V.tensor_copy(y1_hi[:, i, :], y).then_inc(conv_used, 1)
                    dve.wait_ge(conv_used, 4 * l + i + 1)
                    last = V.tensor_tensor(y1_lo[:, i, :], y, y1_hi[:, i, :], SUB)
                    if i < 3:
                        C.do(last)
                last.then_inc(y_ready, 1)
                E.need(tile_out, RH + GH)
                for b, (o, gate, name) in enumerate(((o_ret, silu_r, "ret_gn_w"), (o_gla, silu_g, "gla_gn_w"))):
                    if b == 0:
                        for i in range(2):
                            E.need(mean_done)
                            two = o[:, 2 * i:2 * i + 2, :]
                            V.scalar_tensor_tensor(two, X[i][:, :].rearrange("p (a n) -> p a n", a=2), -1.0 / RD, two,
                                                   MUL, ADD).then_inc(centred, 1)
                    for i in range(2):
                        inverse_root(0, T2)
                        for j in range(2):
                            h = 2 * i + j
                            C.do(V.scalar_tensor_tensor(o[:, h, :], o[:, h, :], v_(name, l, h), sd[:, j * SEQ:(j + 1) * SEQ],
                                                        MUL, MUL))
                        C.settle()
                        for j in range(2):
                            h = 2 * i + j
                            V.tensor_tensor(o[:, h, :], o[:, h, :], gate[:, h, :], MUL).then_inc(y_rows, 1)
                        for j in range(2):
                            h = 2 * i + j
                            E.need(y_hi_done)
                            last = V.tensor_tensor(y1_lo[:, 4 + 4 * b + h, :], o[:, h, :], y1_hi[:, 4 + 4 * b + h, :], SUB)
                    last.then_inc(y_ready, 1)
                for b in range(3):
                    for f in range(KD):
                        E.need(tile_out, 2)
                        g, y, p = gate_sb[:, f % 2, 0:SEQ], branch_sb[:, f % 2, 0:SEQ], prod_sb[:, f % 2, 0:SEQ]
                        if b == 0:
                            V.tensor_tensor(mix[:, f, 0:SEQ], g, y, MUL).then_inc(merge_used, 1)
                            continue
                        V.tensor_tensor(p, g, y, MUL).then_inc(merge_used, 1)
                        dve.wait_ge(merge_used, 3 * KD * l + KD * b + f + 1)
                        last = V.tensor_tensor(mix[:, f, 0:SEQ], mix[:, f, 0:SEQ], p, ADD)
                        if b == 2:
                            last.then_inc(merged_rows, 1)
                        else:
                            C.do(last)
                            C.settle()
                for f in range(KD):
                    E.need(merged_hi)
                    last = V.tensor_tensor(y1_lo[:, f, :], mix[:, f, 0:SEQ], y1_hi[:, f, :], SUB)
                last.then_inc(merged_ready, 1)
                E.need(tile_out, KD)
                add_normed("norm_mix_post", l)
                norm1("norm_ffn_pre", l)
                for t in range(NFF):
                    E.need(tile_out, 2)
                    if t >= 2:
                        dve.wait_ge(ff_ready, NFF * l + t - 1)
                    V.tensor_tensor(ff_p[:, t % 2, :], ff_g[:, t % 2, :], ff_u[:, t % 2, :], MUL).then_inc(ff_rows, 1)
                    if t:
                        dve.wait_ge(ff_hi, NFF * l + t)
                        V.tensor_tensor(hid_lo[:, t - 1, :], ff_p[:, (t - 1) % 2, :], hid_hi[:, t - 1, :], SUB)\
                            .then_inc(ff_ready, 1)
                dve.wait_ge(ff_hi, NFF * (l + 1))
                V.tensor_tensor(hid_lo[:, NFF - 1, :], ff_p[:, (NFF - 1) % 2, :], hid_hi[:, NFF - 1, :], SUB)\
                    .then_inc(ff_ready, 1)
                E.need(tile_out, KD)
                add_normed("norm_ffn_post", l)

            def norm2(n, l, c0):
                inverse_root(c0, T2)
                streams = [(i, slice(i * SEQ, (i + 1) * SEQ)) for i in range(c0 // SEQ, 2)]
                for k in range(KD):
                    for i, part in streams:
                        C.do(V.scalar_tensor_tensor(work[:, k, part], xs[:, k, part], gain[:, n, k, i:i + 1],
                                                    sd[:, part], MUL, MUL))
                C.settle()
                for k in range(KD):
                    for i, part in streams:
                        last = V.tensor_scalar(work[:, k, part], work[:, k, part],
                                               mod[:, l, 3 * n * KD + k, i:i + 1], None, ADD)
                    last.then_inc(norm_rows, 1)
                split_low_norm(c0, T2)

            def add_gated(part_of_mod, l, c0, signal):
                for f in range(KD):
                    E.need(tile_out)
                    for i in range(c0 // SEQ, 2):
                        part = slice(i * SEQ, (i + 1) * SEQ)
                        last = V.scalar_tensor_tensor(xs[:, f, part], mix[:, f, part],
                                                      mod[:, l, part_of_mod * KD + f, i:i + 1], xs[:, f, part], MUL, ADD)
                        if f < KD - 1 or i == 0 or not signal:
                            C.do(last)
                if signal:
                    last.then_inc(x_ready, 1)
                else:
                    C.settle()

            for l in range(DEPTH):
                c0 = 0 if l < DEPTH - 1 else SEQ
                cols = slice(c0, T2)
                first, ns = c0 // SEQ, 2 - c0 // SEQ
                for n in range(2):
                    C.do(V.scalar_tensor_tensor(gain[:, n, :, :], mod[:, l, (3 * n + 1) * KD:(3 * n + 2) * KD, :], 1.0,
                                                v_(("norm1_w_2", "norm2_w_2")[n], l, 0, KD).unsqueeze(2)
                                                .to_broadcast([P, KD, 2]), ADD, MUL))
                norm2(0, l, 0)
                C.do(V.memset(z2[:, :, :, :], 0.0))
                C.settle()

                def by_stream(rows):
                    return rows.rearrange("p (s n) -> p s n", n=SEQ)

                for i in range(0, 4, 2):
                    for j in range(2):
                        E.need(tile_out, 2)
                        V.tensor_tensor(z2[:, j, first:2, PAD:PAD + SEQ], by_stream(cin[:, j, 0, cols]),
                                        by_stream(cin[:, j, 1, cols]), MUL).then_inc(cin_used, 1)
                    dve.wait_ge(cin_used, 4 * l + i + 2)
                    for tap in range(CONV_K):
                        for j in range(2):
                            y = by_stream(cy[:, i + j, cols])
                            z = z2[:, j, first:2, tap:tap + SEQ]
                            w = v_("conv_dw_w_2", l, 4 * tap + i + j)
                            if tap == 0:
                                C.do(V.tensor_scalar(y, z, w, v_("conv_dw_b_2", l, i + j), MUL, ADD))
                            else:
                                C.do(V.scalar_tensor_tensor(y, z, w, y, MUL, ADD))
                        C.settle()
                dve.sem_inc(cy_ready, 1)
                E.need(tile_out, AG + 3)
                for j in range(AG + 2):
                    if j <= AG:
                        a = c0 if j < AG else 0
                        inverse_root(a, T2)
                        V.scalar_tensor_tensor(aq[:, j, a:T2], aq[:, j, a:T2],
                                               v_("q_norm_w_2" if j < AG else "k_norm_w_2", l), sd[:, a:T2], MUL, MUL)\
                            .then_inc(aq_scaled, 1)
                    if j:
                        x = aq[:, j - 1, SEQ:T2]
                        E.need(aq_rot)
                        C.do(V.tensor_tensor(a_rot[:, :], X[j % 2][:, 0:SEQ], c_("sin_ax"), MUL))
                        C.do(V.tensor_tensor(x, x, c_("cos_ax"), MUL))
                        C.settle()
                        V.tensor_tensor(x, x, a_rot[:, :], ADD).then_inc(aq_ready, 1)
                        dve.wait_ge(aq_ready, (AG + 1) * l + j)
                steps, before = att_steps(l), att_before(l)
                for i in range(len(steps) + 2):
                    if i < len(steps):
                        keys, b = steps[i][3], i % 2
                        E.need(a_score)
                        C.do(V.reduce_max(a_stat[:, b, 0:1], X[b][:, 0:keys], AX_X))
                        C.settle()
                        V.tensor_scalar(a_stat[:, b, 1:2], a_stat[:, b, 0:1], -AD ** -0.5, None, MUL).then_inc(a_neg, 1)
                    if 1 <= i <= len(steps):
                        keys, b = steps[i - 1][3], (i - 1) % 2
                        E.need(a_exp)
                        C.do(V.reciprocal(a_stat[:, b, 3:4], a_stat[:, b, 2:3]))
                        C.settle()
                        V.tensor_scalar(p_sb[:, b, 0:keys], p_sb[:, b, 0:keys], a_stat[:, b, 3:4], None, MUL)\
                            .then_inc(a_prob, 1)
                    if i >= 2 and steps[i - 2][2] == 1:
                        q, j, _, _ = steps[i - 2]
                        E.need(a_o_hi)
                        V.tensor_tensor(y2_lo[:, 4 + j, q * P:(q + 1) * P], X[4][:, 0:P],
                                        y2_hi[:, 4 + j, q * P:(q + 1) * P], SUB).then_inc(a_o_out, 1)
                E.need(mean_done)
                for i in range(4):
                    last = V.scalar_tensor_tensor(cy[:, i, cols], X[0][:, cols], -1.0 / CONV, cy[:, i, cols], MUL, ADD)
                last.then_inc(centred, 1)
                inverse_root(c0, T2)
                for i in range(4):
                    V.tensor_tensor(cy[:, i, cols], cy[:, i, cols], sd[:, cols], MUL).then_inc(ln_rows, 1)
                for i in range(4):
                    E.need(y_hi_done)
                    last = V.tensor_tensor(y2_lo[:, i, cols], cy[:, i, cols], y2_hi[:, i, cols], SUB)
                last.then_inc(y_ready, 1)
                dve.sem_inc(y_ready, 1)
                E.need(mg_turned)
                V.tensor_tensor(pre[:, :, :], X[0][:, 0:64].rearrange("p (t g) -> p t g", g=16),
                                v_("mlstm_gate_b_2", l, 0, 16).unsqueeze(1).to_broadcast([P, 4, 16]), ADD)\
                    .then_inc(pre_ready, 1)
                E.need(lsg_ln)
                V.scalar_tensor_tensor(lsg[:, :, :], pre[:, :, :], 0.0, lsg[:, :, :], ALU.min, SUB).then_inc(lsg_ready, 1)
                E.need(fsum_done)
                sums = X[1][:, 0:4 * 2 * MH].rearrange("p (t d h) -> p t d h", t=4, d=2)
                C.do(V.tensor_copy(fsum[:, :, :, :], sums))
                dve.wait_ge(pre_ready, l + 1)
                for d in range(2):
                    last = V.tensor_tensor(gcol[:, :, d, :], pre[:, :, 8 * d:8 * d + MH],
                                           sums[:, :, d, :], SUB)
                last.then_inc(gcol_ready, 1)
                E.need(rows_turned)
                for d in range(2):
                    C.do(V.tensor_copy(g_row[:, d, :], X[2 + d][0:MH, :]))
                C.settle()
                C.do(V.tensor_tensor_scan(mx_row[:, 0, :], g_row[:, 0, :], g_row[:, 0, :], M_INIT, ALU.max, ALU.max))
                back = slice(SEQ - 1, None, -1)
                C.do(V.tensor_tensor_scan(mx_row[:, 1, back], g_row[:, 1, back], g_row[:, 1, back], M_INIT,
                                          ALU.max, ALU.max))
                C.settle()
                back = slice(T2 - 1, SEQ - 1, -1)
                C.do(V.tensor_tensor_scan(mx_row[:, 1, back], g_row[:, 1, back], g_row[:, 1, back], mx_row[:, 1, 0:1],
                                          ALU.max, ALU.max))
                C.settle()
                for d in range(2):
                    last = V.tensor_tensor(g_row[:, d, :], mx_row[:, d, :], X[4 * d][0:MH, :], ADD)
                    if d == 0:
                        C.do(last)
                last.then_inc(rows_ready, 1)

                def merge(b):
                    for f in range(KD):
                        E.need(tile_out, 2)
                        g, y, p = gate_sb[:, f % 2, cols], branch_sb[:, f % 2, cols], prod_sb[:, f % 2, cols]
                        n = KD * (3 * l + b) + f + 1
                        if b == 0:
                            V.tensor_tensor(mix[:, f, cols], g, y, MUL).then_inc(merge2_used, 1)
                            continue
                        V.tensor_tensor(p, g, y, MUL).then_inc(merge2_used, 1)
                        dve.wait_ge(merge2_used, n)
                        last = V.tensor_tensor(mix[:, f, cols], mix[:, f, cols], p, ADD)
                        if b == 2:
                            last.then_inc(merged_rows, 1)
                        else:
                            C.do(last)
                            C.settle()

                merge(0)
                merge(1)
                E.need(tile_out, 4)
                dve.wait_ge(rows_ready, l + 1)
                for h in range(MH):
                    n_head = l * MH + h
                    for d in range(2):
                        E.need(mx_done)
                        for n in range(5):
                            if n < 4:
                                t = ORDER[d][n]
                                a, b = hull(spans(d, t, c0)[0])
                                m = 8 * n_head + 4 * d + n
                                if m >= 3:
                                    dve.wait_ge(m_acc, m - 2)
                                V.tensor_scalar(wgt[:, (4 * d + n) % 3, a:b], X[2][:, a:b],
                                                gcol[:, t, d, h:h + 1], 0.0, SUB, ALU.max).then_inc(w_arg, 1)
                            if n >= 1:
                                t = ORDER[d][n - 1]
                                ranges, own = spans(d, t, c0)
                                a, b = hull(ranges)
                                w = wgt[:, (4 * d + n - 1) % 3, :]
                                if n == 1 and d == 0:
                                    dve.wait_ge(m_score_out, 4 * n_head + 4)
                                E.need(w_exp)
                                last = V.tensor_tensor(w[:, a:b], w[:, a:b], s_sb[:, t, a:b], MUL)
                                if own is not None:
                                    C.do(last)
                                    C.settle()
                                    last = V.tensor_tensor(w[:, own:own + P], w[:, own:own + P],
                                                           c_("upto" if d == 0 else "from"), MUL)
                                last.then_inc(w_ready, 1)
                        E.need(den_abs)
                        dve.wait_ge(em_out, 2 * n_head + d + 1)
                        C.do(V.tensor_tensor(nt[:, cols], nt[:, cols], em[:, cols], ALU.max))
                        C.settle()
                        C.do(V.reciprocal(nt[:, cols], nt[:, cols]))
                        C.settle()
                        for i in range(2):
                            if d == 0:
                                last = V.tensor_tensor(hacc[:, i, cols], X[i][:, cols], nt[:, cols], MUL)
                                if i == 0:
                                    C.do(last)
                                continue
                            if i:
                                C.settle()
                            last = V.tensor_tensor(em[:, cols], X[i][:, cols], nt[:, cols], MUL)
                            if i == 0:
                                C.do(last)
                                C.settle()
                                C.do(V.tensor_tensor(hacc[:, 0, cols], hacc[:, 0, cols], em[:, cols], ADD))
                        last.then_inc(m_taken, 1)
                        if d:
                            dve.wait_ge(m_taken, 2 * n_head + 2)
                            V.tensor_tensor(hacc[:, 1, cols], hacc[:, 1, cols], em[:, cols], ADD).then_inc(head_done, 1)
                        elif h or l:
                            pass
                    E.need(tile_out, 4 + 2 + (4 if h + 1 < MH else 0))
                    inverse_root(c0, T2)
                    for i in range(2):
                        C.do(V.scalar_tensor_tensor(hacc[:, i, cols], hacc[:, i, cols], v_("mlstm_norm_w_2", l, 2 * h + i),
                                                    sd[:, cols], MUL, MUL))
                    C.settle()
                    for i in range(2):
                        V.tensor_tensor(hacc[:, i, cols], hacc[:, i, cols], smo[:, i, cols], MUL).then_inc(y_rows, 1)
                    for i in range(2):
                        E.need(y_hi_done)
                        last = V.tensor_tensor(y2_lo[:, 2 * h + i, cols], hacc[:, i, cols], y2_hi[:, 2 * h + i, cols], SUB)
                        if i == 0 or h < MH - 1:
                            C.do(last)
                    if h < MH - 1:
                        C.settle()
                last.then_inc(y_ready, 1)
                merge(2)
                for f in range(KD):
                    E.need(merged_hi)
                    last = V.tensor_tensor(h_lo[:, f, cols], mix[:, f, cols], h_hi[:, f, cols], SUB)
                last.then_inc(merged_ready, 1)
                add_gated(2, l, c0, True)
                norm2(1, l, c0)
                dve.wait_ge(h_ready, DEPTH * 2 + 2 * l + 2)
                V.memset(up[:, :, :, :, :], 0.0).then_inc(up_zero, 1)
                for half in range(2):
                    n0 = NFF * l + FF_HALF * half
                    for t in range(FF_HALF + 2):
                        if t < FF_HALF:
                            E.need(tile_out, 2)
                            b = t % 2
                            if t >= 2:
                                dve.wait_ge(ff2_rows, n0 + t - 1)
                            for tap in range(3):
                                for j in range(2):
                                    y = by_stream(fc[:, b, j, cols])
                                    z = up[:, b, j, first:2, tap:tap + SEQ]
                                    at = j * NFF + half * FF_HALF + t
                                    w = v_("ffn_conv_w_2", l, 2 * NFF * tap + at)
                                    if tap == 0:
                                        C.do(V.tensor_scalar(y, z, w, v_("ffn_conv_b_2", l, at), MUL, ADD))
                                        continue
                                    last = V.scalar_tensor_tensor(y, z, w, y, MUL, ADD)
                                    if tap == 1 or j == 0:
                                        C.do(last)
                                if tap < 2:
                                    C.settle()
                            last.then_inc(fc_rows, 1)
                        if 1 <= t <= FF_HALF:
                            b = (t - 1) % 2
                            E.need(fc_gate)
                            C.settle()
                            if t >= 3:
                                dve.wait_ge(ff2_ready, n0 + t - 2)
                            V.tensor_tensor(fh[:, b, cols], fc[:, b, 0, cols], fc[:, b, 1, cols], MUL).then_inc(ff2_rows, 1)
                        if t >= 2:
                            E.need(ff2_hi)
                            V.tensor_tensor(hid2_lo[:, t - 2, cols], fh[:, t % 2, cols], hid2_hi[:, t - 2, cols], SUB)\
                                .then_inc(ff2_ready, 1)
                    add_gated(5, l, c0, half == 1)


def kernel(**inputs):
    import concourse.bacc as bacc
    from concourse.bass_utils import run_bass_kernel_spmd

    inputs = {k: np.asarray(v) for k, v in inputs.items()}
    cst, decay, masks = constants()

    def rows(a):
        return np.ascontiguousarray(a.T.reshape(KD, P, SEQ).transpose(1, 0, 2))

    arrays = {
        "stream": pack_weights(inputs),
        "vectors": pack_vectors(inputs),
        "consts": cst,
        "decay": decay,
        "gla_masks": masks,
        "positions": np.ascontiguousarray(np.broadcast_to(inputs["positions"].astype(np.int32), (P, SEQ))),
        "x_rows": rows(inputs["x"][0]),
        "ctx_rows": rows(inputs["ctx_2"][0]),
    }
    nc = bacc.Bacc("TRN2", target_bir_lowering=False, num_devices=1)
    args = [nc.dram_tensor(n, a.shape, mybir.dt.from_np(a.dtype), kind="ExternalInput").ap()
            for n, a in arrays.items()]
    out = nc.dram_tensor("out_rows", (P, KD, SEQ), F32, kind="ExternalOutput").ap()
    mixer_stack_kernel(nc, *args, out)
    got = run_bass_kernel_spmd(nc, [arrays], core_ids=[0]).results[0]["out_rows"]
    return np.ascontiguousarray(got.transpose(1, 0, 2).reshape(D, SEQ).T)[None]
```

```python
import numpy as np

import concourse.bass as bass
from concourse import mybir
from concourse.alu_op_type import AluOpType as ALU

F32 = mybir.dt.float32
F32R = mybir.dt.float32r
I32 = mybir.dt.int32
ACT = mybir.ActivationFunctionType
AX_X = mybir.AxisListType.X

P = 128
D = 1024
KD = D // P
SEQ = 256
T2 = 2 * SEQ
CTX, LAT = (0, SEQ), (SEQ, T2)
DEPTH = 2
EPS = 1e-6

CONV = 512
RH, RD = 4, 128
GH, GK, GV = 4, 64, 128
GTAU = 16.0
RANK = 16
FF = 2816
NFF = FF // P
FF_HALF = NFF // 2
CONV_K = 31
PAD = CONV_K // 2
MH, MD = 4, 256
AH, AKV, AD = 8, 2, 64
AG = AH // AKV
GRID_W = 64
M_INIT = -1e30
GLA_LEVELS = [64, 32, 16, 8, 4, 2, 1]
N_LEV = len(GLA_LEVELS) + 2

UNIT = 8
RAW, SPLIT = 3, 4
ADA_COLS = 256
N_ADA = DEPTH * (6 * D // ADA_COLS)
ADA_UNITS = N_ADA * KD * (ADA_COLS // P) // UNIT


class Tile:

    def __init__(self, name, array, layer, rows, cols):
        self.name, self.array, self.layer, self.rows, self.cols = name, array, layer, rows, cols
        self.k = len(rows)
        self.wide = len(cols) // P


def span(start, n=P):
    return list(range(start, start + n))


def stream_tiles():
    full = list(range(KD))
    out = []

    def put(name, array, layer, cols, rows=None):
        out.append(Tile(name, array, layer, full if rows is None else rows, cols))

    cu, cb, cc, rq, rk, rv, rg, gq, gk, gv, gr, ga, gates = np.cumsum(
        [0, CONV, CONV, CONV, 512, 512, 512, 512, 256, 256, 512, 512, RANK]).tolist()
    for l in range(DEPTH):
        for i in range(2):
            put("gq", "w_in", l, span(gq + i * P))
            put("gk", "w_in", l, span(gk + i * P))
        put("ga", "w_in", l, span(ga, RANK) + [-1] * (P - RANK))
        for h in range(RH):
            put("rq", "w_in", l, span(rq + h * P))
            put("rk", "w_in", l, span(rk + h * P))
        for v in range(2):
            put("rv", "w_in", l, span(rv + 256 * v, 256))
        for v in range(2):
            put("gv", "w_in", l, span(gv + 256 * v, 256))
        for i in range(4):
            put("cu", "w_in", l, span(cu + i * P))
            put("cc", "w_in", l, span(cc + i * P))
            put("cb", "w_in", l, span(cb + i * P))
        for i in range(4):
            put("rg", "w_in", l, span(rg + i * P))
        for i in range(4):
            put("gr", "w_in", l, span(gr + i * P))
        for b, name in enumerate(("w_branch_a", "w_branch_b", "w_branch_c")):
            for f in range(KD):
                put("gate", "w_in", l, span(gates + b * D + f * P))
                put("branch", name, l, span(f * P), list(range(4)))
        for f in range(KD):
            put("out", "w_out", l, span(f * P))
        for t in range(NFF):
            put("ffg", "w_ffn_gate", l, span(t * P))
            put("ffu", "w_ffn_up", l, span(t * P))
        for f in range(KD):
            put("ffd", "w_ffn_down", l, span(f * P), list(range(NFF)))

    cu, mq, mk, mv, mo, mg, aq, ak, av, bg = np.cumsum([0, 2 * CONV, D, D, D, D, 16, 512, 128, 128]).tolist()
    pair = [span(j * AD, AD) + span((j + AG) * AD, AD) for j in range(AG)]
    for l in range(DEPTH):
        for i in range(4):
            put("ca", "w_in_2", l, span(cu + i * P))
            put("cg", "w_in_2", l, span(cu + CONV + i * P))
        for j in range(AG):
            put("aq", "w_in_2", l, [aq + c for c in pair[j]])
        put("ak", "w_in_2", l, span(ak))
        put("av", "w_in_2", l, span(av))
        put("mg", "w_in_2", l, span(mg, 16) + [-1] * (P - 16))
        for b, (name, rows) in enumerate((("w_conv_out_2", 4), ("w_attn_out_2", 4))):
            for f in range(KD):
                put("gate", "w_in_2", l, span(bg + (0, 2)[b] * D + f * P))
                put("branch", name, l, span(f * P), list(range(rows)))
        for h in range(MH):
            for i in range(2):
                put("mq", "w_in_2", l, span(mq + h * MD + i * P))
            for i in range(2):
                put("mk", "w_in_2", l, span(mk + h * MD + i * P))
            put("mv", "w_in_2", l, span(mv + h * MD, MD))
            for i in range(2):
                put("mo", "w_in_2", l, span(mo + h * MD + i * P))
        for f in range(KD):
            put("gate", "w_in_2", l, span(bg + D + f * P))
            put("branch", "w_mlstm_out_2", l, span(f * P))
        for f in range(KD):
            put("out", "w_out_2", l, span(f * P))
        for half in range(2):
            for t in range(half * FF_HALF, (half + 1) * FF_HALF):
                put("fa", "ffn_w_up_2", l, span(t * P))
                put("fg", "ffn_w_up_2", l, span(FF + t * P))
            for f in range(KD):
                put("fd", "ffn_w_down_2", l, span(f * P), span(half * FF_HALF, FF_HALF))
    return out


MIX1 = [("g", 0), ("diag", 0), ("r", 0), ("logit", 0), ("r", 1), ("rot", 0), ("gates", 0), ("diff", 0), ("r", 2),
        ("rot", 1), ("rows", 0), ("diff", 1), ("r", 3), ("rot", 2), ("take", 0), ("rows", 1), ("diff", 2),
        ("rv", 0), ("rot", 3), ("take", 1), ("rows", 2), ("diff", 3), ("score", 0), ("rv", 1), ("take", 2),
        ("rows", 3), ("diff", 4), ("score", 1), ("mix", 0), ("gv", 0), ("take", 3), ("rows", 4), ("diff", 5),
        ("score", 2), ("mix", 1), ("gv", 1), ("take", 4), ("rows", 5), ("diff", 6), ("score", 3), ("mix", 2),
        ("c", 0), ("conv", 0), ("take", 5), ("rows", 6), ("diff", 7), ("mix", 3), ("c", 1), ("conv", 1), ("take", 6),
        ("rows", 7), ("mean", 0), ("c", 2), ("conv", 2), ("take", 7), ("c", 3), ("conv", 3), ("gout", 0), ("rg", 0),
        ("norm", 0), ("gr", 0), ("split", 0), ("norm", 1),
        ("split", 1)]

TILES = stream_tiles()
N_BLOCKS = sum(t.k * t.wide for t in TILES)
N_UNITS = N_BLOCKS // UNIT
assert N_BLOCKS % UNIT == 0 and N_UNITS % RAW == 0


def pack_weights(inputs):
    stream = np.zeros((ADA_UNITS + N_UNITS, P, UNIT * P), np.float32)
    blocks = stream.reshape(-1, P, UNIT, P)
    n = 0

    def put(block):
        nonlocal n
        blocks[n // UNIT, :, n % UNIT, :block.shape[1]] = block
        n += 1

    for l in range(DEPTH):
        w = inputs["ada_w_2"][l]
        for c in range(0, 6 * D, P * 2):
            for k in range(KD):
                for j in range(2):
                    put(w[k * P:(k + 1) * P, c + j * P:c + (j + 1) * P])
    for t in TILES:
        w = inputs[t.array][t.layer]
        if t.array == "w_attn_out_2":
            order = [r for j in range(AG) for r in span(j * AD, AD) + span((j + AG) * AD, AD)]
            w = w[order]
        for k in t.rows:
            for j in range(t.wide):
                cols = [c for c in t.cols[j * P:(j + 1) * P] if c >= 0]
                put(w[k * P:(k + 1) * P, cols])
    assert n == N_BLOCKS + ADA_UNITS * UNIT
    return stream


def vector_layout():
    at, out = 0, {}

    def put(name, n):
        nonlocal at
        out[name] = (at, n)
        at += n

    for l in range(DEPTH):
        for name in ("norm_mix_pre", "norm_mix_post", "norm_ffn_pre", "norm_ffn_post"):
            put((name, l), KD)
        put(("conv_w", l), 3 * 4)
        put(("ret_gn_w", l), RH)
        put(("gla_gn_w", l), GH)
        put(("gla_b_a", l), 2)
        put(("gla_w_a2", l), GH * GK)
    for l in range(DEPTH):
        put(("norm1_w_2", l), KD)
        put(("norm2_w_2", l), KD)
        put(("branch_gate_b_2", l), 3 * KD)
        put(("conv_dw_w_2", l), CONV_K * 4)
        put(("conv_dw_b_2", l), 4)
        put(("conv_ln_w_2", l), 4)
        put(("conv_ln_b_2", l), 4)
        put(("mlstm_gate_b_2", l), 16)
        put(("mlstm_norm_w_2", l), KD)
        put(("q_norm_w_2", l), 1)
        put(("k_norm_w_2", l), 1)
        put(("ffn_conv_w_2", l), 3 * 2 * NFF)
        put(("ffn_conv_b_2", l), 2 * NFF)
        put(("ada_b_2", l), 6 * KD)
    put("c", 2 * KD)
    return out, at


VEC, N_VEC = vector_layout()


def pack_vectors(inputs):
    vec = np.zeros((P, N_VEC), np.float32)

    def columns(a):
        return np.ascontiguousarray(a.reshape(-1, P).T)

    for key, (at, n) in VEC.items():
        if key == "c":
            both = np.stack([inputs["c_ctx_2"], inputs["c_2"][0]])
            vec[:, at:at + n] = both.reshape(2, KD, P).transpose(2, 1, 0).reshape(P, n)
            continue
        name, l = key
        a = inputs[name][l]
        if name == "gla_w_a2":
            vec[:RANK, at:at + n] = a
        elif name == "mlstm_gate_b_2":
            vec[:, at:at + n] = np.broadcast_to(a, (P, n))
        elif name in ("q_norm_w_2", "k_norm_w_2"):
            vec[:, at] = np.concatenate([a, a])
        else:
            vec[:, at:at + n] = columns(a)
    return vec


CONST_PARTS = [("ident", P), ("rot_ret", P), ("rot_att", P), ("upto", P), ("from", P), ("ones", P),
               ("one64", P), ("cos_ax", SEQ), ("sin_ax", SEQ), ("head_row", MH * P), ("inv_freq", 1)]
CONST = {}
for _name, _n in CONST_PARTS:
    CONST[_name] = (sum(n for _, n in CONST_PARTS[:len(CONST)]), _n)
N_CONST = sum(n for _, n in CONST_PARTS)
N_DECAY = RH * 3 * P


def constants():
    c = np.zeros((P, N_CONST), np.float32)

    def at(name):
        return c[:, CONST[name][0]:CONST[name][0] + CONST[name][1]]

    p, n = np.arange(P)[:, None], np.arange(P)[None, :]
    at("ident")[:] = p == n

    def rotation(half):
        r = np.zeros((P, P), np.float32)
        for base in range(0, P, 2 * half):
            for i in range(half):
                r[base + half + i, base + i] = -1.0
                r[base + i, base + half + i] = 1.0
        return r

    at("rot_ret")[:] = rotation(RD // 2)
    at("rot_att")[:] = rotation(AD // 2)
    at("upto")[:] = p <= n
    at("from")[:] = p >= n
    at("ones")[:] = 1.0
    at("one64")[:] = p // AD == n // AD
    n_freq = AD // 4
    inv = (10000.0 ** (-np.arange(n_freq, dtype=np.float32) / n_freq)).astype(np.float32)
    tok = np.arange(SEQ)
    ang = np.concatenate([(tok // GRID_W).astype(np.float32)[:, None] * inv,
                          (tok % GRID_W).astype(np.float32)[:, None] * inv], axis=-1)
    at("cos_ax")[:] = np.tile(np.cos(ang).T, (4, 1))
    at("sin_ax")[:] = np.tile(np.sin(ang).T, (4, 1))
    for h in range(MH):
        at("head_row")[h, h * P:(h + 1) * P] = 1.0
    half = RD // 2
    at("inv_freq")[:, 0] = np.tile((10000.0 ** (-np.arange(half, dtype=np.float32) / half)).astype(np.float32), 2)
    decay = np.zeros((P, RH, 3, P), np.float32)
    for h in range(RH):
        log_g = np.log(1.0 - 2.0 ** (-5.0 - h))
        for b, off in enumerate((0, P, 0)):
            diff = n + off - p
            decay[:, h, b, :] = np.where(diff >= 0, np.exp(log_g * np.maximum(diff, 0)), 0.0)
    masks = np.zeros((P, len(GLA_LEVELS) + 1, P), np.int32)
    for i, m in enumerate(GLA_LEVELS):
        masks[:, i, :] = (p // (2 * m) == n // (2 * m)) & (p % (2 * m) < m) & (n % (2 * m) >= m)
    masks[:, -1, :] = p == n
    return c, decay.reshape(P, N_DECAY), masks.reshape(P, -1)


class Expect:

    def __init__(self, engine):
        self.engine, self.seen = engine, {}

    def need(self, sem, more=1):
        self.seen[sem.name] = self.seen.get(sem.name, 0) + more
        self.engine.wait_ge(sem, self.seen[sem.name])

    def later(self, sem, more):
        self.seen[sem.name] = self.seen.get(sem.name, 0) + more
        return self.seen[sem.name]


class Chain:

    def __init__(self, engine, sem):
        self.engine, self.sem, self.n = engine, sem, 0

    def do(self, instruction):
        instruction.then_inc(self.sem, 1)
        self.n += 1
        return self.n

    def settle(self, n=None):
        self.engine.wait_ge(self.sem, self.n if n is None else n)


class Place:

    def __init__(self):
        self.first_out, self.first_block, self.outs = [], [], []
        out = block = 0
        for t in TILES:
            self.first_out.append(out)
            self.first_block.append(block)
            n = 1
            if t.wide == 2:
                n = 2 if t.array == "w_in" else T2 // P
            self.outs.append(n)
            out += n
            block += t.k * t.wide
        self.free, ends = [None] * N_UNITS, 0
        for i, t in enumerate(TILES):
            b0, b1 = self.first_block[i], self.first_block[i] + t.k * t.wide
            for u in range(b0 // UNIT, (b1 - 1) // UNIT + 1):
                last = UNIT * (u + 1) - 1
                if b0 <= last < b1:
                    if t.wide == 2 or last == b1 - 1:
                        self.free[u] = ("tile", self.first_out[i] + self.outs[i])
                    else:
                        ends += 1
                        self.free[u] = ("unit", ends)


PLACE = Place()


def mixer_stack_kernel(nc, stream, vectors, consts, decay, gla_masks, positions, x_in, ctx_in, out):
    names = set()

    class Region:
        def __init__(self, start, size):
            self.at, self.end = start, start + size

        def put(self, name, shape, dtype=F32):
            size = 4 * int(np.prod(shape[1:]))
            size += -size % 32
            assert self.at + size <= self.end, (name, self.at + size - self.end)
            assert name not in names
            names.add(name)
            t = nc.alloc_sbuf_tensor_at(name, shape, dtype, offset=self.at)
            self.at += size
            return t

        def view(self):
            return Region(self.at, self.end - self.at)

        def part(self, size):
            self.at += size
            assert self.at <= self.end
            return Region(self.at - size, size)

    base = nc.sbuf_base + (-nc.sbuf_base % 64)
    sbuf = Region(base, nc.sbuf_usable_end - base)

    cst = sbuf.put("cst", [P, N_CONST])
    vec = sbuf.put("vec", [P, N_VEC])
    mod = sbuf.put("mod", [P, DEPTH, 6 * KD, 2])
    gain = sbuf.put("gain", [P, 2, KD, 2])
    silu_c = sbuf.put("silu_c", [P, KD, 2])
    eps = sbuf.put("eps", [P, 1])
    raw = sbuf.put("raw", [P, RAW, UNIT * P])
    w_hi = sbuf.put("w_hi", [P, SPLIT, UNIT * P], F32R)
    w_lo = sbuf.put("w_lo", [P, SPLIT, UNIT * P], F32R)
    xs = sbuf.put("xs", [P, KD, T2])
    at_h_hi = sbuf.at
    h_hi = sbuf.put("h_hi", [P, KD, T2], F32R)
    at_h_lo = sbuf.at
    h_lo = sbuf.put("h_lo", [P, KD, T2], F32R)
    sd = sbuf.put("sd", [P, T2])
    R0 = sbuf.part(4 * KD * T2)
    R1 = sbuf.part(4 * KD * T2)
    RY = sbuf.part(8 * NFF * SEQ)
    RE = sbuf.view()
    work = R0.view().put("work", [P, KD, T2])
    mix = R1.view().put("mix", [P, KD, T2])

    e = RE.view()
    dec = e.put("dec", [P, RH, 3 * P])
    gmask = e.put("gmask", [P, len(GLA_LEVELS) + 1, P], I32)
    cos1 = e.put("cos1", [P, SEQ])
    sin1 = e.put("sin1", [P, SEQ])
    ret_a = e.put("ret_a", [P, 3 * P])
    ga_t = e.put("ga_t", [RANK, SEQ])
    logit = e.put("logit", [P, 2, SEQ])
    gdec = e.put("gdec", [P, 2, SEQ])
    q_dec = e.put("q_dec", [P, 2, SEQ])
    k_dec = e.put("k_dec", [P, 2, SEQ])
    zrow = e.put("zrow", [P, SEQ + 2])
    r = R0.view()
    rq_raw = r.put("rq_raw", [P, RH, 2, SEQ])
    rqk = r.put("rqk", [P, RH, 2, SEQ])
    r = R0.view()
    gate1 = r.put("gate1", [P, 2, SEQ])
    branch1 = r.put("branch1", [P, 2, SEQ])
    prod1 = r.put("prod1", [P, 2, SEQ])
    r.part(2 * 1024)
    o_sq = r.put("o_sq", [P, 2, 2 * SEQ])
    r = R0.view()
    gate_sb = r.put("gate_sb", [P, 2, T2])
    branch_sb = r.put("branch_sb", [P, 2, T2])
    prod_sb = r.put("prod_sb", [P, 2, T2])
    r = R0.view()
    ff_g = r.put("ff_g", [P, 2, SEQ])
    ff_u = r.put("ff_u", [P, 2, SEQ])
    ff_p = r.put("ff_p", [P, 2, SEQ])
    r = R1.view()
    g_acc = r.put("g_acc", [P, GH, 3, P])
    g_cum = r.put("g_cum", [P, 2, SEQ])
    spare_hi = nc.alloc_sbuf_tensor_at("spare_hi", [P, KD, T2], F32, offset=at_h_hi)
    spare_lo = nc.alloc_sbuf_tensor_at("spare_lo", [P, KD, T2], F32, offset=at_h_lo)
    silu_r, silu_g = spare_hi[:, 0:RH, 0:SEQ], spare_hi[:, RH:RH + GH, 0:SEQ]
    conv_in = spare_lo[:, 0:6, 0:SEQ].rearrange("p (b j) n -> p b j n", b=2)
    conv_y = spare_lo[:, 6:8, 0:SEQ]
    r = RY.view()
    y1_hi = r.put("y1_hi", [P, 12, SEQ], F32R)
    y1_lo = r.put("y1_lo", [P, 12, SEQ], F32R)
    rv = r.put("rv", [P, 2, RH * RD])
    gv = r.put("gv", [P, 2, GH * GV])
    o_ret = r.put("o_ret", [P, RH, SEQ])
    o_gla = r.put("o_gla", [P, GH, SEQ])
    gqk = r.put("gqk", [P, 2, 2, SEQ])
    r = RY.view()
    hid_hi = r.put("hid_hi", [P, NFF, SEQ], F32R)
    hid_lo = r.put("hid_lo", [P, NFF, SEQ], F32R)
    r = R0.view()
    pos_i = r.put("pos_i", [P, SEQ], I32)
    ang = r.put("ang", [P, SEQ])
    turns = r.put("turns", [P, SEQ])
    turns_i = r.put("turns_i", [P, SEQ], I32)
    ang2 = r.put("ang2", [P, SEQ])
    mod_rows = RY.view().put("mod_rows", [2, 6 * D])

    e = RE.view()
    z2 = e.put("z2", [P, 2, 2, SEQ + 2 * PAD])
    a_sq = e.put("a_sq", [P, T2])
    p_sb = e.put("p_sb", [P, 2, T2])
    pt_sb = e.put("pt_sb", [P, 2, T2])
    a_stat = e.put("a_stat", [P, 2, 4])
    a_rot = e.put("a_rot", [P, SEQ])
    e = RE.view()
    g_row = e.put("g_row", [MH, 2, T2])
    mx_row = e.put("mx_row", [MH, 2, T2])
    wgt = e.put("wgt", [P, 3, T2])
    em = e.put("em", [P, T2])
    nt = e.put("nt", [P, T2])
    pre = e.put("pre", [P, 4, 16])
    lsg = e.put("lsg", [P, 4, 16])
    fsum = e.put("fsum", [P, 4, 2, MH])
    gcol = e.put("gcol", [P, 4, 2, MH])
    r = R1.view()
    cin = r.put("cin", [P, 2, 2, T2])
    cy = r.put("cy", [P, 4, T2])
    r = R0.view()
    aq = r.put("aq", [P, AG + 1, T2])
    av_t = r.put("av_t", [P, T2])
    av = r.put("av", [P, 4, P])
    mg_t = r.put("mg_t", [16, T2])
    r = R0.view()
    s_sb = r.put("s_sb", [P, 4, T2])
    hacc = r.put("hacc", [P, 2, T2])
    smo = r.put("smo", [P, 2, T2])
    r = R0.view()
    up = r.put("up", [P, 2, 2, 2, SEQ + 2])
    e = RE.view()
    fc = e.put("fc", [P, 2, 2, T2])
    fh = e.put("fh", [P, 2, T2])
    r = RY.view()
    y2_hi = r.put("y2_hi", [P, KD, T2], F32R)
    y2_lo = r.put("y2_lo", [P, KD, T2], F32R)
    mqk = r.put("mqk", [P, 4, T2])
    mv = r.put("mv", [P, 4, MD])
    r = RY.view()
    hid2_hi = r.put("hid2_hi", [P, FF_HALF, T2], F32R)
    hid2_lo = r.put("hid2_lo", [P, FF_HALF, T2], F32R)

    def c_(name):
        return cst[:, CONST[name][0]:CONST[name][0] + CONST[name][1]]

    def v_(name, l, i=0, n=1):
        return vec[:, VEC[name, l][0] + i:VEC[name, l][0] + i + n]

    ident, ones = c_("ident"), c_("ones")

    banks = [nc.alloc_psum_tensor(f"bank{i}", [P, T2], F32) for i in range(8)]
    LIN, STAT, X = banks[0:2], banks[2], banks[3:8]


    def sem(name):
        return nc.alloc_semaphore(name)

    raw_loaded = [sem(f"raw_loaded{i}") for i in range(RAW)]
    ada_used = sem("ada_used")
    ada_out = sem("ada_out")
    mod_turned = sem("mod_turned")
    mod_ready = sem("mod_ready")
    hi_ready = sem("hi_ready")
    lo_ready = sem("lo_ready")
    unit_used = sem("unit_used")
    tile_done = sem("tile_done")
    tile_out = sem("tile_out")
    params_in, x_in_sem, stored = sem("params_in"), sem("x_loaded"), sem("stored")
    trig_args, trig_done = sem("trig_args"), sem("trig_done")
    silu_c_ready = sem("silu_c_ready")
    x_ready, sq_ready, stat_ready, std_ready = sem("x_ready"), sem("sq_ready"), sem("stat_ready"), sem("std_ready")
    norm_rows, hi_done, h_ready = sem("norm_rows"), sem("hi_done"), sem("h_ready")
    rot_done, qk_ready = sem("rot_done"), sem("qk_ready")
    score_done, ret_a_ready, ret_o_done, ret_o_out = (sem("ret_score_done"), sem("ret_a_ready"),
                                                      sem("ret_o_done"), sem("ret_o_out"))
    logit_done, logit_out, logit_ln = sem("logit_done"), sem("logit_out"), sem("logit_ln")
    lev_diff, lev_exp, lev_rows, lev_done, lev_taken = (sem("lev_diff"), sem("lev_exp"), sem("lev_rows"),
                                                        sem("lev_done"), sem("lev_taken"))
    gla_o_done, gla_o_out = sem("gla_o_done"), sem("gla_o_out")
    conv_used, conv_ready = sem("conv_used"), sem("conv_ready")
    mean_done, centred = sem("mean_done"), sem("centred")
    y_rows, y_hi_done, y_ready = sem("y_rows"), sem("y_hi_done"), sem("y_ready")
    merge_used, merged_rows, merged_hi, merged_ready = (sem("merge_used"), sem("merged_rows"), sem("merged_hi"),
                                                        sem("merged_ready"))
    ff_used, ff_rows, ff_hi, ff_ready = sem("ff_used"), sem("ff_rows"), sem("ff_hi"), sem("ff_ready")
    down_used = sem("down_used")
    av_turned, av_out = sem("av_turned"), sem("av_out")
    aq_scaled, aq_rot = sem("aq_scaled"), sem("aq_rot")
    a_score, a_neg, a_exp, a_prob, a_turned, a_pt, a_o_done, a_o_out = [
        sem(n) for n in ("a_score", "a_neg", "a_exp", "a_prob", "a_turned", "a_pt", "a_o_done", "a_o_out")]
    mg_turned, lsg_abs, lsg_ln, lsg_ready, fsum_done, gcol_ready, rows_turned, rows_ready = [
        sem(n) for n in ("mg_turned", "lsg_abs", "lsg_ln", "lsg_ready", "fsum_done", "gcol_ready",
                         "rows_turned", "rows_ready")]
    m_score, m_score_out, mx_done, w_arg, w_exp, w_ready, m_acc, em_in, em_out, m_taken, head_done = [
        sem(n) for n in ("m_score", "m_score_out", "mx_done", "w_arg", "w_exp", "w_ready", "m_acc", "em_in",
                         "em_out", "m_taken", "m_head_done")]
    cin_used, cy_ready, ln_rows, aq_ready, a_o_hi, pre_ready, merge2_used, den_abs = [
        sem(n) for n in ("cin_used", "cy_ready", "ln_rows", "aq_ready", "a_o_hi", "pre_ready", "merge2_used", "den_abs")]
    up_zero, fc_rows, fc_gate, ff2_rows, ff2_hi, ff2_ready = [
        sem(n) for n in ("up_zero", "fc_rows", "fc_gate", "ff2_rows", "ff2_hi", "ff2_ready")]
    dve_chain, act_chain = sem("dve_chain"), sem("act_chain")

    def spans(direction, tile, c0):
        own = tile * P
        if direction == 0:
            lo = max(own, c0)
            return [(lo, T2)], own if own >= c0 else None
        if tile < 2:
            if c0:
                return [(SEQ, T2)], None
            return ([(0, T2)] if tile == 1 else [(0, P), (SEQ, T2)]), own
        return [(SEQ, own + P)], own

    ORDER = {0: [0, 1, 2, 3], 1: [1, 0, 3, 2]}

    def hull(ranges):
        return ranges[0][0], ranges[-1][1]

    def att_steps(l):
        return [(q, j, g, T2 if q >= 2 else SEQ) for q in range(0 if l < DEPTH - 1 else 2, 4)
                for j in range(AG) for g in range(AKV)]

    def att_before(l):
        return sum(len(att_steps(i)) for i in range(l))

    with nc.Block() as block:

        @block.sync
        def _(sp):
            sp.dma_start(vec[:, :], vectors).then_inc(params_in, 16)
            sp.dma_start(cst[:, :], consts).then_inc(params_in, 16)

            def load(slot, unit):
                sp.dma_start(raw[:, slot, :], stream[unit]).then_inc(raw_loaded[slot], 16)

            for slot in range(RAW):
                load(slot, slot)
            sp.dma_start(dec[:, :, :], decay.rearrange("p (h n) -> p h n", h=RH)).then_inc(params_in, 16)
            sp.dma_start(gmask[:, :, :], gla_masks.rearrange("p (h n) -> p h n", n=P)).then_inc(params_in, 16)
            sp.dma_start(pos_i[:, :], positions).then_inc(params_in, 16)
            sp.dma_start(xs[:, :, SEQ:T2], x_in).then_inc(x_in_sem, 16)
            sp.dma_start(xs[:, :, 0:SEQ], ctx_in).then_inc(x_in_sem, 16)
            with sp.Fori(1, ADA_UNITS // RAW) as i:
                for slot in range(RAW):
                    sp.wait_ge(ada_used, i * RAW + (slot - RAW + 1))
                    load(slot, i * RAW + slot)
            for slot in range(RAW):
                sp.wait_ge(ada_used, ADA_UNITS - RAW + slot + 1)
                load(slot, ADA_UNITS + slot)
            with sp.Fori(1, N_UNITS // RAW) as i:
                for slot in range(RAW):
                    sp.wait_ge(lo_ready, i * RAW + (slot - RAW + 1))
                    load(slot, i * RAW + (ADA_UNITS + slot))
            for unit in range(N_UNITS // RAW * RAW, N_UNITS):
                sp.wait_ge(lo_ready, unit - RAW + 1)
                load(unit % RAW, ADA_UNITS + unit)
            sp.wait_ge(x_ready, 4 * DEPTH * KD)
            sp.dma_start(out, xs[:, :, SEQ:T2]).then_inc(stored, 16)
            sp.wait_ge(stored, 16)

        @block.gpsimd
        def _(pool):
            step = RAW * SPLIT

            def low_part(unit, ordinal):
                pool.wait_ge(hi_ready, ordinal)
                nc.gpsimd.tensor_tensor(w_lo[:, unit % SPLIT, :], raw[:, unit % RAW, :], w_hi[:, unit % SPLIT, :],
                                        ALU.subtract).then_inc(lo_ready, 1)

            with pool.Fori(0, N_UNITS // step) as i:
                for j in range(step):
                    low_part(j, i * step + (j + 1))
            for unit in range(N_UNITS // step * step, N_UNITS):
                low_part(unit, unit + 1)

        @block.tensor
        def _(pe):
            E = Expect(pe)
            at = {"tile": 0, "unit": -1, "stat": 0, "rows": 0}

            def wait_unit(u):
                if u > at["unit"]:
                    pe.wait_ge(lo_ready, u + 1)
                    at["unit"] = u

            def bank_of(n):
                if n >= len(LIN):
                    pe.wait_ge(tile_out, n - len(LIN) + 1)
                return LIN[n % len(LIN)]

            def product(x_hi, x_lo, c0, c1, count=1, fresh=False):
                for i_tile in range(count):
                    t, n, b = TILES[at["tile"]], PLACE.first_out[at["tile"]], PLACE.first_block[at["tile"]]
                    acc = bank_of(n)[:, c0:c1]
                    for k in range(t.k):
                        wait_unit((b + k) // UNIT)
                        slot, i = (b + k) // UNIT % SPLIT, (b + k) % UNIT
                        wh, wl = w_hi[:, slot, i * P:(i + 1) * P], w_lo[:, slot, i * P:(i + 1) * P]
                        if fresh and i_tile == 0:
                            E.need(h_ready)
                        nc.tensor.matmul(acc, wh, x_hi[:, k, c0:c1], start=k == 0, stop=False)
                        nc.tensor.matmul(acc, wh, x_lo[:, k, c0:c1], start=False, stop=False)
                        last = nc.tensor.matmul(acc, wl, x_hi[:, k, c0:c1], start=False, stop=k == t.k - 1)
                        if k == t.k - 1:
                            last.then_inc(tile_done, 1)
                        elif i == UNIT - 1:
                            last.then_inc(unit_used, 1)
                    at["tile"] += 1

            def values(first, count=1):
                for _ in range(count):
                    t, n, b = TILES[at["tile"]], PLACE.first_out[at["tile"]], PLACE.first_block[at["tile"]]
                    for i in range(PLACE.outs[at["tile"]]):
                        acc = bank_of(n + i)[:, 0:2 * P]
                        c = first + i * P
                        for k in range(t.k):
                            u, j = (b + 2 * k) // UNIT, (b + 2 * k) % UNIT
                            wait_unit(u)
                            wh, wl = w_hi[:, u % SPLIT, j * P:(j + 2) * P], w_lo[:, u % SPLIT, j * P:(j + 2) * P]
                            nc.tensor.matmul(acc, h_hi[:, k, c:c + P], wh, start=k == 0, stop=False)
                            nc.tensor.matmul(acc, h_hi[:, k, c:c + P], wl, start=False, stop=False)
                            last = nc.tensor.matmul(acc, h_lo[:, k, c:c + P], wh, start=False, stop=k == t.k - 1)
                        last.then_inc(tile_done, 1)
                    at["tile"] += 1

            def row_sum(i, n, row, c0, c1, weights=ones):
                E.need(sq_ready)
                if i == 0:
                    if at["stat"]:
                        E.need(std_ready)
                    at["stat"] += 1
                last = nc.tensor.matmul(STAT[:, c0:c1], weights, row, start=i == 0, stop=i == n - 1)
                if i == n - 1:
                    last.then_inc(stat_ready, 1)

            def norm_sum(k, c0, c1):
                row_sum(k, KD, work[:, k, c0:c1], c0, c1)

            def norm_sums(c0, c1):
                for k in range(KD):
                    norm_sum(k, c0, c1)

            def projected(x_hi, x_lo, c0, c1, cols):
                for f in range(KD):
                    product(x_hi, x_lo, c0, c1)
                    if f >= 2:
                        norm_sum(f - 2, *cols)
                for f in range(KD - 2, KD):
                    norm_sum(f, *cols)

            E.need(silu_c_ready)
            for n in range(N_ADA):
                if n >= len(LIN):
                    pe.wait_ge(ada_out, n - len(LIN) + 1)
                for k in range(KD):
                    u = 2 * n + k // 4
                    if k % 4 == 0:
                        pe.wait_ge(raw_loaded[u % RAW], 16 * (u // RAW + 1))
                    last = nc.tensor.matmul(LIN[n % len(LIN)][0:2, 0:ADA_COLS], silu_c[:, k, :],
                                            raw[:, u % RAW, (k % 4) * ADA_COLS:(k % 4 + 1) * ADA_COLS],
                                            start=k == 0, stop=k == KD - 1)
                    if k % 4 == 3:
                        last.then_inc(ada_used, 1)
                if (n + 1) % (N_ADA // DEPTH) == 0:
                    l = n // (N_ADA // DEPTH)
                    pe.wait_ge(ada_out, n + 1)
                    for i in range(6 * KD):
                        last = nc.tensor.transpose(X[l][:, 2 * i:2 * i + 2], mod_rows[0:2, i * P:(i + 1) * P],
                                                   ident[0:2, 0:2])
                    last.then_inc(mod_turned, 1)

            c0, c1 = LAT
            for l in range(DEPTH):
                norm_sums(c0, c1)
                if l == 0:
                    E.need(mod_ready, 2)
                outs = {}
                for step, i in MIX1:
                    if step in ("g", "r", "c", "rg", "gr"):
                        n = {"g": 5, "r": 2, "c": 3, "rg": RH, "gr": GH}[step]
                        product(h_hi, h_lo, c0, c1, n, fresh=step == "g")
                    elif step in ("rv", "gv"):
                        values(c0)
                    elif step == "diag" or step == "take":
                        if step == "take":
                            E.need(lev_rows)
                            E.need(lev_taken)
                        else:
                            pe.wait_ge(tile_out, outs["g"])
                        for h in range(GH):
                            rows = slice(GK * (h % 2), GK * (h % 2) + GK)
                            q = gqk[rows, 0, h // 2, :] if step == "diag" else q_dec[rows, h // 2, :]
                            k = gqk[rows, 1, h // 2, :] if step == "diag" else k_dec[rows, h // 2, :]
                            bank = X[1 + h % 2]
                            if step == "take" and i == 0:
                                last = nc.tensor.matmul(bank[:, h // 2 * P:(h // 2 + 1) * P], k[:, 0:P], q[:, P:SEQ],
                                                        start=True, stop=True)
                                continue
                            for j in range(2):
                                c = (h // 2 * 2 + j) * P
                                last = nc.tensor.matmul(bank[:, c:c + P], k[:, j * P:(j + 1) * P],
                                                        q[:, j * P:(j + 1) * P], start=True, stop=True)
                        last.then_inc(lev_done, 1)
                    elif step == "logit":
                        for j in range(2):
                            last = nc.tensor.matmul(X[0][:, j * SEQ:(j + 1) * SEQ],
                                                    v_("gla_w_a2", l, j * P, P)[0:RANK, :], ga_t[:, :],
                                                    start=True, stop=True)
                        last.then_inc(logit_done, 1)
                    elif step == "rot":
                        pe.wait_ge(tile_out, outs["r", i])
                        if i == 0:
                            pe.wait_ge(logit_out, l + 1)
                        else:
                            E.need(qk_ready)
                        nc.tensor.matmul(X[0][:, :], c_("rot_ret"), rq_raw[:, i, :, :], start=True, stop=True)\
                            .then_inc(rot_done, 1)
                    elif step == "score":
                        q, k = rqk[:, i, 0, :], rqk[:, i, 1, :]
                        if i == 0:
                            E.need(qk_ready)
                        else:
                            pe.wait_ge(ret_a_ready, RH * l + i)
                        nc.tensor.matmul(X[3][:, 0:SEQ], k[:, 0:P], q, start=True, stop=True)
                        nc.tensor.matmul(X[3][:, SEQ:SEQ + P], k[:, P:SEQ], q[:, P:SEQ], start=True, stop=True)\
                            .then_inc(score_done, 1)
                    elif step == "mix":
                        pe.wait_ge(tile_out, outs["rv"])
                        pe.wait_ge(ret_a_ready, RH * l + i + 1)
                        if i:
                            pe.wait_ge(ret_o_out, RH * l + i)
                        o = X[4][:, 0:SEQ]
                        nc.tensor.matmul(o, rv[:, 0, i * P:(i + 1) * P], ret_a[:, 0:SEQ], start=True, stop=False)
                        nc.tensor.matmul(o[:, P:SEQ], rv[:, 1, i * P:(i + 1) * P], ret_a[:, SEQ:SEQ + P],
                                         start=False, stop=True).then_inc(ret_o_done, 1)
                    elif step == "mean":
                        pe.wait_ge(ret_o_out, RH * (l + 1))
                        for j in range(2):
                            nc.tensor.matmul(X[3 * j][:, :], ones, o_ret[:, 2 * j:2 * j + 2, :], start=True, stop=True)\
                                .then_inc(mean_done, 1)
                    elif step == "gout":
                        E.need(lev_taken)
                        pe.wait_ge(tile_out, outs["gv"])
                        for h in range(GH):
                            if h:
                                pe.wait_ge(gla_o_out, GH * l + h)
                            o = X[4][:, 0:SEQ]
                            nc.tensor.matmul(o, gv[:, 0, h * P:(h + 1) * P], g_acc[:, h, 0:2, :], start=True,
                                             stop=False)
                            nc.tensor.matmul(o[:, P:SEQ], gv[:, 1, h * P:(h + 1) * P], g_acc[:, h, 2, :],
                                             start=False, stop=True).then_inc(gla_o_done, 1)
                    elif step == "norm":
                        row_sum(0, 1, o_sq[:, i, :], 0, T2)
                    outs[step] = outs[step, i] = PLACE.first_out[at["tile"]]
                for b in range(3):
                    E.need(y_ready)
                    for f in range(KD):
                        product(h_hi, h_lo, c0, c1)
                        product(y1_hi[:, 4 * b:4 * b + 4, :], y1_lo[:, 4 * b:4 * b + 4, :], 0, SEQ)
                        if b == 0 and f in (1, 3):
                            row_sum(0, 1, o_sq[:, f // 2, :], 0, T2)
                E.need(merged_ready)
                projected(y1_hi, y1_lo, 0, SEQ, LAT)
                norm_sums(c0, c1)
                product(h_hi, h_lo, c0, c1, 2 * NFF, fresh=True)
                E.need(ff_ready, NFF)
                projected(hid_hi, hid_lo, 0, SEQ, LAT)

            for l in range(DEPTH):
                c0 = 0 if l < DEPTH - 1 else SEQ
                cols = slice(c0, T2)
                if l == 0:
                    norm_sums(0, T2)
                product(h_hi, h_lo, c0, T2, 8, fresh=True)
                product(h_hi, h_lo, c0, T2, AG)
                product(h_hi, h_lo, 0, T2, 3)
                for j in range(AG + 2):
                    if j <= AG:
                        row_sum(0, 1, a_sq[:, c0 if j < AG else 0:T2], c0 if j < AG else 0, T2, c_("one64"))
                    if j:
                        E.need(aq_scaled)
                        if j > 2:
                            E.need(aq_ready)
                        nc.tensor.matmul(X[j % 2][:, 0:SEQ], c_("rot_att"), aq[:, j - 1, SEQ:T2], start=True,
                                         stop=True).then_inc(aq_rot, 1)
                pe.wait_ge(tile_out, PLACE.first_out[at["tile"] - 1])
                for i in range(4):
                    last = nc.tensor.transpose(X[2][:, i * P:(i + 1) * P], av_t[:, i * P:(i + 1) * P], ident)
                last.then_inc(av_turned, 1)
                E.need(aq_ready, 2)
                steps = att_steps(l)
                before = att_before(l)
                for i in range(len(steps) + 2):
                    if i < len(steps):
                        q, j, g, keys = steps[i]
                        rows = slice(AD * g, AD * g + AD)
                        if i >= 2:
                            pe.wait_ge(a_exp, before + i - 1)
                        nc.tensor.matmul(X[i % 2][:, 0:keys], aq[rows, j, q * P:(q + 1) * P], aq[rows, AG, 0:keys],
                                         start=True, stop=True).then_inc(a_score, 1)
                    if 1 <= i <= len(steps):
                        keys = steps[i - 1][3]
                        E.need(a_prob)
                        if i == 1:
                            E.need(av_out)
                        for t in range(keys // P):
                            last = nc.tensor.transpose(X[2 + (i - 1) % 2][:, t * P:(t + 1) * P],
                                                       p_sb[:, (i - 1) % 2, t * P:(t + 1) * P], ident)
                        last.then_inc(a_turned, 1)
                    if i >= 2:
                        q, j, g, keys = steps[i - 2]
                        E.need(a_pt)
                        if g == 0 and i > 2:
                            pe.wait_ge(a_o_out, (before + i - 2) // 2)
                        for t in range(keys // P):
                            last = nc.tensor.matmul(X[4][AD * g:AD * g + AD, 0:P], av[:, t, AD * g:AD * g + AD],
                                                    pt_sb[:, i % 2, t * P:(t + 1) * P], start=t == 0,
                                                    stop=t == keys // P - 1)
                        last.then_inc(a_o_done, 1)
                E.need(cy_ready)
                pe.wait_ge(a_exp, att_before(l + 1))
                for i in range(4):
                    last = nc.tensor.matmul(X[0][:, cols], ones, cy[:, i, cols], start=i == 0, stop=i == 3)
                last.then_inc(mean_done, 1)
                for i in range(4):
                    row_sum(i, 4, cin[:, i // 2, i % 2, cols], c0, T2)
                for i in range(4):
                    last = nc.tensor.transpose(X[0][:, i * 16:(i + 1) * 16], mg_t[:, i * P:(i + 1) * P], ident[0:16, 0:16])
                last.then_inc(mg_turned, 1)
                E.need(lsg_ready)
                for i in range(4):
                    for d in range(2):
                        if d == 0:
                            parts = [(t, "ones") for t in range(i)] + [(i, "upto")]
                        elif i < 2:
                            parts = [(t, "ones") for t in range(i + 1, 2)] + [(i, "from")]
                        else:
                            parts = [(0, "ones"), (1, "ones")] + [(t, "ones") for t in range(i + 1, 4)] + [(i, "from")]
                        for n, (t, name) in enumerate(parts):
                            last = nc.tensor.matmul(X[1][:, (2 * i + d) * MH:(2 * i + d + 1) * MH], c_(name),
                                                    lsg[:, t, 8 * d + MH:8 * d + 2 * MH], start=n == 0,
                                                    stop=n == len(parts) - 1)
                last.then_inc(fsum_done, 1)
                E.need(gcol_ready)
                pe.wait_ge(a_o_out, att_before(l + 1) // 2)
                for d in range(2):
                    for i in range(4):
                        nc.tensor.transpose(X[2 + d][0:MH, i * P:(i + 1) * P], gcol[:, i, d, :], ident)
                        last = nc.tensor.transpose(X[4 * d][0:MH, i * P:(i + 1) * P], fsum[:, i, d, :], ident)
                last.then_inc(rows_turned, 1)
                for b in range(2):
                    E.need(y_ready)
                    for f in range(KD):
                        product(h_hi, h_lo, c0, T2)
                        product(y2_hi[:, 4 * b:4 * b + 4, :], y2_lo[:, 4 * b:4 * b + 4, :], c0, T2)
                E.need(rows_ready)

                def queries_keys():
                    product(h_hi, h_lo, c0, T2, 2)
                    product(h_hi, h_lo, 0, T2, 2)

                queries_keys()
                for h in range(MH):
                    n_head = l * MH + h
                    pe.wait_ge(tile_out, PLACE.first_out[at["tile"]])
                    for t in range(4):
                        if t >= 2:
                            pe.wait_ge(m_score_out, 4 * n_head + t - 1)
                        for i in range(2):
                            last = nc.tensor.matmul(X[t % 2][:, cols], mqk[:, 2 + i, t * P:(t + 1) * P],
                                                    mqk[:, i, cols], start=i == 0, stop=i == 1)
                        last.then_inc(m_score, 1)
                    head = c_("head_row")[0:MH, h * P:(h + 1) * P]
                    for d in range(2):
                        def running_max():
                            nc.tensor.matmul(X[2][:, cols], head, mx_row[:, d, cols], start=True, stop=True)\
                                .then_inc(mx_done, 1)
                            nc.tensor.matmul(X[4][:, cols], head, g_row[:, d, cols], start=True, stop=True)\
                                .then_inc(em_in, 1)

                        if d == 0:
                            running_max()
                            values(0)
                            product(h_hi, h_lo, c0, T2, 2)
                            pe.wait_ge(tile_out, PLACE.first_out[at["tile"] - 2])
                            pe.wait_ge(m_score_out, 4 * n_head + 4)
                        else:
                            pe.wait_ge(w_arg, 8 * n_head + 4)
                            pe.wait_ge(em_out, 2 * n_head + 1)
                            running_max()
                            pe.wait_ge(m_taken, 2 * n_head + 1)
                        for n, t in enumerate(ORDER[d]):
                            E.need(w_ready)
                            ranges = spans(d, t, c0)[0]
                            for i in range(3):
                                acc = X[3] if i == 0 else X[i - 1]
                                for a, b in ranges:
                                    w = wgt[:, (4 * d + n) % 3, a:b]
                                    left = ones if i == 0 else mv[:, t, (i - 1) * P:i * P]
                                    last = nc.tensor.matmul(acc[:, a:b], left, w, start=n == 0, stop=n == 3,
                                                            skip_group_check=True)
                            last.then_inc(m_acc, 1)
                    if h + 1 < MH:
                        queries_keys()
                    for i in range(2):
                        row_sum(i, 2, s_sb[:, i, cols], c0, T2)
                E.need(y_ready)
                for f in range(KD):
                    product(h_hi, h_lo, c0, T2)
                    product(y2_hi, y2_lo, c0, T2)
                E.need(merged_ready)
                projected(h_hi, h_lo, c0, T2, (c0, T2))
                for half in range(2):
                    product(h_hi, h_lo, c0, T2, 2 * FF_HALF, fresh=half == 0)
                    E.need(ff2_ready, FF_HALF)
                    if half == 0 or l == DEPTH - 1:
                        product(hid2_hi, hid2_lo, c0, T2, KD)
                    else:
                        projected(hid2_hi, hid2_lo, c0, T2, (0, T2))

        @block.scalar
        def _(act):
            E = Expect(act)
            C = Chain(act, act_chain)
            at = {"tile": 0, "unit": 0}

            def split_through(u):
                while at["unit"] <= min(u, N_UNITS - 1):
                    n = at["unit"]
                    act.wait_ge(raw_loaded[n % RAW], 16 * ((n + ADA_UNITS) // RAW + 1))
                    if n >= SPLIT:
                        kind, count = PLACE.free[n - SPLIT]
                        act.wait_ge(tile_done if kind == "tile" else unit_used, count)
                    nc.scalar.activation(w_hi[:, n % SPLIT, :], raw[:, n % RAW, :], ACT.Copy).then_inc(hi_ready, 1)
                    at["unit"] += 1

            def next_tile():
                i = at["tile"]
                first, t = PLACE.first_block[i], TILES[i]
                split_through(max((first + t.k * t.wide - 1) // UNIT, first // UNIT + SPLIT - 1))
                at["tile"] += 1
                return PLACE.first_out[i]

            def take(dst, c0, c1, func=ACT.Copy, scale=1.0, bias=0.0):
                n = next_tile()
                E.need(tile_done)
                src = LIN[n % len(LIN)][:dst.shape[0], c0:c1]
                if len(dst.shape) == 3:
                    src = src.rearrange("p (s n) -> p s n", n=SEQ)
                nc.scalar.activation(dst, src, func, bias=bias, scale=scale).then_inc(tile_out, 1)

            def take_values(dst, v):
                n = next_tile()
                for i in range(PLACE.outs[at["tile"] - 1]):
                    E.need(tile_done)
                    nc.scalar.activation(dst[:, i, v * 2 * P:(v + 1) * 2 * P], LIN[(n + i) % len(LIN)][:, 0:2 * P],
                                         ACT.Copy).then_inc(tile_out, 1)

            def square(k, src, c0, c1):
                nc.scalar.activation(work[:, k, c0:c1], src[:, k, c0:c1], ACT.Square).then_inc(sq_ready, 1)

            def squares_of_x(c0, c1, updated=True):
                for k in range(KD):
                    if updated:
                        E.need(x_ready)
                    square(k, xs, c0, c1)

            def root(c0, c1, n):
                nc.scalar.preload_act_table(ACT.Sqrt)
                E.need(stat_ready)
                nc.scalar.activation(sd[:, c0:c1], STAT[:, c0:c1], ACT.Sqrt, bias=eps[:, 0:1], scale=1.0 / n)\
                    .then_inc(std_ready, 1)

            def split_norm(c0, c1):
                for k in range(KD):
                    E.need(norm_rows)
                    nc.scalar.activation(h_hi[:, k, c0:c1], work[:, k, c0:c1], ACT.Copy).then_inc(hi_done, 1)

            def split_shifted(n, l, c0):
                for k in range(KD):
                    E.need(norm_rows)
                    for i in range(c0 // SEQ, 2):
                        part = slice(i * SEQ, (i + 1) * SEQ)
                        last = nc.scalar.activation(h_hi[:, k, part], work[:, k, part], ACT.Identity,
                                                    bias=mod[:, l, 3 * n * KD + k, i:i + 1])
                    last.then_inc(hi_done, 1)

            def take_rows(x0, x1):
                c0, c1 = LAT
                for f in range(KD + 1):
                    if f < KD:
                        take(mix[:, f, c0:c1], x0, x1)
                    if f:
                        act.wait_ge(tile_out, E.seen[tile_done.name] - (f < KD))
                        square(f - 1, mix, c0, c1)

            def take_update(c0, c1, next_norm):
                for f in range(KD + 1):
                    if f < KD:
                        take(mix[:, f, c0:c1], c0, c1)
                    if f and next_norm:
                        E.need(x_ready)
                        square(f - 1, xs, c0, c1)

            act.wait_ge(params_in, 16 * 5)
            at_c = VEC["c"][0]
            nc.scalar.activation(silu_c[:, :, :], vec[:, at_c:at_c + 2 * KD], ACT.Silu).then_inc(silu_c_ready, 1)
            E.need(trig_args)
            nc.scalar.activation(sin1[:, :], ang[:, :], ACT.Sin)
            nc.scalar.activation(cos1[:, :], ang2[:, :], ACT.Sin).then_inc(trig_done, 1)
            for n in range(N_ADA):
                act.wait_ge(ada_used, 2 * n + 2)
                l, c = n // (N_ADA // DEPTH), n % (N_ADA // DEPTH)
                if c == 0 and l:
                    E.need(mod_turned)
                nc.scalar.activation(mod_rows[0:2, c * ADA_COLS:(c + 1) * ADA_COLS],
                                     LIN[n % len(LIN)][0:2, 0:ADA_COLS], ACT.Copy).then_inc(ada_out, 1)

            act.wait_ge(x_in_sem, 32)
            c0, c1 = LAT
            for l in range(DEPTH):
                squares_of_x(c0, c1, updated=l > 0)
                split_through(SPLIT - 1)
                root(c0, c1, D)
                split_norm(c0, c1)

                def split_y(b, rows):
                    E.need(y_rows)
                    nc.scalar.activation(y1_hi[:, b, :], rows, ACT.Copy).then_inc(y_hi_done, 1)

                def square_heads(o, i):
                    nc.scalar.activation(o_sq[:, i, :], o[:, 2 * i:2 * i + 2, :], ACT.Square).then_inc(sq_ready, 1)

                for step, i in MIX1:
                    if step == "g":
                        for j in range(2):
                            take(gqk[:, 0, j, :], c0, c1, scale=GK ** -0.5)
                            take(gqk[:, 1, j, :], c0, c1)
                        take(ga_t[:, :], c0, c1)
                    elif step == "r":
                        take(rq_raw[:, i, 0, :], c0, c1, scale=RD ** -0.5)
                        take(rq_raw[:, i, 1, :], c0, c1)
                    elif step == "rv":
                        take_values(rv, i)
                    elif step == "gv":
                        take_values(gv, i)
                    elif step == "c":
                        if i >= 2:
                            act.wait_ge(conv_used, 4 * l + i - 1)
                        for j in range(3):
                            take(conv_in[:, i % 2, j, :], c0, c1)
                    elif step == "rg":
                        for j in range(RH):
                            take(silu_r[:, j, :], c0, c1, ACT.Silu)
                    elif step == "gr":
                        for j in range(GH):
                            take(silu_g[:, j, :], c0, c1, ACT.Silu)
                    elif step == "logit":
                        E.need(logit_done)
                        for j in range(2):
                            last = nc.scalar.activation(logit[:, j, :], X[0][:, j * SEQ:(j + 1) * SEQ], ACT.Identity,
                                                        bias=v_("gla_b_a", l, j))
                        last.then_inc(logit_out, 1)
                        act.wait_ge(logit_out, l + 1)
                        C.do(nc.scalar.activation(gdec[:, :, :], logit[:, :, :], ACT.Abs))
                        C.settle()
                        C.do(nc.scalar.activation(gdec[:, :, :], gdec[:, :, :], ACT.Exp, scale=-1.0))
                        C.settle()
                        nc.scalar.activation(gdec[:, :, :], gdec[:, :, :], ACT.Ln, bias=1.0).then_inc(logit_ln, 1)
                    elif step == "diff":
                        E.need(lev_diff)
                        C.do(nc.scalar.activation(gdec[:, :, :], gdec[:, :, :], ACT.Abs))
                        C.settle()
                        nc.scalar.activation(gdec[:, :, :], gdec[:, :, :], ACT.Exp, scale=-1.0 / GTAU)\
                            .then_inc(lev_exp, 1)
                    elif step == "mix":
                        E.need(ret_o_done)
                        nc.scalar.activation(o_ret[:, i, :], X[4][:, 0:SEQ], ACT.Copy).then_inc(ret_o_out, 1)
                    elif step == "gout":
                        for h in range(GH):
                            E.need(gla_o_done)
                            nc.scalar.activation(o_gla[:, h, :], X[4][:, 0:SEQ], ACT.Copy).then_inc(gla_o_out, 1)
                    elif step == "norm":
                        E.need(centred)
                        square_heads(o_ret, i)
                        root(0, T2, RD)
                    elif step == "split":
                        for j in range(2):
                            split_y(4 + 2 * i + j, o_ret[:, 2 * i + j, :])
                act.wait_ge(gla_o_out, GH * (l + 1))
                square_heads(o_gla, 0)
                for b in range(3):
                    for f in range(KD):
                        if b or f >= 2:
                            act.wait_ge(merge_used, 3 * KD * l + KD * b + f - 1)
                        take(gate1[:, f % 2, :], c0, c1, ACT.Sigmoid)
                        take(branch1[:, f % 2, :], 0, SEQ)
                        if b == 0 and f in (1, 3):
                            root(0, T2, GV)
                            if f == 1:
                                square_heads(o_gla, 1)
                        elif b == 0 and f in (2, 4):
                            for j in range(2):
                                split_y(8 + f - 2 + j, o_gla[:, f - 2 + j, :])
                for f in range(KD):
                    E.need(merged_rows)
                    nc.scalar.activation(y1_hi[:, f, :], mix[:, f, 0:SEQ], ACT.Copy).then_inc(merged_hi, 1)
                take_rows(0, SEQ)
                root(c0, c1, D)
                squares_of_x(c0, c1)
                root(c0, c1, D)
                split_norm(c0, c1)
                for t in range(NFF):
                    take(ff_g[:, t % 2, :], c0, c1, ACT.Silu)
                    take(ff_u[:, t % 2, :], c0, c1)
                    if t >= 1:
                        E.need(ff_rows)
                        nc.scalar.activation(hid_hi[:, t - 1, :], ff_p[:, (t - 1) % 2, :], ACT.Copy).then_inc(ff_hi, 1)
                E.need(ff_rows)
                nc.scalar.activation(hid_hi[:, NFF - 1, :], ff_p[:, (NFF - 1) % 2, :], ACT.Copy).then_inc(ff_hi, 1)
                take_rows(0, SEQ)
                root(c0, c1, D)

            for l in range(DEPTH):
                c0 = 0 if l < DEPTH - 1 else SEQ
                cols = slice(c0, T2)
                if l == 0:
                    squares_of_x(0, T2)
                root(0, T2, D)
                split_shifted(0, l, 0)
                for i in range(4):
                    if i >= 2:
                        act.wait_ge(cin_used, 4 * l + i - 1)
                    take(cin[:, i % 2, 0, cols], c0, T2)
                    take(cin[:, i % 2, 1, cols], c0, T2, ACT.Sigmoid)
                for j in range(AG):
                    take(aq[:, j, cols], c0, T2)
                take(aq[:, AG, :], 0, T2)
                take(av_t[:, :], 0, T2)
                take(mg_t[:, :], 0, T2)
                act.wait_ge(tile_out, E.seen[tile_done.name])
                for j in range(AG + 1):
                    a = c0 if j < AG else 0
                    nc.scalar.activation(a_sq[:, a:T2], aq[:, j, a:T2], ACT.Square).then_inc(sq_ready, 1)
                    if j:
                        E.need(aq_scaled)
                    root(a, T2, AD)
                E.need(aq_scaled)
                E.need(av_turned)
                nc.scalar.activation(av[:, :, :], X[2][:, :].rearrange("p (t n) -> p t n", n=P), ACT.Copy)\
                    .then_inc(av_out, 1)
                steps, before = att_steps(l), att_before(l)
                for i in range(len(steps) + 2):
                    if i < len(steps):
                        keys = steps[i][3]
                        E.need(a_neg)
                        nc.scalar.activation(p_sb[:, i % 2, 0:keys], X[i % 2][:, 0:keys], ACT.Exp,
                                             bias=a_stat[:, i % 2, 1:2], scale=AD ** -0.5,
                                             accum_out=a_stat[:, i % 2, 2:3]).then_inc(a_exp, 1)
                    if 1 <= i <= len(steps):
                        keys, b = steps[i - 1][3], (i - 1) % 2
                        E.need(a_turned)
                        if i > 2:
                            act.wait_ge(a_o_done, before + i - 2)
                        nc.scalar.activation(pt_sb[:, b, 0:keys], X[2 + b][:, 0:keys], ACT.Copy).then_inc(a_pt, 1)
                    if i >= 2 and steps[i - 2][2] == 1:
                        q, j, _, _ = steps[i - 2]
                        act.wait_ge(a_o_done, before + i - 1)
                        nc.scalar.activation(y2_hi[:, 4 + j, q * P:(q + 1) * P], X[4][:, 0:P], ACT.Copy)\
                            .then_inc(a_o_hi, 1)
                E.need(centred)
                for i in range(4):
                    nc.scalar.activation(cin[:, i // 2, i % 2, cols], cy[:, i, cols], ACT.Square).then_inc(sq_ready, 1)
                root(c0, T2, CONV)
                for i in range(4):
                    E.need(ln_rows)
                    C.do(nc.scalar.activation(cy[:, i, cols], cy[:, i, cols], ACT.Silu, bias=v_("conv_ln_b_2", l, i),
                                              scale=v_("conv_ln_w_2", l, i)))
                for i in range(4):
                    if i == 0:
                        C.settle()
                    nc.scalar.activation(y2_hi[:, i, cols], cy[:, i, cols], ACT.Copy).then_inc(y_hi_done, 1)
                E.need(pre_ready)
                C.do(nc.scalar.activation(lsg[:, :, :], pre[:, :, :], ACT.Abs))
                C.settle()
                C.do(nc.scalar.activation(lsg[:, :, :], lsg[:, :, :], ACT.Exp, scale=-1.0))
                C.settle()
                nc.scalar.activation(lsg[:, :, :], lsg[:, :, :], ACT.Ln, bias=1.0).then_inc(lsg_ln, 1)

                def take_merge(b, gate):
                    for f in range(KD):
                        if b % 3 or f >= 2:
                            act.wait_ge(merge2_used, KD * b + f - 1)
                        take(gate_sb[:, f % 2, cols], c0, T2, ACT.Sigmoid, bias=v_("branch_gate_b_2", l, gate * KD + f))
                        take(branch_sb[:, f % 2, cols], c0, T2)

                take_merge(3 * l, 0)
                take_merge(3 * l + 1, 2)

                def take_queries_keys():
                    for i in range(2):
                        take(mqk[:, i, cols], c0, T2)
                    for i in range(2):
                        take(mqk[:, 2 + i, :], 0, T2, scale=MD ** -0.5)

                take_queries_keys()
                act.wait_ge(merge2_used, KD * (3 * l + 2))
                for h in range(MH):
                    n_head = l * MH + h
                    for t in range(4):
                        E.need(m_score)
                        nc.scalar.activation(s_sb[:, t, cols], X[t % 2][:, cols], ACT.Copy).then_inc(m_score_out, 1)
                    for d in range(2):
                        if d == 0:
                            take_values(mv, 0)
                            for i in range(2):
                                take(smo[:, i, cols], c0, T2, ACT.Sigmoid)
                        E.need(em_in)
                        if d:
                            act.wait_ge(m_taken, 2 * n_head + 1)
                        nc.scalar.activation(em[:, cols], X[4][:, cols], ACT.Exp, scale=-1.0).then_inc(em_out, 1)
                        for n, t in enumerate(ORDER[d]):
                            E.need(w_arg)
                            a, b = hull(spans(d, t, c0)[0])
                            w = wgt[:, (4 * d + n) % 3, a:b]
                            nc.scalar.activation(w, w, ACT.Exp, scale=-1.0).then_inc(w_exp, 1)
                        act.wait_ge(m_acc, 8 * n_head + 4 * d + 4)
                        nc.scalar.activation(nt[:, cols], X[3][:, cols], ACT.Abs).then_inc(den_abs, 1)
                    if h + 1 < MH:
                        take_queries_keys()
                    E.need(head_done)
                    for i in range(2):
                        nc.scalar.activation(s_sb[:, i, cols], hacc[:, i, cols], ACT.Square).then_inc(sq_ready, 1)
                    root(c0, T2, MD)
                    for i in range(2):
                        E.need(y_rows)
                        nc.scalar.activation(y2_hi[:, 2 * h + i, cols], hacc[:, i, cols], ACT.Copy).then_inc(y_hi_done, 1)
                take_merge(3 * l + 2, 1)
                for f in range(KD):
                    E.need(merged_rows)
                    nc.scalar.activation(h_hi[:, f, cols], mix[:, f, cols], ACT.Copy).then_inc(merged_hi, 1)
                take_update(c0, T2, True)
                root(c0, T2, D)
                split_shifted(1, l, c0)
                E.need(up_zero)
                first = c0 // SEQ
                for half in range(2):
                    n0 = NFF * l + FF_HALF * half
                    for t in range(FF_HALF + 2):
                        if t < FF_HALF:
                            if t >= 2:
                                act.wait_ge(fc_rows, n0 + t - 1)
                            for j in range(2):
                                take(up[:, t % 2, j, first:2, 1:SEQ + 1], c0, T2)
                        if 1 <= t <= FF_HALF:
                            E.need(fc_rows)
                            g = fc[:, (t - 1) % 2, 1, cols]
                            nc.scalar.activation(g, g, ACT.Silu).then_inc(fc_gate, 1)
                        if t >= 2:
                            E.need(ff2_rows)
                            nc.scalar.activation(hid2_hi[:, t - 2, cols], fh[:, t % 2, cols], ACT.Copy).then_inc(ff2_hi, 1)
                    take_update(c0, T2, half == 1 and l < DEPTH - 1)

        @block.vector
        def _(dve):
            E = Expect(dve)
            C = Chain(dve, dve_chain)
            V = nc.vector
            MUL, ADD, SUB = ALU.mult, ALU.add, ALU.subtract

            def inverse_root(c0, c1):
                E.need(std_ready)
                C.do(V.reciprocal(sd[:, c0:c1], sd[:, c0:c1]))
                C.settle()

            def norm1(name, l):
                c0, c1 = LAT
                inverse_root(c0, c1)
                for k in range(KD + 2):
                    if k < KD:
                        V.scalar_tensor_tensor(work[:, k, c0:c1], xs[:, k, c0:c1], v_(name, l, k), sd[:, c0:c1],
                                               MUL, MUL).then_inc(norm_rows, 1)
                    if k >= 2:
                        E.need(hi_done)
                        V.tensor_tensor(h_lo[:, k - 2, c0:c1], work[:, k - 2, c0:c1], h_hi[:, k - 2, c0:c1], SUB)\
                            .then_inc(h_ready, 1)

            def add_normed(name, l):
                c0, c1 = LAT
                inverse_root(c0, c1)
                written = []
                for k in range(KD + 1):
                    if k < KD:
                        written.append(C.do(V.scalar_tensor_tensor(work[:, k, c0:c1], mix[:, k, c0:c1], v_(name, l, k),
                                                                   sd[:, c0:c1], MUL, MUL)))
                    if k:
                        C.settle(written[k - 1])
                        V.tensor_tensor(xs[:, k - 1, c0:c1], xs[:, k - 1, c0:c1], work[:, k - 1, c0:c1], ADD)\
                            .then_inc(x_ready, 1)

            dve.wait_ge(params_in, 16 * 5)
            C.do(V.memset(eps[:, :], EPS))
            C.do(V.tensor_copy(ang[:, :], pos_i[:, :]))
            C.settle()
            C.do(V.tensor_scalar(ang[:, :], ang[:, :], c_("inv_freq"), None, MUL))
            C.settle()
            ROUND = 1.5 * 2.0 ** 23
            T1 = 6.28125
            T2_ = 0.0019350051879882812
            T3 = 2 * np.pi - T1 - T2_
            for dst, quarter in ((ang2, 0.25), (ang, 0.0)):
                C.do(V.tensor_scalar(turns[:, :], ang[:, :], float(1 / (2 * np.pi)), quarter, MUL, ADD))
                C.settle()
                C.do(V.tensor_scalar(turns[:, :], turns[:, :], ROUND, ROUND, ADD, SUB))
                C.settle()
                src = ang
                for part in (T1, T2_, T3):
                    C.do(V.scalar_tensor_tensor(dst[:, :], turns[:, :], -float(part), src[:, :], MUL, ADD))
                    C.settle()
                    src = dst
                if quarter:
                    C.do(V.tensor_scalar(dst[:, :], dst[:, :], float(np.pi / 2), None, ADD))
                    C.settle()
                last = V.tensor_scalar(dst[:, :], dst[:, :], 3.1415925, -3.1415925, ALU.min, ALU.max)
                if quarter:
                    C.do(last)
            last.then_inc(trig_args, 1)
            for l in range(DEPTH):
                E.need(mod_turned)
                turned = X[l][:, 0:2 * 6 * KD].rearrange("p (i s) -> p i s", s=2)
                V.tensor_tensor(mod[:, l, :, :], turned,
                                v_("ada_b_2", l, 0, 6 * KD).unsqueeze(2).to_broadcast([P, 6 * KD, 2]), ADD)\
                    .then_inc(mod_ready, 1)
            E.need(trig_done)

            dve.wait_ge(x_in_sem, 32)
            c0, c1 = LAT
            for l in range(DEPTH):
                if l:
                    dve.wait_ge(x_ready, 2 * KD * l)
                norm1("norm_mix_pre", l)
                both = [P, 2, SEQ]
                outs = {}

                def pairs(level):
                    return gmask[:, level, :].unsqueeze(1).unsqueeze(1).to_broadcast([P, 2, 2, P])

                def blocks_of(bank):
                    return bank[:, :].rearrange("p (h j n) -> p h j n", h=2, j=2)

                def head_norm(o, i, name):
                    inverse_root(0, T2)
                    for h in (2 * i, 2 * i + 1):
                        C.do(V.scalar_tensor_tensor(o[:, h, :], o[:, h, :], v_(name, l, h),
                                                    sd[:, h % 2 * SEQ:(h % 2 + 1) * SEQ], MUL, MUL))
                    C.settle()
                    for h in (2 * i, 2 * i + 1):
                        gate = (silu_r if o is o_ret else silu_g)[:, h, :]
                        V.tensor_tensor(o[:, h, :], o[:, h, :], gate, MUL).then_inc(y_rows, 1)

                def head_low(o, i, first):
                    for h in (2 * i, 2 * i + 1):
                        E.need(y_hi_done)
                        last = V.tensor_tensor(y1_lo[:, first + h, :], o[:, h, :], y1_hi[:, first + h, :], SUB)
                    if i:
                        last.then_inc(y_ready, 1)

                for step, i in MIX1:
                    if step in ("g", "r", "rv", "gv", "c", "rg", "gr"):
                        n = {"g": 5, "r": 2, "rv": 2, "gv": 2, "c": 3, "rg": RH, "gr": GH}[step]
                        outs[step] = outs[step, i] = E.later(tile_out, n)
                    elif step == "diag":
                        C.do(V.memset(g_acc[:, :, :, :], 0.0))
                        C.settle()
                        E.need(lev_done)
                        for odd in range(2):
                            last = V.copy_predicated(g_acc[:, odd::2, 0::2, :], pairs(len(GLA_LEVELS)),
                                                     blocks_of(X[1 + odd]))
                        last.then_inc(lev_taken, 1)
                        dve.wait_ge(lev_taken, N_LEV * l + 1)
                    elif step == "rot":
                        dve.wait_ge(tile_out, outs["r", i])
                        C.do(V.tensor_tensor(rqk[:, i, :, :], rq_raw[:, i, :, :],
                                             cos1[:, :].unsqueeze(1).to_broadcast(both), MUL))
                        E.need(rot_done)
                        C.settle()
                        C.do(V.tensor_tensor(rq_raw[:, i, :, :], X[0][:, :].rearrange("p (a n) -> p a n", a=2),
                                             sin1[:, :].unsqueeze(1).to_broadcast(both), MUL))
                        C.settle()
                        V.tensor_tensor(rqk[:, i, :, :], rqk[:, i, :, :], rq_raw[:, i, :, :], ADD).then_inc(qk_ready, 1)
                    elif step == "score":
                        E.need(score_done)
                        if i or l:
                            E.need(ret_o_done)
                        V.tensor_tensor(ret_a[:, :], X[3][:, 0:3 * P], dec[:, i, :], MUL).then_inc(ret_a_ready, 1)
                    elif step == "gates":
                        E.need(logit_out)
                        E.need(logit_ln)
                        C.do(V.tensor_scalar(logit[:, :, :], logit[:, :, :], 0.0, None, ALU.min))
                        C.settle()
                        C.do(V.tensor_tensor(logit[:, :, :], logit[:, :, :], gdec[:, :, :], SUB))
                        C.do(V.memset(k_dec[:, 0, :], 1.0))
                        C.settle()
                        for j in range(2):
                            C.do(V.tensor_tensor_scan(g_cum[:, j, :], k_dec[:, 0, :], logit[:, j, :], 0.0, MUL, ADD))
                        C.settle()
                    elif step == "diff":
                        m = ([P] + GLA_LEVELS)[i]
                        blocks = g_cum[:, :, :].rearrange("p a (b t) -> p (a b) t", t=2 * m)
                        middle = blocks[:, :, m - 1:m].to_broadcast([P, 2 * SEQ // (2 * m), 2 * m])
                        V.tensor_tensor(gdec[:, :, :].rearrange("p a (b t) -> p (a b) t", t=2 * m), blocks, middle, SUB)\
                            .then_inc(lev_diff, 1)
                    elif step == "rows":
                        E.need(lev_exp)
                        C.do(V.tensor_tensor(q_dec[:, :, :], gqk[:, 0, :, :], gdec[:, :, :], MUL))
                        V.tensor_tensor(k_dec[:, :, :], gqk[:, 1, :, :], gdec[:, :, :], MUL).then_inc(lev_rows, 1)
                        C.settle()
                        dve.wait_ge(lev_rows, (N_LEV - 1) * l + i + 1)
                    elif step == "take":
                        E.need(lev_done)
                        for odd in range(2):
                            if i == 0:
                                last = V.tensor_copy(g_acc[:, odd::2, 1, :],
                                                     X[1 + odd][:, 0:2 * P].rearrange("p (h n) -> p h n", n=P))
                            else:
                                last = V.copy_predicated(g_acc[:, odd::2, 0::2, :], pairs(i - 1), blocks_of(X[1 + odd]))
                        last.then_inc(lev_taken, 1)
                        dve.wait_ge(lev_taken, N_LEV * l + i + 2)
                    elif step == "conv":
                        if i == 0:
                            C.do(V.memset(zrow[:, 0:2], 0.0))
                        dve.wait_ge(tile_out, outs["c", i])
                        u, g, b = (conv_in[:, i % 2, j, :] for j in range(3))
                        C.do(V.tensor_tensor(zrow[:, 2:], u, g, MUL))
                        C.settle()
                        y = conv_y[:, i % 2, :]
                        C.do(V.tensor_scalar(y, zrow[:, 0:SEQ], v_("conv_w", l, i), None, MUL))
                        for j in (1, 2):
                            C.settle()
                            C.do(V.scalar_tensor_tensor(y, zrow[:, j:j + SEQ], v_("conv_w", l, 4 * j + i), y, MUL, ADD))
                        C.settle()
                        C.do(V.tensor_tensor(y, y, b, MUL))
                        C.settle()
                        V.tensor_copy(y1_hi[:, i, :], y).then_inc(conv_used, 1)
                        dve.wait_ge(conv_used, 4 * l + i + 1)
                        last = V.tensor_tensor(y1_lo[:, i, :], y, y1_hi[:, i, :], SUB)
                        if i < 3:
                            C.do(last)
                        else:
                            last.then_inc(y_ready, 1)
                    elif step == "mean":
                        for j in range(2):
                            E.need(mean_done)
                            two = o_ret[:, 2 * j:2 * j + 2, :]
                            V.scalar_tensor_tensor(two, X[3 * j][:, :].rearrange("p (a n) -> p a n", a=2), -1.0 / RD, two,
                                                   MUL, ADD).then_inc(centred, 1)
                        due = E.seen[mean_done.name]
                        dve.wait_ge(centred, due)
                    elif step == "norm":
                        dve.wait_ge(tile_out, outs["rg"])
                        head_norm(o_ret, i, "ret_gn_w")
                    elif step == "split":
                        head_low(o_ret, i, 4)
                for b in range(3):
                    for f in range(KD):
                        E.need(tile_out, 2)
                        g, y, p = gate1[:, f % 2, :], branch1[:, f % 2, :], prod1[:, f % 2, :]
                        if b == 0:
                            V.tensor_tensor(mix[:, f, 0:SEQ], g, y, MUL).then_inc(merge_used, 1)
                            if f in (1, 3):
                                head_norm(o_gla, f // 2, "gla_gn_w")
                            elif f in (2, 4):
                                head_low(o_gla, f // 2 - 1, 8)
                            continue
                        V.tensor_tensor(p, g, y, MUL).then_inc(merge_used, 1)
                        dve.wait_ge(merge_used, 3 * KD * l + KD * b + f + 1)
                        last = V.tensor_tensor(mix[:, f, 0:SEQ], mix[:, f, 0:SEQ], p, ADD)
                        if b == 2:
                            last.then_inc(merged_rows, 1)
                        else:
                            C.do(last)
                            C.settle()
                for f in range(KD):
                    E.need(merged_hi)
                    last = V.tensor_tensor(y1_lo[:, f, :], mix[:, f, 0:SEQ], y1_hi[:, f, :], SUB)
                last.then_inc(merged_ready, 1)
                E.need(tile_out, KD)
                add_normed("norm_mix_post", l)
                dve.wait_ge(x_ready, KD * (2 * l + 1))
                norm1("norm_ffn_pre", l)
                for t in range(NFF):
                    E.need(tile_out, 2)
                    if t >= 2:
                        dve.wait_ge(ff_ready, NFF * l + t - 1)
                    V.tensor_tensor(ff_p[:, t % 2, :], ff_g[:, t % 2, :], ff_u[:, t % 2, :], MUL).then_inc(ff_rows, 1)
                    if t:
                        dve.wait_ge(ff_hi, NFF * l + t)
                        V.tensor_tensor(hid_lo[:, t - 1, :], ff_p[:, (t - 1) % 2, :], hid_hi[:, t - 1, :], SUB)\
                            .then_inc(ff_ready, 1)
                dve.wait_ge(ff_hi, NFF * (l + 1))
                V.tensor_tensor(hid_lo[:, NFF - 1, :], ff_p[:, (NFF - 1) % 2, :], hid_hi[:, NFF - 1, :], SUB)\
                    .then_inc(ff_ready, 1)
                E.need(tile_out, KD)
                add_normed("norm_ffn_post", l)

            def norm2(n, l, c0):
                inverse_root(c0, T2)
                streams = [(i, slice(i * SEQ, (i + 1) * SEQ)) for i in range(c0 // SEQ, 2)]
                for k in range(KD + 2):
                    if k < KD:
                        for i, part in streams:
                            last = V.scalar_tensor_tensor(work[:, k, part], xs[:, k, part], gain[:, n, k, i:i + 1],
                                                          sd[:, part], MUL, MUL)
                        last.then_inc(norm_rows, 1)
                    if k >= 2:
                        E.need(hi_done)
                        for i, part in streams:
                            last = V.scalar_tensor_tensor(h_lo[:, k - 2, part], work[:, k - 2, part],
                                                          mod[:, l, 3 * n * KD + k - 2, i:i + 1], h_hi[:, k - 2, part],
                                                          ADD, SUB)
                        last.then_inc(h_ready, 1)

            def add_gated(part_of_mod, l, c0, signal):
                for f in range(KD):
                    E.need(tile_out)
                    for i in range(c0 // SEQ, 2):
                        part = slice(i * SEQ, (i + 1) * SEQ)
                        last = V.scalar_tensor_tensor(xs[:, f, part], mix[:, f, part],
                                                      mod[:, l, part_of_mod * KD + f, i:i + 1], xs[:, f, part], MUL, ADD)
                        if not signal:
                            C.do(last)
                    if signal:
                        last.then_inc(x_ready, 1)
                if not signal:
                    C.settle()
                else:
                    updates["x"] += KD
                    dve.wait_ge(x_ready, updates["x"])

            updates = {"x": 2 * KD * DEPTH}
            dve.wait_ge(x_ready, updates["x"])
            for l in range(DEPTH):
                c0 = 0 if l < DEPTH - 1 else SEQ
                cols = slice(c0, T2)
                first, ns = c0 // SEQ, 2 - c0 // SEQ
                for n in range(2):
                    C.do(V.scalar_tensor_tensor(gain[:, n, :, :], mod[:, l, (3 * n + 1) * KD:(3 * n + 2) * KD, :], 1.0,
                                                v_(("norm1_w_2", "norm2_w_2")[n], l, 0, KD).unsqueeze(2)
                                                .to_broadcast([P, KD, 2]), ADD, MUL))
                norm2(0, l, 0)
                C.do(V.memset(z2[:, :, :, :], 0.0))
                C.settle()

                def by_stream(rows):
                    return rows.rearrange("p (s n) -> p s n", n=SEQ)

                for i in range(0, 4, 2):
                    for j in range(2):
                        E.need(tile_out, 2)
                        V.tensor_tensor(z2[:, j, first:2, PAD:PAD + SEQ], by_stream(cin[:, j, 0, cols]),
                                        by_stream(cin[:, j, 1, cols]), MUL).then_inc(cin_used, 1)
                    dve.wait_ge(cin_used, 4 * l + i + 2)
                    for tap in range(CONV_K):
                        for j in range(2):
                            y = by_stream(cy[:, i + j, cols])
                            z = z2[:, j, first:2, tap:tap + SEQ]
                            w = v_("conv_dw_w_2", l, 4 * tap + i + j)
                            if tap == 0:
                                C.do(V.tensor_scalar(y, z, w, v_("conv_dw_b_2", l, i + j), MUL, ADD))
                            else:
                                C.do(V.scalar_tensor_tensor(y, z, w, y, MUL, ADD))
                        C.settle()
                dve.sem_inc(cy_ready, 1)
                E.need(tile_out, AG + 3)
                for j in range(AG + 2):
                    if j <= AG:
                        a = c0 if j < AG else 0
                        inverse_root(a, T2)
                        V.scalar_tensor_tensor(aq[:, j, a:T2], aq[:, j, a:T2],
                                               v_("q_norm_w_2" if j < AG else "k_norm_w_2", l), sd[:, a:T2], MUL, MUL)\
                            .then_inc(aq_scaled, 1)
                    if j:
                        x = aq[:, j - 1, SEQ:T2]
                        E.need(aq_rot)
                        C.do(V.tensor_tensor(a_rot[:, :], X[j % 2][:, 0:SEQ], c_("sin_ax"), MUL))
                        C.do(V.tensor_tensor(x, x, c_("cos_ax"), MUL))
                        C.settle()
                        V.tensor_tensor(x, x, a_rot[:, :], ADD).then_inc(aq_ready, 1)
                        dve.wait_ge(aq_ready, (AG + 1) * l + j)
                steps, before = att_steps(l), att_before(l)
                for i in range(len(steps) + 2):
                    if i < len(steps):
                        keys, b = steps[i][3], i % 2
                        E.need(a_score)
                        C.do(V.reduce_max(a_stat[:, b, 0:1], X[b][:, 0:keys], AX_X))
                        C.settle()
                        V.tensor_scalar(a_stat[:, b, 1:2], a_stat[:, b, 0:1], -AD ** -0.5, None, MUL).then_inc(a_neg, 1)
                    if 1 <= i <= len(steps):
                        keys, b = steps[i - 1][3], (i - 1) % 2
                        E.need(a_exp)
                        C.do(V.reciprocal(a_stat[:, b, 3:4], a_stat[:, b, 2:3]))
                        C.settle()
                        V.tensor_scalar(p_sb[:, b, 0:keys], p_sb[:, b, 0:keys], a_stat[:, b, 3:4], None, MUL)\
                            .then_inc(a_prob, 1)
                    if i >= 2 and steps[i - 2][2] == 1:
                        q, j, _, _ = steps[i - 2]
                        E.need(a_o_hi)
                        V.tensor_tensor(y2_lo[:, 4 + j, q * P:(q + 1) * P], X[4][:, 0:P],
                                        y2_hi[:, 4 + j, q * P:(q + 1) * P], SUB).then_inc(a_o_out, 1)
                E.need(mean_done)
                for i in range(4):
                    last = V.scalar_tensor_tensor(cy[:, i, cols], X[0][:, cols], -1.0 / CONV, cy[:, i, cols], MUL, ADD)
                last.then_inc(centred, 1)
                inverse_root(c0, T2)
                for i in range(4):
                    V.tensor_tensor(cy[:, i, cols], cy[:, i, cols], sd[:, cols], MUL).then_inc(ln_rows, 1)
                for i in range(4):
                    E.need(y_hi_done)
                    last = V.tensor_tensor(y2_lo[:, i, cols], cy[:, i, cols], y2_hi[:, i, cols], SUB)
                last.then_inc(y_ready, 1)
                dve.sem_inc(y_ready, 1)
                E.need(mg_turned)
                V.tensor_tensor(pre[:, :, :], X[0][:, 0:64].rearrange("p (t g) -> p t g", g=16),
                                v_("mlstm_gate_b_2", l, 0, 16).unsqueeze(1).to_broadcast([P, 4, 16]), ADD)\
                    .then_inc(pre_ready, 1)
                E.need(lsg_ln)
                V.scalar_tensor_tensor(lsg[:, :, :], pre[:, :, :], 0.0, lsg[:, :, :], ALU.min, SUB).then_inc(lsg_ready, 1)
                E.need(fsum_done)
                sums = X[1][:, 0:4 * 2 * MH].rearrange("p (t d h) -> p t d h", t=4, d=2)
                C.do(V.tensor_copy(fsum[:, :, :, :], sums))
                dve.wait_ge(pre_ready, l + 1)
                for d in range(2):
                    last = V.tensor_tensor(gcol[:, :, d, :], pre[:, :, 8 * d:8 * d + MH],
                                           sums[:, :, d, :], SUB)
                last.then_inc(gcol_ready, 1)
                E.need(rows_turned)
                for d in range(2):
                    C.do(V.tensor_copy(g_row[:, d, :], X[2 + d][0:MH, :]))
                C.settle()
                C.do(V.tensor_tensor_scan(mx_row[:, 0, :], g_row[:, 0, :], g_row[:, 0, :], M_INIT, ALU.max, ALU.max))
                back = slice(SEQ - 1, None, -1)
                C.do(V.tensor_tensor_scan(mx_row[:, 1, back], g_row[:, 1, back], g_row[:, 1, back], M_INIT,
                                          ALU.max, ALU.max))
                C.settle()
                back = slice(T2 - 1, SEQ - 1, -1)
                C.do(V.tensor_tensor_scan(mx_row[:, 1, back], g_row[:, 1, back], g_row[:, 1, back], mx_row[:, 1, 0:1],
                                          ALU.max, ALU.max))
                C.settle()
                for d in range(2):
                    last = V.tensor_tensor(g_row[:, d, :], mx_row[:, d, :], X[4 * d][0:MH, :], ADD)
                    if d == 0:
                        C.do(last)
                last.then_inc(rows_ready, 1)

                def merge(b):
                    for f in range(KD):
                        E.need(tile_out, 2)
                        g, y, p = gate_sb[:, f % 2, cols], branch_sb[:, f % 2, cols], prod_sb[:, f % 2, cols]
                        n = KD * (3 * l + b) + f + 1
                        if b == 0:
                            V.tensor_tensor(mix[:, f, cols], g, y, MUL).then_inc(merge2_used, 1)
                            continue
                        V.tensor_tensor(p, g, y, MUL).then_inc(merge2_used, 1)
                        dve.wait_ge(merge2_used, n)
                        last = V.tensor_tensor(mix[:, f, cols], mix[:, f, cols], p, ADD)
                        if b == 2:
                            last.then_inc(merged_rows, 1)
                        else:
                            C.do(last)
                            C.settle()

                merge(0)
                merge(1)
                E.need(tile_out, 4)
                dve.wait_ge(rows_ready, l + 1)
                for h in range(MH):
                    n_head = l * MH + h
                    for d in range(2):
                        E.need(mx_done)
                        for n in range(5):
                            if n < 4:
                                t = ORDER[d][n]
                                a, b = hull(spans(d, t, c0)[0])
                                m = 8 * n_head + 4 * d + n
                                if m >= 3:
                                    dve.wait_ge(m_acc, m - 2)
                                V.tensor_scalar(wgt[:, (4 * d + n) % 3, a:b], X[2][:, a:b],
                                                gcol[:, t, d, h:h + 1], 0.0, SUB, ALU.max).then_inc(w_arg, 1)
                            if n >= 1:
                                t = ORDER[d][n - 1]
                                ranges, own = spans(d, t, c0)
                                a, b = hull(ranges)
                                w = wgt[:, (4 * d + n - 1) % 3, :]
                                if n == 1 and d == 0:
                                    dve.wait_ge(m_score_out, 4 * n_head + 4)
                                E.need(w_exp)
                                last = V.tensor_tensor(w[:, a:b], w[:, a:b], s_sb[:, t, a:b], MUL)
                                if own is not None:
                                    C.do(last)
                                    C.settle()
                                    last = V.tensor_tensor(w[:, own:own + P], w[:, own:own + P],
                                                           c_("upto" if d == 0 else "from"), MUL)
                                last.then_inc(w_ready, 1)
                        E.need(den_abs)
                        dve.wait_ge(em_out, 2 * n_head + d + 1)
                        C.do(V.tensor_tensor(nt[:, cols], nt[:, cols], em[:, cols], ALU.max))
                        C.settle()
                        C.do(V.reciprocal(nt[:, cols], nt[:, cols]))
                        C.settle()
                        for i in range(2):
                            if d == 0:
                                last = V.tensor_tensor(hacc[:, i, cols], X[i][:, cols], nt[:, cols], MUL)
                                if i == 0:
                                    C.do(last)
                                continue
                            if i:
                                C.settle()
                            last = V.tensor_tensor(em[:, cols], X[i][:, cols], nt[:, cols], MUL)
                            if i == 0:
                                C.do(last)
                                C.settle()
                                C.do(V.tensor_tensor(hacc[:, 0, cols], hacc[:, 0, cols], em[:, cols], ADD))
                        last.then_inc(m_taken, 1)
                        if d:
                            dve.wait_ge(m_taken, 2 * n_head + 2)
                            V.tensor_tensor(hacc[:, 1, cols], hacc[:, 1, cols], em[:, cols], ADD).then_inc(head_done, 1)
                        elif h or l:
                            pass
                    E.need(tile_out, 4 + 2 + (4 if h + 1 < MH else 0))
                    inverse_root(c0, T2)
                    for i in range(2):
                        C.do(V.scalar_tensor_tensor(hacc[:, i, cols], hacc[:, i, cols], v_("mlstm_norm_w_2", l, 2 * h + i),
                                                    sd[:, cols], MUL, MUL))
                    C.settle()
                    for i in range(2):
                        V.tensor_tensor(hacc[:, i, cols], hacc[:, i, cols], smo[:, i, cols], MUL).then_inc(y_rows, 1)
                    for i in range(2):
                        E.need(y_hi_done)
                        last = V.tensor_tensor(y2_lo[:, 2 * h + i, cols], hacc[:, i, cols], y2_hi[:, 2 * h + i, cols], SUB)
                        if i == 0 or h < MH - 1:
                            C.do(last)
                    if h < MH - 1:
                        C.settle()
                last.then_inc(y_ready, 1)
                merge(2)
                for f in range(KD):
                    E.need(merged_hi)
                    last = V.tensor_tensor(h_lo[:, f, cols], mix[:, f, cols], h_hi[:, f, cols], SUB)
                last.then_inc(merged_ready, 1)
                add_gated(2, l, c0, True)
                norm2(1, l, c0)
                dve.wait_ge(h_ready, KD * (DEPTH * 2 + 2 * l + 2))
                V.memset(up[:, :, :, :, :], 0.0).then_inc(up_zero, 1)
                for half in range(2):
                    n0 = NFF * l + FF_HALF * half
                    for t in range(FF_HALF + 2):
                        if t < FF_HALF:
                            E.need(tile_out, 2)
                            b = t % 2
                            if t >= 2:
                                dve.wait_ge(ff2_rows, n0 + t - 1)
                            for tap in range(3):
                                for j in range(2):
                                    y = by_stream(fc[:, b, j, cols])
                                    z = up[:, b, j, first:2, tap:tap + SEQ]
                                    at = j * NFF + half * FF_HALF + t
                                    w = v_("ffn_conv_w_2", l, 2 * NFF * tap + at)
                                    if tap == 0:
                                        C.do(V.tensor_scalar(y, z, w, v_("ffn_conv_b_2", l, at), MUL, ADD))
                                        continue
                                    last = V.scalar_tensor_tensor(y, z, w, y, MUL, ADD)
                                    if tap == 1 or j == 0:
                                        C.do(last)
                                if tap < 2:
                                    C.settle()
                            last.then_inc(fc_rows, 1)
                        if 1 <= t <= FF_HALF:
                            b = (t - 1) % 2
                            E.need(fc_gate)
                            C.settle()
                            if t >= 3:
                                dve.wait_ge(ff2_ready, n0 + t - 2)
                            V.tensor_tensor(fh[:, b, cols], fc[:, b, 0, cols], fc[:, b, 1, cols], MUL).then_inc(ff2_rows, 1)
                        if t >= 2:
                            E.need(ff2_hi)
                            V.tensor_tensor(hid2_lo[:, t - 2, cols], fh[:, t % 2, cols], hid2_hi[:, t - 2, cols], SUB)\
                                .then_inc(ff2_ready, 1)
                    add_gated(5, l, c0, half == 1)


def kernel(**inputs):
    import concourse.bacc as bacc
    from concourse.bass_utils import run_bass_kernel_spmd

    inputs = {k: np.asarray(v) for k, v in inputs.items()}
    cst, decay, masks = constants()

    def rows(a):
        return np.ascontiguousarray(a.T.reshape(KD, P, SEQ).transpose(1, 0, 2))

    arrays = {
        "stream": pack_weights(inputs),
        "vectors": pack_vectors(inputs),
        "consts": cst,
        "decay": decay,
        "gla_masks": masks,
        "positions": np.ascontiguousarray(np.broadcast_to(inputs["positions"].astype(np.int32), (P, SEQ))),
        "x_rows": rows(inputs["x"][0]),
        "ctx_rows": rows(inputs["ctx_2"][0]),
    }
    nc = bacc.Bacc("TRN2", target_bir_lowering=False, num_devices=1)
    args = [nc.dram_tensor(n, a.shape, mybir.dt.from_np(a.dtype), kind="ExternalInput").ap()
            for n, a in arrays.items()]
    out = nc.dram_tensor("out_rows", (P, KD, SEQ), F32, kind="ExternalOutput").ap()
    mixer_stack_kernel(nc, *args, out)
    got = run_bass_kernel_spmd(nc, [arrays], core_ids=[0]).results[0]["out_rows"]
    return np.ascontiguousarray(got.transpose(1, 0, 2).reshape(D, SEQ).T)[None]
```

```python
import numpy as np

import concourse.bass as bass
from concourse import mybir
from concourse.alu_op_type import AluOpType as ALU

F32 = mybir.dt.float32
F32R = mybir.dt.float32r
I32 = mybir.dt.int32
ACT = mybir.ActivationFunctionType
AX_X = mybir.AxisListType.X

P = 128
D = 1024
KD = D // P
SEQ = 256
T2 = 2 * SEQ
CTX, LAT = (0, SEQ), (SEQ, T2)
DEPTH = 2
EPS = 1e-6

CONV = 512
RH, RD = 4, 128
GH, GK, GV = 4, 64, 128
GTAU = 16.0
RANK = 16
FF = 2816
NFF = FF // P
FF_HALF = NFF // 2
CONV_K = 31
PAD = CONV_K // 2
MH, MD = 4, 256
AH, AKV, AD = 8, 2, 64
AG = AH // AKV
GRID_W = 64
M_INIT = -1e30
GLA_LEVELS = [64, 32, 16, 8, 4, 2, 1]
N_LEV = len(GLA_LEVELS) + 2

UNIT = 8
RAW, SPLIT = 3, 4
MODS = 6
ADA_LAYER = MODS * KD
ADA_UNITS = DEPTH * ADA_LAYER
ADA_SLOTS = 3
N_PLACES = 3 * KD + NFF
ADA_AT, _n = [], 0
for _i in range(N_PLACES):
    _more = 0 if 1 <= _i <= 4 or 3 * KD - 2 <= _i < 3 * KD or _i == N_PLACES - 1 else 1
    if _i < 3 * KD:
        _more = min(_more, 2 * KD - _n)
    if _i > 3 * KD and _i % 2 and _n + N_PLACES - 1 - _i < ADA_LAYER:
        _more = 2
    _more = min(_more, ADA_LAYER - _n)
    ADA_AT.append(list(range(_n, _n + _more)))
    _n += _more
assert _n == ADA_LAYER
SUM_AT = {"mix_post": [0], "ffn_pre": [1], "ffn_post": [4], "mix_pre": [5]}
for _i, _steps in enumerate(ADA_AT):
    for _s in _steps:
        if _s % KD == KD - 1 and _s // KD in (2, 3):
            SUM_AT[_i + 2] = [_s // KD]


class Tile:

    def __init__(self, name, array, layer, rows, cols):
        self.name, self.array, self.layer, self.rows, self.cols = name, array, layer, rows, cols
        self.k = len(rows)
        self.wide = len(cols) // P


def span(start, n=P):
    return list(range(start, start + n))


def stream_tiles():
    full = list(range(KD))
    out = []

    def put(name, array, layer, cols, rows=None):
        out.append(Tile(name, array, layer, full if rows is None else rows, cols))

    cu, cb, cc, rq, rk, rv, rg, gq, gk, gv, gr, ga, gates = np.cumsum(
        [0, CONV, CONV, CONV, 512, 512, 512, 512, 256, 256, 512, 512, RANK]).tolist()
    for l in range(DEPTH):
        for i in range(2):
            put("gq", "w_in", l, span(gq + i * P))
            put("gk", "w_in", l, span(gk + i * P))
        put("ga", "w_in", l, span(ga, RANK) + [-1] * (P - RANK))
        for h in range(RH):
            put("rq", "w_in", l, span(rq + h * P))
            put("rk", "w_in", l, span(rk + h * P))
        for v in range(2):
            put("rv", "w_in", l, span(rv + 256 * v, 256))
        for v in range(2):
            put("gv", "w_in", l, span(gv + 256 * v, 256))
        for i in range(4):
            put("cu", "w_in", l, span(cu + i * P))
            put("cc", "w_in", l, span(cc + i * P))
            put("cb", "w_in", l, span(cb + i * P))
        for i in range(4):
            put("rg", "w_in", l, span(rg + i * P))
        for i in range(4):
            put("gr", "w_in", l, span(gr + i * P))
        for b, name in enumerate(("w_branch_a", "w_branch_b", "w_branch_c")):
            for f in range(KD):
                put("gate", "w_in", l, span(gates + b * D + f * P))
                put("branch", name, l, span(f * P), list(range(4)))
        for f in range(KD):
            put("out", "w_out", l, span(f * P))
        for t in range(NFF):
            put("ffg", "w_ffn_gate", l, span(t * P))
            put("ffu", "w_ffn_up", l, span(t * P))
        for f in range(KD):
            put("ffd", "w_ffn_down", l, span(f * P), list(range(NFF)))

    cu, mq, mk, mv, mo, mg, aq, ak, av, bg = np.cumsum([0, 2 * CONV, D, D, D, D, 16, 512, 128, 128]).tolist()
    pair = [span(j * AD, AD) + span((j + AG) * AD, AD) for j in range(AG)]
    for l in range(DEPTH):
        for step, i in mixer2(l):
            if step == "c":
                put("ca", "w_in_2", l, span(cu + i * P))
                put("cg", "w_in_2", l, span(cu + CONV + i * P))
            elif step == "q":
                put("aq", "w_in_2", l, [aq + c for c in pair[i]])
            elif step in ("k", "v"):
                put("a" + step, "w_in_2", l, span(ak if step == "k" else av))
            elif step == "mg":
                put("mg", "w_in_2", l, span(mg, 16) + [-1] * (P - 16))
            elif step == "gate":
                put("gate", "w_in_2", l, span(bg + (0, 2, 1)[i[0]] * D + i[1] * P))
            elif step == "branch":
                name, rows = (("w_conv_out_2", 4), ("w_attn_out_2", 4), ("w_mlstm_out_2", KD))[i[0]]
                put("branch", name, l, span(i[1] * P), list(range(rows)))
            elif step in ("mq", "mk", "mo"):
                for j in range(2):
                    put(step, "w_in_2", l, span({"mq": mq, "mk": mk, "mo": mo}[step] + i * MD + j * P))
            elif step == "mv":
                put("mv", "w_in_2", l, span(mv + i * MD, MD))
        for f in range(KD):
            put("out", "w_out_2", l, span(f * P))
        for half in range(2):
            for t in range(half * FF_HALF, (half + 1) * FF_HALF):
                put("fa", "ffn_w_up_2", l, span(t * P))
                put("fg", "ffn_w_up_2", l, span(FF + t * P))
            for f in range(KD):
                put("fd", "ffn_w_down_2", l, span(f * P), span(half * FF_HALF, FF_HALF))
    return out


MIX1 = [("g", 0), ("diag", 0), ("r", 0), ("logit", 0), ("r", 1), ("rot", 0), ("gates", 0), ("diff", 0), ("r", 2),
        ("rot", 1), ("rows", 0), ("diff", 1), ("r", 3), ("rot", 2), ("take", 0), ("rows", 1), ("diff", 2),
        ("rv", 0), ("rot", 3), ("take", 1), ("rows", 2), ("diff", 3), ("score", 0), ("rv", 1), ("take", 2),
        ("rows", 3), ("diff", 4), ("score", 1), ("mix", 0), ("gv", 0), ("take", 3), ("rows", 4), ("diff", 5),
        ("score", 2), ("mix", 1), ("gv", 1), ("take", 4), ("rows", 5), ("diff", 6), ("score", 3), ("mix", 2),
        ("c", 0), ("conv", 0), ("take", 5), ("rows", 6), ("diff", 7), ("mix", 3), ("c", 1), ("conv", 1), ("take", 6),
        ("rows", 7), ("mean", 0), ("c", 2), ("conv", 2), ("take", 7), ("c", 3), ("conv", 3), ("gout", 0), ("rg", 0),
        ("norm", 0), ("gr", 0), ("split", 0), ("norm", 1)]


def att_steps(l):
    return [(q, j, g, T2 if q >= 2 else SEQ) for q in range(0 if l < DEPTH - 1 else 2, 4)
            for j in range(AG) for g in range(AKV)]


def att_before(l):
    return sum(len(att_steps(i)) for i in range(l))


EARLY = 3
TAPS1 = [0, 6, 11, 16, 21, 26, CONV_K]


def mixer2(l):
    out = [("c", 0), ("c", 1), ("glu", 0), ("c", 2), ("c", 3), ("taps", (0, 0, CONV_K)), ("glu", 2),
           ("q", 0), ("q", 1), ("q", 2), ("q", 3), ("k", 0)]
    fill = [[("v", 0)], [("mg", 0)], [("vturn", 0), ("gturn", 0), ("gate", (0, 0))], [("mq", 0), ("glsg", 0)],
            [("mk", 0), ("gsum", 0)], [("mv", 0)], [("gate", (0, f)) for f in range(1, EARLY)]]
    for j in range(AG + 3):
        if j <= AG:
            out.append(("qsq", j))
        if j >= 2:
            out.append(("qrot", j - 2))
        out += fill[j]
        if 1 <= j <= AG + 1:
            out.append(("qscale", j - 1))
        if j < len(TAPS1) - 1:
            out.append(("taps", (2, TAPS1[j], TAPS1[j + 1])))
    n = len(att_steps(l)) + 2
    ln_at = {0: 0, 2: 1, 3: 2, 5: 3}
    conv = []
    for f in range(KD + 1):
        if f < KD:
            conv += [("gate", (0, f))] if f >= EARLY else []
            conv.append(("branch", (0, f)))
        if f:
            conv.append(("merge", (0, f - 1)))
    placed = 0
    for i in range(n):
        out.append(("att", i))
        if i in ln_at:
            out.append(("ln", ln_at[i]))
        if i > 5:
            upto = len(conv) * (i - 5) // (n - 6)
            out += conv[placed:upto]
            placed = upto

    def merges(*fs):
        return [(s, (1, f)) for f in fs for s in ("gate", "branch", "merge")]

    out += [("rows", 0)] + merges(0)
    for h in range(MH):
        out += [("mscore", h), ("mmax", (h, 0)), ("em", (h, 0)), ("warg", (h, 0, 0)), ("warg", (h, 0, 1)),
                ("wmul", (h, 0, 0)), ("warg", (h, 0, 2)), ("wmul", (h, 0, 1)), ("wmul", (h, 0, 2))]
        out.append(("mo", h))
        out += [("mv", h)] if h else []
        out += [("acc", (h, 0, 0)), ("warg", (h, 0, 3)), ("acc", (h, 0, 1)), ("wmul", (h, 0, 3)),
                ("acc", (h, 0, 2)), ("mmax", (h, 1)), ("warg", (h, 1, 0)), ("warg", (h, 1, 1)), ("acc", (h, 0, 3)),
                ("wmul", (h, 1, 0)), ("wmul", (h, 1, 1)), ("taken", (h, 0))]
        behind = (merges(1, 2), merges(3, 4), merges(5, 6, 7), [("gate", (2, 0))])[h]
        out += behind[:2] + [("em", (h, 1)), ("warg", (h, 1, 2)), ("wmul", (h, 1, 2))] + behind[2:]
        out += [("acc", (h, 1, 0)), ("warg", (h, 1, 3)), ("acc", (h, 1, 1)), ("wmul", (h, 1, 3)), ("acc", (h, 1, 2)),
                ("acc", (h, 1, 3)), ("taken", (h, 1))]
        out += [("mq", h + 1)] if h + 1 < MH else [("gate", (2, 1))]
        out.append(("hsq", h))
        out += [("mk", h + 1)] if h + 1 < MH else []
        out.append(("hout", h))
    for f in range(KD):
        out += [("gate", (2, f + 1))] if 1 <= f < KD - 1 else []
        out += [("branch", (2, f)), ("merge", (2, f))]
    return out


TILES = stream_tiles()
N_BLOCKS = sum(t.k * t.wide for t in TILES)
N_UNITS = N_BLOCKS // UNIT
assert N_BLOCKS % UNIT == 0 and N_UNITS % RAW == 0


def pack_weights(inputs):
    stream = np.zeros((ADA_UNITS + N_UNITS, P, UNIT * P), np.float32)
    blocks = stream.reshape(-1, P, UNIT, P)
    n = 0

    def put(block):
        nonlocal n
        blocks[n // UNIT, :, n % UNIT, :block.shape[1]] = block
        n += 1

    for l in range(DEPTH):
        w = inputs["ada_w_2"][l]
        for c in range(0, MODS * D, D):
            for k in range(KD):
                for j in range(UNIT):
                    put(w[k * P:(k + 1) * P, c + j * P:c + (j + 1) * P])
    for t in TILES:
        w = inputs[t.array][t.layer]
        if t.array == "w_attn_out_2":
            order = [r for j in range(AG) for r in span(j * AD, AD) + span((j + AG) * AD, AD)]
            w = w[order]
        for k in t.rows:
            for j in range(t.wide):
                cols = [c for c in t.cols[j * P:(j + 1) * P] if c >= 0]
                put(w[k * P:(k + 1) * P, cols])
    assert n == N_BLOCKS + ADA_UNITS * UNIT
    return stream


def vector_layout():
    at, out = 0, {}

    def put(name, n):
        nonlocal at
        out[name] = (at, n)
        at += n

    for l in range(DEPTH):
        for name in ("norm_mix_pre", "norm_mix_post", "norm_ffn_pre", "norm_ffn_post"):
            put((name, l), KD)
        put(("conv_w", l), 3 * 4)
        put(("ret_gn_w", l), RH)
        put(("gla_gn_w", l), GH)
        put(("gla_b_a", l), 2)
        put(("gla_w_a2", l), GH * GK)
    for l in range(DEPTH):
        put(("norm1_w_2", l), KD)
        put(("norm2_w_2", l), KD)
        put(("branch_gate_b_2", l), 3 * KD)
        put(("conv_dw_w_2", l), CONV_K * 4)
        put(("conv_dw_b_2", l), 4)
        put(("conv_ln_w_2", l), 4)
        put(("conv_ln_b_2", l), 4)
        put(("mlstm_gate_b_2", l), 16)
        put(("mlstm_norm_w_2", l), KD)
        put(("q_norm_w_2", l), 1)
        put(("k_norm_w_2", l), 1)
        put(("ffn_conv_w_2", l), 3 * 2 * NFF)
        put(("ffn_conv_b_2", l), 2 * NFF)
        put(("ada_b_2", l), 6 * KD)
    put("c", 2 * KD)
    return out, at


VEC, N_VEC = vector_layout()


def pack_vectors(inputs):
    vec = np.zeros((P, N_VEC), np.float32)

    def columns(a):
        return np.ascontiguousarray(a.reshape(-1, P).T)

    for key, (at, n) in VEC.items():
        if key == "c":
            both = np.stack([inputs["c_ctx_2"], inputs["c_2"][0]])
            vec[:, at:at + n] = both.reshape(2, KD, P).transpose(2, 1, 0).reshape(P, n)
            continue
        name, l = key
        a = inputs[name][l]
        if name == "gla_w_a2":
            vec[:RANK, at:at + n] = a
        elif name == "mlstm_gate_b_2":
            vec[:, at:at + n] = np.broadcast_to(a, (P, n))
        elif name in ("q_norm_w_2", "k_norm_w_2"):
            vec[:, at] = np.concatenate([a, a])
        else:
            vec[:, at:at + n] = columns(a)
    return vec


CONST_PARTS = [("ident", P), ("rot_ret", P), ("rot_att", P), ("upto", P), ("from", P), ("ones", P),
               ("one64", P), ("cos_ax", SEQ), ("sin_ax", SEQ), ("head_row", MH * P), ("inv_freq", 1)]
CONST = {}
for _name, _n in CONST_PARTS:
    CONST[_name] = (sum(n for _, n in CONST_PARTS[:len(CONST)]), _n)
N_CONST = sum(n for _, n in CONST_PARTS)
N_DECAY = RH * 3 * P


def constants():
    c = np.zeros((P, N_CONST), np.float32)

    def at(name):
        return c[:, CONST[name][0]:CONST[name][0] + CONST[name][1]]

    p, n = np.arange(P)[:, None], np.arange(P)[None, :]
    at("ident")[:] = p == n

    def rotation(half):
        r = np.zeros((P, P), np.float32)
        for base in range(0, P, 2 * half):
            for i in range(half):
                r[base + half + i, base + i] = -1.0
                r[base + i, base + half + i] = 1.0
        return r

    at("rot_ret")[:] = rotation(RD // 2)
    at("rot_att")[:] = rotation(AD // 2)
    at("upto")[:] = p <= n
    at("from")[:] = p >= n
    at("ones")[:] = 1.0
    at("one64")[:] = p // AD == n // AD
    n_freq = AD // 4
    inv = (10000.0 ** (-np.arange(n_freq, dtype=np.float32) / n_freq)).astype(np.float32)
    tok = np.arange(SEQ)
    ang = np.concatenate([(tok // GRID_W).astype(np.float32)[:, None] * inv,
                          (tok % GRID_W).astype(np.float32)[:, None] * inv], axis=-1)
    at("cos_ax")[:] = np.tile(np.cos(ang).T, (4, 1))
    at("sin_ax")[:] = np.tile(np.sin(ang).T, (4, 1))
    for h in range(MH):
        at("head_row")[h, h * P:(h + 1) * P] = 1.0
    half = RD // 2
    at("inv_freq")[:, 0] = np.tile((10000.0 ** (-np.arange(half, dtype=np.float32) / half)).astype(np.float32), 2)
    decay = np.zeros((P, RH, 3, P), np.float32)
    for h in range(RH):
        log_g = np.log(1.0 - 2.0 ** (-5.0 - h))
        for b, off in enumerate((0, P, 0)):
            diff = n + off - p
            decay[:, h, b, :] = np.where(diff >= 0, np.exp(log_g * np.maximum(diff, 0)), 0.0)
    masks = np.zeros((P, len(GLA_LEVELS) + 1, P), np.int32)
    for i, m in enumerate(GLA_LEVELS):
        masks[:, i, :] = (p // (2 * m) == n // (2 * m)) & (p % (2 * m) < m) & (n % (2 * m) >= m)
    masks[:, -1, :] = p == n
    return c, decay.reshape(P, N_DECAY), masks.reshape(P, -1)


class Expect:

    def __init__(self, engine):
        self.engine, self.seen = engine, {}

    def need(self, sem, more=1):
        self.seen[sem.name] = self.seen.get(sem.name, 0) + more
        self.engine.wait_ge(sem, self.seen[sem.name])

    def later(self, sem, more):
        self.seen[sem.name] = self.seen.get(sem.name, 0) + more
        return self.seen[sem.name]


class Chain:

    def __init__(self, engine, sem):
        self.engine, self.sem, self.n = engine, sem, 0

    def do(self, instruction):
        instruction.then_inc(self.sem, 1)
        self.n += 1
        return self.n

    def settle(self, n=None):
        self.engine.wait_ge(self.sem, self.n if n is None else n)


class Place:

    def __init__(self):
        self.first_out, self.first_block, self.outs = [], [], []
        out = block = 0
        for t in TILES:
            self.first_out.append(out)
            self.first_block.append(block)
            n = 1
            if t.wide == 2:
                n = 2 if t.array == "w_in" else T2 // P
            self.outs.append(n)
            out += n
            block += t.k * t.wide
        self.free, ends = [None] * N_UNITS, 0
        for i, t in enumerate(TILES):
            b0, b1 = self.first_block[i], self.first_block[i] + t.k * t.wide
            for u in range(b0 // UNIT, (b1 - 1) // UNIT + 1):
                last = UNIT * (u + 1) - 1
                if b0 <= last < b1:
                    if t.wide == 2 or last == b1 - 1:
                        self.free[u] = ("tile", self.first_out[i] + self.outs[i])
                    else:
                        ends += 1
                        self.free[u] = ("unit", ends)


PLACE = Place()


def mixer_stack_kernel(nc, stream, vectors, consts, decay, gla_masks, positions, x_in, ctx_in, out):
    names = set()

    class Region:
        def __init__(self, start, size):
            self.at, self.end = start, start + size

        def put(self, name, shape, dtype=F32):
            size = 4 * int(np.prod(shape[1:]))
            size += -size % 32
            assert self.at + size <= self.end, (name, self.at + size - self.end)
            assert name not in names
            names.add(name)
            t = nc.alloc_sbuf_tensor_at(name, shape, dtype, offset=self.at)
            self.at += size
            return t

        def view(self):
            return Region(self.at, self.end - self.at)

        def part(self, size):
            self.at += size
            assert self.at <= self.end
            return Region(self.at - size, size)

    base = nc.sbuf_base + (-nc.sbuf_base % 64)
    sbuf = Region(base, nc.sbuf_usable_end - base)

    cst = sbuf.put("cst", [P, N_CONST])
    vec = sbuf.put("vec", [P, N_VEC])
    mod = sbuf.put("mod", [P, DEPTH, 6 * KD, 2])
    gain = sbuf.put("gain", [P, 2, KD, 2])
    silu_c = sbuf.put("silu_c", [P, KD, 2])
    eps = sbuf.put("eps", [P, 1])
    raw = sbuf.put("raw", [P, RAW, UNIT * P])
    w_hi = sbuf.put("w_hi", [P, SPLIT, UNIT * P], F32R)
    w_lo = sbuf.put("w_lo", [P, SPLIT, UNIT * P], F32R)
    xs = sbuf.put("xs", [P, KD, T2])
    at_h_hi = sbuf.at
    h_hi = sbuf.put("h_hi", [P, KD, T2], F32R)
    at_h_lo = sbuf.at
    h_lo = sbuf.put("h_lo", [P, KD, T2], F32R)
    sd = sbuf.put("sd", [P, T2])
    R0 = sbuf.part(4 * KD * T2)
    R1 = sbuf.part(4 * KD * T2)
    RY = sbuf.part(8 * NFF * SEQ)
    RE = sbuf.view()
    work = R0.view().put("work", [P, KD, T2])
    mix = R1.view().put("mix", [P, KD, T2])

    e = RE.view()
    dec = e.put("dec", [P, RH, 3 * P])
    gmask = e.put("gmask", [P, len(GLA_LEVELS) + 1, P], I32)
    cos1 = e.put("cos1", [P, SEQ])
    sin1 = e.put("sin1", [P, SEQ])
    ret_a = e.put("ret_a", [P, 3 * P])
    ga_t = e.put("ga_t", [RANK, SEQ])
    at_logit = e.view()
    logit = e.put("logit", [P, 2, SEQ])
    gdec = e.put("gdec", [P, 2, SEQ])
    q_dec = e.put("q_dec", [P, 2, SEQ])
    k_dec = e.put("k_dec", [P, 2, SEQ])
    zrow = e.put("zrow", [P, SEQ + 2])
    r = R0.view()
    rq_raw = r.put("rq_raw", [P, RH, 2, SEQ])
    rqk = r.put("rqk", [P, RH, 2, SEQ])
    r = R0.view()
    gate1 = r.put("gate1", [P, 2, SEQ])
    branch1 = r.put("branch1", [P, 2, SEQ])
    prod1 = r.put("prod1", [P, 2, SEQ])
    r.part(2 * 1024)
    o_sq = r.put("o_sq", [P, 2, 2 * SEQ])
    r = R0.view()
    ff_g = r.put("ff_g", [P, 2, SEQ])
    ff_u = r.put("ff_u", [P, 2, SEQ])
    ff_p = r.put("ff_p", [P, 2, SEQ])
    r = R1.view()
    g_acc = r.put("g_acc", [P, GH, 3, P])
    g_cum = r.put("g_cum", [P, 2, SEQ])
    pos_i = r.put("pos_i", [P, SEQ], I32)
    ang = r.put("ang", [P, SEQ])
    turns = r.put("turns", [P, SEQ])
    turns_i = r.put("turns_i", [P, SEQ], I32)
    ang2 = r.put("ang2", [P, SEQ])
    spare_hi = nc.alloc_sbuf_tensor_at("spare_hi", [P, KD, T2], F32, offset=at_h_hi)
    spare_lo = nc.alloc_sbuf_tensor_at("spare_lo", [P, KD, T2], F32, offset=at_h_lo)
    silu_r, silu_g = spare_hi[:, 0:RH, 0:SEQ], spare_hi[:, RH:RH + GH, 0:SEQ]
    conv_in = spare_lo[:, 0:6, 0:SEQ].rearrange("p (b j) n -> p b j n", b=2)
    conv_y = spare_lo[:, 6:8, 0:SEQ]
    ada_raw = [spare_lo[:, 0:4, 0:SEQ], spare_lo[:, 4:8, 0:SEQ], spare_hi[:, 0:4, 0:SEQ]]
    ada_tail = at_logit.put("ada_tail", [P, 4, SEQ])
    ada_acc = [[mix[:, 0:4, 0:SEQ], mix[:, 4:8, 0:SEQ]],
               [spare_hi[:, 4:8, 0:SEQ], ada_tail[:, :, :]]]
    r = RY.view()
    y1_hi = r.put("y1_hi", [P, 12, SEQ], F32R)
    y1_lo = r.put("y1_lo", [P, 12, SEQ], F32R)
    rv = r.put("rv", [P, 2, RH * RD])
    gv = r.put("gv", [P, 2, GH * GV])
    o_ret = r.put("o_ret", [P, RH, SEQ])
    o_gla = r.put("o_gla", [P, GH, SEQ])
    gqk = r.put("gqk", [P, 2, 2, SEQ])
    r = RY.view()
    hid_hi = r.put("hid_hi", [P, NFF, SEQ], F32R)
    hid_lo = r.put("hid_lo", [P, NFF, SEQ], F32R)

    e = RE.view()
    u = e.part(4 * 4 * T2)
    p_at = e.view()
    p_sb = e.put("p_sb", [P, 2, T2])
    pt_sb = e.put("pt_sb", [P, 2, T2])
    wgt = e.put("wgt", [P, 3, T2])
    a_stat = e.put("a_stat", [P, 2, 4])
    pre = e.put("pre", [P, 4, 16])
    lsg = e.put("lsg", [P, 4, 16])
    fsum = e.put("fsum", [P, 4, 2, MH])
    gcol = e.put("gcol", [P, 4, 2, MH])
    half_b = e.put("half_b", [P, DEPTH, 3 * KD])
    half_w = e.put("half_w", [P, DEPTH, KD])
    g_row = p_at.put("g_row", [MH, 2, T2])
    mx_row = p_at.put("mx_row", [MH, 2, T2])
    e = u.view()
    z2 = e.put("z2", [P, 2, 2, SEQ + 2 * PAD])
    a_sq = e.put("a_sq", [P, T2])
    a_rot = e.put("a_rot", [P, SEQ])
    e = u.view()
    gate_sb = e.put("gate_sb", [P, 2, T2])
    branch_sb = e.put("branch_sb", [P, 2, T2])
    em = sd
    r = R1.view()
    cin = r.put("cin", [P, 2, 2, T2])
    cy = r.put("cy", [P, 4, T2])
    r = R0.view()
    aq = r.put("aq", [P, AG + 1, T2])
    av_t = r.put("av_t", [P, T2])
    av = r.put("av", [P, 4, P])
    mg_t = r.put("mg_t", [16, T2])
    r = R0.view()
    s_sb = r.put("s_sb", [P, 4, T2])
    hacc = r.put("hacc", [P, 2, T2])
    smo = r.put("smo", [P, 2, T2])
    r = R0.view()
    up = r.put("up", [P, 2, 2, 2, SEQ + 2])
    e = RE.view()
    fc = e.put("fc", [P, 2, 2, T2])
    fh = e.put("fh", [P, 2, T2])
    r = RY.view()
    y2_hi = r.put("y2_hi", [P, KD, T2], F32R)
    y2_lo = r.put("y2_lo", [P, KD, T2], F32R)
    mqk = r.put("mqk", [P, 4, T2])
    mv = r.put("mv", [P, 4, MD])
    r = RY.view()
    hid2_hi = r.put("hid2_hi", [P, FF_HALF, T2], F32R)
    hid2_lo = r.put("hid2_lo", [P, FF_HALF, T2], F32R)

    def c_(name):
        return cst[:, CONST[name][0]:CONST[name][0] + CONST[name][1]]

    def v_(name, l, i=0, n=1):
        return vec[:, VEC[name, l][0] + i:VEC[name, l][0] + i + n]

    ident, ones = c_("ident"), c_("ones")

    def gate_rows(b, f):
        return wgt[:, f, :] if b == 0 and f < EARLY else gate_sb[:, f % 2, :]

    banks = [nc.alloc_psum_tensor(f"bank{i}", [P, T2], F32) for i in range(8)]
    LIN, STAT, X = banks[0:2], banks[2], banks[3:8]


    def sem(name):
        return nc.alloc_semaphore(name)

    raw_loaded = [sem(f"raw_loaded{i}") for i in range(RAW)]
    ada_loaded = [sem(f"ada_loaded{i}") for i in range(ADA_SLOTS)]
    ada_used = sem("ada_used")
    ada_summed = sem("ada_summed")
    mod_ready = sem("mod_ready")
    hi_ready = sem("hi_ready")
    lo_ready = sem("lo_ready")
    unit_used = sem("unit_used")
    tile_done = sem("tile_done")
    tile_out = sem("tile_out")
    x_loaded, ctx_loaded, vec_loaded, cst_loaded, tables_loaded, stored = [
        sem(n) for n in ("x_loaded", "ctx_loaded", "vec_loaded", "cst_loaded", "tables_loaded", "stored")]
    trig_args, trig_done, eps_ready, half_ready = [sem(n) for n in ("trig_args", "trig_done", "eps_ready", "half_ready")]
    silu_c_ready = sem("silu_c_ready")
    x_ready, sq_ready, stat_ready, std_ready = sem("x_ready"), sem("sq_ready"), sem("stat_ready"), sem("std_ready")
    norm_rows, hi_done, h_ready = sem("norm_rows"), sem("hi_done"), sem("h_ready")
    rot_done, qk_ready = sem("rot_done"), sem("qk_ready")
    score_done, ret_a_ready, ret_o_done, ret_o_out = (sem("ret_score_done"), sem("ret_a_ready"),
                                                      sem("ret_o_done"), sem("ret_o_out"))
    logit_done, logit_out, logit_ln = sem("logit_done"), sem("logit_out"), sem("logit_ln")
    lev_diff, lev_exp, lev_rows, lev_done, lev_taken = (sem("lev_diff"), sem("lev_exp"), sem("lev_rows"),
                                                        sem("lev_done"), sem("lev_taken"))
    gla_o_done, gla_o_out = sem("gla_o_done"), sem("gla_o_out")
    conv_used, conv_ready = sem("conv_used"), sem("conv_ready")
    mean_done, centred = sem("mean_done"), sem("centred")
    y_rows, y_hi_done, y_ready = sem("y_rows"), sem("y_hi_done"), sem("y_ready")
    merge_used, merged_rows, merged_hi, merged_ready = (sem("merge_used"), sem("merged_rows"), sem("merged_hi"),
                                                        sem("merged_ready"))
    ff_used, ff_rows, ff_hi, ff_ready = sem("ff_used"), sem("ff_rows"), sem("ff_hi"), sem("ff_ready")
    down_used = sem("down_used")
    av_turned, av_out = sem("av_turned"), sem("av_out")
    aq_scaled, aq_rot = sem("aq_scaled"), sem("aq_rot")
    a_score, a_neg, a_exp, a_prob, a_turned, a_pt, a_o_done, a_o_out = [
        sem(n) for n in ("a_score", "a_neg", "a_exp", "a_prob", "a_turned", "a_pt", "a_o_done", "a_o_out")]
    mg_turned, lsg_abs, lsg_ln, lsg_ready, fsum_done, gcol_ready, rows_turned, rows_ready = [
        sem(n) for n in ("mg_turned", "lsg_abs", "lsg_ln", "lsg_ready", "fsum_done", "gcol_ready",
                         "rows_turned", "rows_ready")]
    m_score, m_score_out, mx_done, w_arg, w_exp, w_ready, m_acc, em_in, em_out, m_taken, head_done = [
        sem(n) for n in ("m_score", "m_score_out", "mx_done", "w_arg", "w_exp", "w_ready", "m_acc", "em_in",
                         "em_out", "m_taken", "m_head_done")]
    cin_used, cy_ready, ln_rows, aq_ready, a_o_hi, pre_ready, merge2_used, den_abs = [
        sem(n) for n in ("cin_used", "cy_ready", "ln_rows", "aq_ready", "a_o_hi", "pre_ready", "merge2_used", "den_abs")]
    up_zero, fc_rows, fc_gate, ff2_rows, ff2_hi, ff2_ready = [
        sem(n) for n in ("up_zero", "fc_rows", "fc_gate", "ff2_rows", "ff2_hi", "ff2_ready")]
    dve_chain, act_chain = sem("dve_chain"), sem("act_chain")

    def spans(direction, tile, c0):
        own = tile * P
        if direction == 0:
            lo = max(own, c0)
            return [(lo, T2)], own if own >= c0 else None
        if tile < 2:
            if c0:
                return [(SEQ, T2)], None
            return ([(0, T2)] if tile == 1 else [(0, P), (SEQ, T2)]), own
        return [(SEQ, own + P)], own

    ORDER = {0: [0, 1, 2, 3], 1: [1, 0, 3, 2]}

    def hull(ranges):
        return ranges[0][0], ranges[-1][1]

    with nc.Block() as block:

        @block.sync
        def _(sp):
            sp.dma_start(xs[:, :, SEQ:T2], x_in).then_inc(x_loaded, 16)
            sp.dma_start(cst[:, :], consts).then_inc(cst_loaded, 16)
            sp.dma_start(vec[:, :], vectors).then_inc(vec_loaded, 16)

            def load(slot, unit):
                sp.dma_start(raw[:, slot, :], stream[unit]).then_inc(raw_loaded[slot], 16)

            for slot in range(RAW):
                load(slot, ADA_UNITS + slot)
            sp.dma_start(dec[:, :, :], decay.rearrange("p (h n) -> p h n", h=RH)).then_inc(tables_loaded, 16)
            sp.dma_start(gmask[:, :, :], gla_masks.rearrange("p (h n) -> p h n", n=P)).then_inc(tables_loaded, 16)
            sp.dma_start(pos_i[:, :], positions).then_inc(tables_loaded, 16)
            sp.dma_start(xs[:, :, 0:SEQ], ctx_in).then_inc(ctx_loaded, 16)
            with sp.Fori(1, N_UNITS // RAW) as i:
                for slot in range(RAW):
                    sp.wait_ge(lo_ready, i * RAW + (slot - RAW + 1))
                    load(slot, i * RAW + (ADA_UNITS + slot))
            for unit in range(N_UNITS // RAW * RAW, N_UNITS):
                sp.wait_ge(lo_ready, unit - RAW + 1)
                load(unit % RAW, ADA_UNITS + unit)
            sp.wait_ge(x_ready, 4 * DEPTH * KD)
            sp.dma_start(out, xs[:, :, SEQ:T2]).then_inc(stored, 16)
            sp.wait_ge(stored, 16)

        @block.gpsimd
        def _(pool):
            step = RAW * SPLIT

            def low_part(unit, ordinal):
                pool.wait_ge(hi_ready, ordinal)
                nc.gpsimd.tensor_tensor(w_lo[:, unit % SPLIT, :], raw[:, unit % RAW, :], w_hi[:, unit % SPLIT, :],
                                        ALU.subtract).then_inc(lo_ready, 1)

            with pool.Fori(0, N_UNITS // step) as i:
                for j in range(step):
                    low_part(j, i * step + (j + 1))
            for unit in range(N_UNITS // step * step, N_UNITS):
                low_part(unit, unit + 1)

        @block.tensor
        def _(pe):
            E = Expect(pe)
            at = {"tile": 0, "unit": -1, "stat": 0, "rows": 0}

            def wait_unit(u):
                if u > at["unit"]:
                    pe.wait_ge(lo_ready, u + 1)
                    at["unit"] = u

            def bank_of(n):
                if n >= len(LIN):
                    pe.wait_ge(tile_out, n - len(LIN) + 1)
                return LIN[n % len(LIN)]

            def product(x_hi, x_lo, c0, c1, count=1, fresh=None, late=None):
                for i_tile in range(count):
                    t, n, b = TILES[at["tile"]], PLACE.first_out[at["tile"]], PLACE.first_block[at["tile"]]
                    acc = bank_of(n)[:, c0:c1]
                    for k in range(t.k):
                        wait_unit((b + k) // UNIT)
                        slot, i = (b + k) // UNIT % SPLIT, (b + k) % UNIT
                        wh, wl = w_hi[:, slot, i * P:(i + 1) * P], w_lo[:, slot, i * P:(i + 1) * P]
                        if late and late[1] == k:
                            E.need(late[0])
                        if fresh and i_tile == 0:
                            E.need(fresh)
                        nc.tensor.matmul(acc, wh, x_hi[:, k, c0:c1], start=k == 0, stop=False)
                        nc.tensor.matmul(acc, wh, x_lo[:, k, c0:c1], start=False, stop=False)
                        last = nc.tensor.matmul(acc, wl, x_hi[:, k, c0:c1], start=False, stop=k == t.k - 1)
                        if k == t.k - 1:
                            last.then_inc(tile_done, 1)
                        elif i == UNIT - 1:
                            last.then_inc(unit_used, 1)
                    at["tile"] += 1

            def values(first, count=1):
                for _ in range(count):
                    t, n, b = TILES[at["tile"]], PLACE.first_out[at["tile"]], PLACE.first_block[at["tile"]]
                    for i in range(PLACE.outs[at["tile"]]):
                        acc = bank_of(n + i)[:, 0:2 * P]
                        c = first + i * P
                        for k in range(t.k):
                            u, j = (b + 2 * k) // UNIT, (b + 2 * k) % UNIT
                            wait_unit(u)
                            wh, wl = w_hi[:, u % SPLIT, j * P:(j + 2) * P], w_lo[:, u % SPLIT, j * P:(j + 2) * P]
                            nc.tensor.matmul(acc, h_hi[:, k, c:c + P], wh, start=k == 0, stop=False)
                            nc.tensor.matmul(acc, h_hi[:, k, c:c + P], wl, start=False, stop=False)
                            last = nc.tensor.matmul(acc, h_lo[:, k, c:c + P], wh, start=False, stop=k == t.k - 1)
                        last.then_inc(tile_done, 1)
                    at["tile"] += 1

            def row_sum(i, n, row, c0, c1, weights=ones):
                E.need(sq_ready)
                if i == 0:
                    if at["stat"]:
                        E.need(std_ready)
                    at["stat"] += 1
                last = nc.tensor.matmul(STAT[:, c0:c1], weights, row, start=i == 0, stop=i == n - 1)
                if i == n - 1:
                    last.then_inc(stat_ready, 1)

            def norm_sum(k, c0, c1):
                row_sum(k, KD, work[:, k, c0:c1], c0, c1)

            def norm_sums(c0, c1):
                for k in range(KD):
                    norm_sum(k, c0, c1)

            def projected(x_hi, x_lo, c0, c1, cols, fresh=None):
                for f in range(KD):
                    product(x_hi, x_lo, c0, c1, fresh=fresh if f == 0 else None)
                    if f >= 2:
                        norm_sum(f - 2, *cols)
                for f in range(KD - 2, KD):
                    norm_sum(f, *cols)

            def sum_modulation(l, place):
                for part in SUM_AT.get(place, []):
                    pe.wait_ge(ada_used, l * ADA_LAYER + KD * (part + 1))
                    for i in range(KD):
                        for s in range(2):
                            c = 2 * (KD * part + i) + s
                            acc = ada_acc[part % 2][s]
                            last = nc.tensor.matmul(X[2][:, c:c + 1], acc[:, i // 2, i % 2 * P:(i % 2 + 1) * P],
                                                    ones[:, 0:1], start=True, stop=True)
                    last.then_inc(ada_summed, 1)

            pe.wait_ge(cst_loaded, 16)
            c0, c1 = LAT
            for l in range(DEPTH):
                norm_sums(c0, c1)
                if l:
                    sum_modulation(l - 1, "mix_pre")
                outs = {}
                for step, i in MIX1:
                    if step in ("g", "r", "c", "rg", "gr"):
                        n = {"g": 5, "r": 2, "c": 3, "rg": RH, "gr": GH}[step]
                        product(h_hi, h_lo, c0, c1, n, fresh=h_ready if step == "g" else None)
                    elif step in ("rv", "gv"):
                        values(c0)
                    elif step == "diag" or step == "take":
                        if step == "take":
                            E.need(lev_rows)
                            E.need(lev_taken)
                        else:
                            pe.wait_ge(tile_out, outs["g"])
                            if l:
                                pe.wait_ge(mod_ready, l)
                        for h in range(GH):
                            rows = slice(GK * (h % 2), GK * (h % 2) + GK)
                            q = gqk[rows, 0, h // 2, :] if step == "diag" else q_dec[rows, h // 2, :]
                            k = gqk[rows, 1, h // 2, :] if step == "diag" else k_dec[rows, h // 2, :]
                            bank = X[1 + h % 2]
                            if step == "take" and i == 0:
                                last = nc.tensor.matmul(bank[:, h // 2 * P:(h // 2 + 1) * P], k[:, 0:P], q[:, P:SEQ],
                                                        start=True, stop=True)
                                continue
                            for j in range(2):
                                c = (h // 2 * 2 + j) * P
                                last = nc.tensor.matmul(bank[:, c:c + P], k[:, j * P:(j + 1) * P],
                                                        q[:, j * P:(j + 1) * P], start=True, stop=True)
                        last.then_inc(lev_done, 1)
                    elif step == "logit":
                        for j in range(2):
                            last = nc.tensor.matmul(X[0][:, j * SEQ:(j + 1) * SEQ],
                                                    v_("gla_w_a2", l, j * P, P)[0:RANK, :], ga_t[:, :],
                                                    start=True, stop=True)
                        last.then_inc(logit_done, 1)
                    elif step == "rot":
                        pe.wait_ge(tile_out, outs["r", i])
                        if i == 0:
                            pe.wait_ge(logit_out, l + 1)
                        else:
                            E.need(qk_ready)
                        nc.tensor.matmul(X[0][:, :], c_("rot_ret"), rq_raw[:, i, :, :], start=True, stop=True)\
                            .then_inc(rot_done, 1)
                    elif step == "score":
                        q, k = rqk[:, i, 0, :], rqk[:, i, 1, :]
                        if i == 0:
                            E.need(qk_ready)
                        else:
                            pe.wait_ge(ret_a_ready, RH * l + i)
                        nc.tensor.matmul(X[3][:, 0:SEQ], k[:, 0:P], q, start=True, stop=True)
                        nc.tensor.matmul(X[3][:, SEQ:SEQ + P], k[:, P:SEQ], q[:, P:SEQ], start=True, stop=True)\
                            .then_inc(score_done, 1)
                    elif step == "mix":
                        pe.wait_ge(tile_out, outs["rv"])
                        pe.wait_ge(ret_a_ready, RH * l + i + 1)
                        if i:
                            pe.wait_ge(ret_o_out, RH * l + i)
                        o = X[4][:, 0:SEQ]
                        nc.tensor.matmul(o, rv[:, 0, i * P:(i + 1) * P], ret_a[:, 0:SEQ], start=True, stop=False)
                        nc.tensor.matmul(o[:, P:SEQ], rv[:, 1, i * P:(i + 1) * P], ret_a[:, SEQ:SEQ + P],
                                         start=False, stop=True).then_inc(ret_o_done, 1)
                    elif step == "mean":
                        pe.wait_ge(ret_o_out, RH * (l + 1))
                        for j in range(2):
                            nc.tensor.matmul(X[3 * j][:, :], ones, o_ret[:, 2 * j:2 * j + 2, :], start=True, stop=True)\
                                .then_inc(mean_done, 1)
                    elif step == "gout":
                        E.need(lev_taken)
                        pe.wait_ge(tile_out, outs["gv"])
                        for h in range(GH):
                            if h:
                                pe.wait_ge(gla_o_out, GH * l + h)
                            o = X[4][:, 0:SEQ]
                            nc.tensor.matmul(o, gv[:, 0, h * P:(h + 1) * P], g_acc[:, h, 0:2, :], start=True,
                                             stop=False)
                            nc.tensor.matmul(o[:, P:SEQ], gv[:, 1, h * P:(h + 1) * P], g_acc[:, h, 2, :],
                                             start=False, stop=True).then_inc(gla_o_done, 1)
                    elif step == "norm":
                        row_sum(0, 1, o_sq[:, i, :], 0, T2)
                    outs[step] = outs[step, i] = PLACE.first_out[at["tile"]]
                for b in range(3):
                    E.need(y_ready)
                    for f in range(KD):
                        product(h_hi, h_lo, c0, c1)
                        product(y1_hi[:, 4 * b:4 * b + 4, :], y1_lo[:, 4 * b:4 * b + 4, :], 0, SEQ)
                        if b == 0 and f in (1, 3):
                            row_sum(0, 1, o_sq[:, f // 2, :], 0, T2)
                projected(y1_hi, y1_lo, 0, SEQ, LAT, fresh=merged_ready)
                sum_modulation(l, "mix_post")
                norm_sums(c0, c1)
                sum_modulation(l, "ffn_pre")
                for t in range(NFF):
                    product(h_hi, h_lo, c0, c1, 2, fresh=None if t else h_ready)
                    sum_modulation(l, 3 * KD + t)
                projected(hid_hi, hid_lo, 0, SEQ, LAT, ff_ready)
                sum_modulation(l, "ffn_post")
                if l == DEPTH - 1:
                    sum_modulation(l, "mix_pre")

            for l in range(DEPTH):
                c0 = 0 if l < DEPTH - 1 else SEQ
                cols = slice(c0, T2)
                if l == 0:
                    norm_sums(0, T2)
                steps, before = att_steps(l), att_before(l)
                outs = {}
                for step, i in mixer2(l):
                    if step in ("c", "mq", "mo"):
                        product(h_hi, h_lo, c0, T2, 2, fresh=h_ready if (step, i) == ("c", 0) else None)
                    elif step in ("q", "gate"):
                        product(h_hi, h_lo, c0, T2)
                    elif step in ("k", "v", "mg"):
                        product(h_hi, h_lo, 0, T2)
                    elif step == "mk":
                        product(h_hi, h_lo, 0, T2, 2)
                    elif step == "mv":
                        values(0)
                    elif step == "branch":
                        b, f = i
                        if f == 0 and b == 1:
                            pe.wait_ge(a_o_out, att_before(l + 1) // 2)
                        late = (y_ready, (0, 0, KD - 2)[b]) if f == 0 and b != 1 else None
                        rows = slice(4 * b, 4 * b + 4) if b < 2 else slice(0, KD)
                        product(y2_hi[:, rows, :], y2_lo[:, rows, :], c0, T2, late=late)
                    elif step == "qsq":
                        a = c0 if i < AG else 0
                        row_sum(0, 1, a_sq[:, a:T2], a, T2, c_("one64"))
                    elif step == "qrot":
                        pe.wait_ge(aq_scaled, (AG + 1) * l + i + 1)
                        if i >= 2:
                            pe.wait_ge(aq_ready, (AG + 1) * l + i - 1)
                        nc.tensor.matmul(X[i % 2][:, 0:SEQ], c_("rot_att"), aq[:, i, SEQ:T2], start=True, stop=True)\
                            .then_inc(aq_rot, 1)
                    elif step == "vturn":
                        pe.wait_ge(tile_out, outs["v", 0])
                        for t in range(4):
                            last = nc.tensor.transpose(X[2][:, t * P:(t + 1) * P], av_t[:, t * P:(t + 1) * P], ident)
                        last.then_inc(av_turned, 1)
                    elif step == "gturn":
                        pe.wait_ge(tile_out, outs["mg", 0])
                        for t in range(4):
                            last = nc.tensor.transpose(X[3][:, t * 16:(t + 1) * 16], mg_t[:, t * P:(t + 1) * P],
                                                       ident[0:16, 0:16])
                        last.then_inc(mg_turned, 1)
                    elif step == "gsum":
                        E.need(lsg_ready)
                        for t in range(4):
                            for d in range(2):
                                if d == 0:
                                    parts = [(j, "ones") for j in range(t)] + [(t, "upto")]
                                elif t < 2:
                                    parts = [(j, "ones") for j in range(t + 1, 2)] + [(t, "from")]
                                else:
                                    parts = [(j, "ones") for j in (0, 1, *range(t + 1, 4))] + [(t, "from")]
                                for n, (j, name) in enumerate(parts):
                                    last = nc.tensor.matmul(X[4][:, (2 * t + d) * MH:(2 * t + d + 1) * MH], c_(name),
                                                            lsg[:, j, 8 * d + MH:8 * d + 2 * MH], start=n == 0,
                                                            stop=n == len(parts) - 1)
                        last.then_inc(fsum_done, 1)
                    elif step == "att":
                        if i == 0:
                            pe.wait_ge(aq_ready, (AG + 1) * (l + 1))
                            E.need(gcol_ready)
                            E.need(av_out)
                        if i < len(steps):
                            q, j, g, keys = steps[i]
                            rows = slice(AD * g, AD * g + AD)
                            if i >= 2:
                                pe.wait_ge(a_exp, before + i - 1)
                            nc.tensor.matmul(X[i % 2][:, 0:keys], aq[rows, j, q * P:(q + 1) * P], aq[rows, AG, 0:keys],
                                             start=True, stop=True).then_inc(a_score, 1)
                        if 1 <= i <= len(steps):
                            keys = steps[i - 1][3]
                            E.need(a_prob)
                            for t in range(keys // P):
                                last = nc.tensor.transpose(X[2 + (i - 1) % 2][:, t * P:(t + 1) * P],
                                                           p_sb[:, (i - 1) % 2, t * P:(t + 1) * P], ident)
                            last.then_inc(a_turned, 1)
                        if i >= 2:
                            q, j, g, keys = steps[i - 2]
                            E.need(a_pt)
                            if g == 0 and i > 2:
                                pe.wait_ge(a_o_out, (before + i - 2) // 2)
                            for t in range(keys // P):
                                last = nc.tensor.matmul(X[4][AD * g:AD * g + AD, 0:P], av[:, t, AD * g:AD * g + AD],
                                                        pt_sb[:, i % 2, t * P:(t + 1) * P], start=t == 0,
                                                        stop=t == keys // P - 1)
                            last.then_inc(a_o_done, 1)
                    elif (step, i) == ("ln", 0):
                        E.need(cy_ready)
                        E.need(std_ready)
                        at["stat"] = 0
                        for t in range(4):
                            last = nc.tensor.matmul(STAT[:, cols], ones, cy[:, t, cols], start=t == 0, stop=t == 3)
                        last.then_inc(mean_done, 1)
                    elif (step, i) == ("ln", 1):
                        for t in range(4):
                            row_sum(t, 4, cin[:, t // 2, t % 2, cols], c0, T2)
                    elif step == "rows":
                        pe.wait_ge(a_exp, att_before(l + 1))
                        pe.wait_ge(a_o_out, att_before(l + 1) // 2)
                        for d in range(2):
                            for t in range(4):
                                nc.tensor.transpose(X[2 + d][0:MH, t * P:(t + 1) * P], gcol[:, t, d, :], ident)
                                last = nc.tensor.transpose(X[4 * d][0:MH, t * P:(t + 1) * P], fsum[:, t, d, :], ident)
                        last.then_inc(rows_turned, 1)
                    elif step == "mscore":
                        n_head = l * MH + i
                        if i == 0:
                            E.need(rows_ready)
                        else:
                            pe.wait_ge(m_taken, 2 * n_head)
                        pe.wait_ge(tile_out, outs["mk", i])
                        for t in range(4):
                            if t >= 2:
                                pe.wait_ge(m_score_out, 4 * n_head + t - 1)
                            for j in range(2):
                                last = nc.tensor.matmul(X[t % 2][:, cols], mqk[:, 2 + j, t * P:(t + 1) * P],
                                                        mqk[:, j, cols], start=j == 0, stop=j == 1)
                            last.then_inc(m_score, 1)
                    elif step == "mmax":
                        h, d = i
                        n_head = l * MH + h
                        head = c_("head_row")[0:MH, h * P:(h + 1) * P]
                        if h or d:
                            pe.wait_ge(w_arg, 8 * n_head + 4 * d)
                        nc.tensor.matmul(X[2][:, cols], head, mx_row[:, d, cols], start=True, stop=True)\
                            .then_inc(mx_done, 1)
                        if h or d:
                            pe.wait_ge(em_out, 2 * n_head + d)
                        nc.tensor.matmul(X[4][:, cols], head, g_row[:, d, cols], start=True, stop=True)\
                            .then_inc(em_in, 1)
                    elif step == "acc":
                        h, d, n = i
                        n_head = l * MH + h
                        if n == 0 and d == 0:
                            pe.wait_ge(tile_out, outs["mv", h])
                            pe.wait_ge(m_score_out, 4 * n_head + 4)
                        elif n == 0:
                            pe.wait_ge(m_taken, 2 * n_head + 1)
                        E.need(w_ready)
                        t = ORDER[d][n]
                        for j in range(3):
                            acc = X[3] if j == 0 else X[j - 1]
                            for a, b in spans(d, t, c0)[0]:
                                w = wgt[:, (8 * n_head + 4 * d + n) % 3, a:b]
                                left = ones if j == 0 else mv[:, t, (j - 1) * P:j * P]
                                last = nc.tensor.matmul(acc[:, a:b], left, w, start=n == 0, stop=n == 3,
                                                        skip_group_check=True)
                        last.then_inc(m_acc, 1)
                    elif step == "hsq":
                        for j in range(2):
                            row_sum(j, 2, s_sb[:, j, cols], c0, T2)
                    outs[step, i] = PLACE.first_out[at["tile"]]
                projected(h_hi, h_lo, c0, T2, (c0, T2), fresh=merged_ready)
                for half in range(2):
                    product(h_hi, h_lo, c0, T2, 2 * FF_HALF, fresh=None if half else h_ready)
                    if half == 0 or l == DEPTH - 1:
                        product(hid2_hi, hid2_lo, c0, T2, KD, fresh=ff2_ready)
                    else:
                        projected(hid2_hi, hid2_lo, c0, T2, (0, T2), fresh=ff2_ready)

        @block.scalar
        def _(act):
            E = Expect(act)
            C = Chain(act, act_chain)
            at = {"tile": 0, "unit": 0}

            def split_through(u):
                while at["unit"] <= min(u, N_UNITS - 1):
                    n = at["unit"]
                    act.wait_ge(raw_loaded[n % RAW], 16 * (n // RAW + 1))
                    if n >= SPLIT:
                        kind, count = PLACE.free[n - SPLIT]
                        act.wait_ge(tile_done if kind == "tile" else unit_used, count)
                    nc.scalar.activation(w_hi[:, n % SPLIT, :], raw[:, n % RAW, :], ACT.Copy).then_inc(hi_ready, 1)
                    at["unit"] += 1

            def next_tile():
                i = at["tile"]
                first, t = PLACE.first_block[i], TILES[i]
                split_through(max((first + t.k * t.wide - 1) // UNIT, first // UNIT + SPLIT - 1))
                at["tile"] += 1
                return PLACE.first_out[i]

            def take(dst, c0, c1, func=ACT.Copy, scale=1.0, bias=0.0):
                n = next_tile()
                E.need(tile_done)
                src = LIN[n % len(LIN)][:dst.shape[0], c0:c1]
                if len(dst.shape) == 3:
                    src = src.rearrange("p (s n) -> p s n", n=SEQ)
                nc.scalar.activation(dst, src, func, bias=bias, scale=scale).then_inc(tile_out, 1)

            def take_values(dst, v):
                n = next_tile()
                for i in range(PLACE.outs[at["tile"] - 1]):
                    E.need(tile_done)
                    nc.scalar.activation(dst[:, i, v * 2 * P:(v + 1) * 2 * P], LIN[(n + i) % len(LIN)][:, 0:2 * P],
                                         ACT.Copy).then_inc(tile_out, 1)

            def square(k, src, c0, c1):
                nc.scalar.activation(work[:, k, c0:c1], src[:, k, c0:c1], ACT.Square).then_inc(sq_ready, 1)

            def squares_of_x(c0, c1, updated=True):
                for k in range(KD):
                    if updated:
                        E.need(x_ready)
                    square(k, xs, c0, c1)

            def root(c0, c1, n):
                nc.scalar.preload_act_table(ACT.Sqrt)
                E.need(stat_ready)
                nc.scalar.activation(sd[:, c0:c1], STAT[:, c0:c1], ACT.Sqrt, bias=eps[:, 0:1], scale=1.0 / n)\
                    .then_inc(std_ready, 1)

            def split_norm(c0, c1):
                for k in range(KD):
                    E.need(norm_rows)
                    nc.scalar.activation(h_hi[:, k, c0:c1], work[:, k, c0:c1], ACT.Copy).then_inc(hi_done, 1)

            def split_shifted(n, l, c0):
                for k in range(KD):
                    E.need(norm_rows)
                    for i in range(c0 // SEQ, 2):
                        part = slice(i * SEQ, (i + 1) * SEQ)
                        last = nc.scalar.activation(h_hi[:, k, part], work[:, k, part], ACT.Identity,
                                                    bias=mod[:, l, 3 * n * KD + k, i:i + 1])
                    last.then_inc(hi_done, 1)

            def take_rows(x0, x1):
                c0, c1 = LAT
                for f in range(KD + 1):
                    if f < KD:
                        take(mix[:, f, c0:c1], x0, x1)
                    if f:
                        act.wait_ge(tile_out, E.seen[tile_done.name] - (f < KD))
                        square(f - 1, mix, c0, c1)

            def take_update(c0, c1, next_norm):
                for f in range(KD + 1):
                    if f < KD:
                        take(mix[:, f, c0:c1], c0, c1)
                    if f and next_norm:
                        E.need(x_ready)
                        square(f - 1, xs, c0, c1)

            E.need(eps_ready)
            def load_modulation(unit, l):
                if unit < (l + 1) * ADA_LAYER:
                    if unit >= ADA_SLOTS:
                        act.wait_ge(ada_used, unit - ADA_SLOTS + 1)
                    act.dma_start(ada_raw[unit % ADA_SLOTS], stream[unit].rearrange("p (a n) -> p a n", n=SEQ))\
                        .then_inc(ada_loaded[unit % ADA_SLOTS], 16)

            def load_at(l, place):
                for step in ADA_AT[place]:
                    load_modulation(l * ADA_LAYER + step + 2, l)

            act.wait_ge(x_loaded, 16)
            c0, c1 = LAT
            for l in range(DEPTH):
                squares_of_x(c0, c1, updated=l > 0)
                split_through(SPLIT - 1)
                root(c0, c1, D)
                split_norm(c0, c1)

                def split_y(b, rows):
                    E.need(y_rows)
                    nc.scalar.activation(y1_hi[:, b, :], rows, ACT.Copy).then_inc(y_hi_done, 1)

                def square_heads(o, i):
                    nc.scalar.activation(o_sq[:, i, :], o[:, 2 * i:2 * i + 2, :], ACT.Square).then_inc(sq_ready, 1)

                for step, i in MIX1:
                    if step == "g":
                        for j in range(2):
                            take(gqk[:, 0, j, :], c0, c1, scale=GK ** -0.5)
                            take(gqk[:, 1, j, :], c0, c1)
                        take(ga_t[:, :], c0, c1)
                    elif step == "r":
                        take(rq_raw[:, i, 0, :], c0, c1, scale=RD ** -0.5)
                        take(rq_raw[:, i, 1, :], c0, c1)
                    elif step == "rv":
                        take_values(rv, i)
                    elif step == "gv":
                        take_values(gv, i)
                    elif step == "c":
                        if i >= 2:
                            act.wait_ge(conv_used, 4 * l + i - 1)
                        for j in range(3):
                            take(conv_in[:, i % 2, j, :], c0, c1)
                    elif step == "rg":
                        for j in range(RH):
                            take(silu_r[:, j, :], c0, c1, ACT.Silu)
                    elif step == "gr":
                        for j in range(GH):
                            take(silu_g[:, j, :], c0, c1, ACT.Silu)
                    elif step == "logit":
                        act.wait_ge(vec_loaded, 16)
                        E.need(logit_done)
                        for j in range(2):
                            last = nc.scalar.activation(logit[:, j, :], X[0][:, j * SEQ:(j + 1) * SEQ], ACT.Identity,
                                                        bias=v_("gla_b_a", l, j))
                        last.then_inc(logit_out, 1)
                        act.wait_ge(logit_out, l + 1)
                        C.do(nc.scalar.activation(gdec[:, :, :], logit[:, :, :], ACT.Abs))
                        C.settle()
                        C.do(nc.scalar.activation(gdec[:, :, :], gdec[:, :, :], ACT.Exp, scale=-1.0))
                        C.settle()
                        nc.scalar.activation(gdec[:, :, :], gdec[:, :, :], ACT.Ln, bias=1.0).then_inc(logit_ln, 1)
                        if l == 0:
                            E.need(trig_args)
                            nc.scalar.activation(sin1[:, :], ang[:, :], ACT.Sin)
                            nc.scalar.activation(cos1[:, :], ang2[:, :], ACT.Sin).then_inc(trig_done, 1)
                            at_c = VEC["c"][0]
                            nc.scalar.activation(silu_c[:, :, :], vec[:, at_c:at_c + 2 * KD], ACT.Silu)\
                                .then_inc(silu_c_ready, 1)
                    elif step == "diff":
                        E.need(lev_diff)
                        C.do(nc.scalar.activation(gdec[:, :, :], gdec[:, :, :], ACT.Abs))
                        C.settle()
                        nc.scalar.activation(gdec[:, :, :], gdec[:, :, :], ACT.Exp, scale=-1.0 / GTAU)\
                            .then_inc(lev_exp, 1)
                    elif step == "mix":
                        E.need(ret_o_done)
                        nc.scalar.activation(o_ret[:, i, :], X[4][:, 0:SEQ], ACT.Copy).then_inc(ret_o_out, 1)
                    elif step == "gout":
                        for h in range(GH):
                            E.need(gla_o_done)
                            nc.scalar.activation(o_gla[:, h, :], X[4][:, 0:SEQ], ACT.Copy).then_inc(gla_o_out, 1)
                    elif step == "norm":
                        E.need(centred)
                        square_heads(o_ret, i)
                        root(0, T2, RD)
                    elif step == "split":
                        for j in range(2):
                            split_y(4 + 2 * i + j, o_ret[:, 2 * i + j, :])
                for i in range(2):
                    load_modulation(l * ADA_LAYER + i, l)
                act.wait_ge(gla_o_out, GH * (l + 1))
                def merged(f):
                    E.need(merged_rows)
                    nc.scalar.activation(y1_hi[:, f, :], mix[:, f, c0:c1], ACT.Copy).then_inc(merged_hi, 1)

                for b in range(3):
                    for f in range(KD):
                        if b or f >= 2:
                            act.wait_ge(merge_used, 3 * KD * l + KD * b + f - 1)
                        take(gate1[:, f % 2, :], c0, c1, ACT.Tanh, scale=0.5)
                        take(branch1[:, f % 2, :], 0, SEQ, scale=0.5)
                        if b == 2 and f:
                            merged(f - 1)
                        if b == 0 and f == 0:
                            for j in range(2, RH):
                                split_y(4 + j, o_ret[:, j, :])
                            square_heads(o_gla, 0)
                        if b == 0 and f in (1, 3):
                            root(0, T2, GV)
                            if f == 1:
                                square_heads(o_gla, 1)
                        elif b == 0 and f in (2, 4):
                            for j in range(2):
                                split_y(8 + f - 2 + j, o_gla[:, f - 2 + j, :])
                        load_at(l, KD * b + f)
                merged(KD - 1)
                take_rows(0, SEQ)
                root(c0, c1, D)
                squares_of_x(c0, c1)
                root(c0, c1, D)
                split_norm(c0, c1)
                for t in range(NFF):
                    take(ff_g[:, t % 2, :], c0, c1, ACT.Silu)
                    take(ff_u[:, t % 2, :], c0, c1)
                    if t >= 1:
                        E.need(ff_rows)
                        nc.scalar.activation(hid_hi[:, t - 1, :], ff_p[:, (t - 1) % 2, :], ACT.Copy).then_inc(ff_hi, 1)
                    load_at(l, 3 * KD + t)
                E.need(ff_rows)
                nc.scalar.activation(hid_hi[:, NFF - 1, :], ff_p[:, (NFF - 1) % 2, :], ACT.Copy).then_inc(ff_hi, 1)
                take_rows(0, SEQ)
                root(c0, c1, D)

            act.wait_ge(mod_ready, DEPTH)
            act.wait_ge(ctx_loaded, 16)
            act.wait_ge(half_ready, 1)
            for l in range(DEPTH):
                c0 = 0 if l < DEPTH - 1 else SEQ
                cols = slice(c0, T2)
                if l == 0:
                    squares_of_x(0, T2)
                root(0, T2, D)
                split_shifted(0, l, 0)
                steps, before = att_steps(l), att_before(l)
                outs = {}
                for step, i in mixer2(l):
                    if step == "c":
                        if i >= 2:
                            act.wait_ge(cin_used, 4 * l + i - 1)
                        take(cin[:, i % 2, 0, cols], c0, T2, scale=0.5)
                        take(cin[:, i % 2, 1, cols], c0, T2, ACT.Tanh, scale=0.5)
                    elif step == "q":
                        take(aq[:, i, cols], c0, T2)
                    elif step == "k":
                        take(aq[:, AG, :], 0, T2)
                    elif step == "v":
                        take(av_t[:, :], 0, T2)
                    elif step == "mg":
                        take(mg_t[:, :], 0, T2)
                    elif step == "mq":
                        for j in range(2):
                            take(mqk[:, j, cols], c0, T2)
                    elif step == "mk":
                        for j in range(2):
                            take(mqk[:, 2 + j, :], 0, T2, scale=MD ** -0.5)
                    elif step == "mv":
                        take_values(mv, 0)
                    elif step == "mo":
                        for j in range(2):
                            take(smo[:, j, cols], c0, T2, ACT.Tanh, scale=0.5)
                    elif step == "gate":
                        b, f = i
                        n = KD * (3 * l + b) + f
                        if b or f >= EARLY:
                            act.wait_ge(merge2_used, n - 1)
                        i_bias = (0, 2, 1)[b] * KD + f
                        take(gate_rows(b, f)[:, cols], c0, T2, ACT.Tanh, scale=0.5, bias=half_b[:, l, i_bias:i_bias + 1])
                    elif step == "branch":
                        b, f = i
                        n = KD * (3 * l + b) + f
                        if n >= 2:
                            act.wait_ge(merge2_used, n - 1)
                        take(branch_sb[:, f % 2, cols], c0, T2, scale=0.5)
                    elif step == "qsq":
                        a = c0 if i < AG else 0
                        act.wait_ge(tile_out, outs["q", i] if i < AG else outs["k", 0])
                        nc.scalar.activation(a_sq[:, a:T2], aq[:, i, a:T2], ACT.Square).then_inc(sq_ready, 1)
                        if i:
                            act.wait_ge(aq_scaled, (AG + 1) * l + i)
                        root(a, T2, AD)
                    elif step == "vturn":
                        E.need(av_turned)
                        nc.scalar.activation(av[:, :, :], X[2][:, :].rearrange("p (t n) -> p t n", n=P), ACT.Copy)\
                            .then_inc(av_out, 1)
                    elif step == "gturn":
                        E.need(pre_ready)
                        C.do(nc.scalar.activation(lsg[:, :, :], pre[:, :, :], ACT.Abs))
                        C.settle()
                        C.do(nc.scalar.activation(lsg[:, :, :], lsg[:, :, :], ACT.Exp, scale=-1.0))
                        C.settle()
                        nc.scalar.activation(lsg[:, :, :], lsg[:, :, :], ACT.Ln, bias=1.0).then_inc(lsg_ln, 1)
                    elif step == "att":
                        if i < len(steps):
                            keys = steps[i][3]
                            E.need(a_neg)
                            nc.scalar.activation(p_sb[:, i % 2, 0:keys], X[i % 2][:, 0:keys], ACT.Exp,
                                                 bias=a_stat[:, i % 2, 1:2], scale=AD ** -0.5,
                                                 accum_out=a_stat[:, i % 2, 2:3]).then_inc(a_exp, 1)
                        if 1 <= i <= len(steps):
                            keys, b = steps[i - 1][3], (i - 1) % 2
                            E.need(a_turned)
                            if i > 2:
                                act.wait_ge(a_o_done, before + i - 2)
                            nc.scalar.activation(pt_sb[:, b, 0:keys], X[2 + b][:, 0:keys], ACT.Copy).then_inc(a_pt, 1)
                        if i >= 2 and steps[i - 2][2] == 1:
                            q, j, _, _ = steps[i - 2]
                            act.wait_ge(a_o_done, before + i - 1)
                            nc.scalar.activation(y2_hi[:, 4 + j, q * P:(q + 1) * P], X[4][:, 0:P], ACT.Copy)\
                                .then_inc(a_o_hi, 1)
                    elif (step, i) == ("ln", 0):
                        E.need(centred)
                        for t in range(4):
                            nc.scalar.activation(cin[:, t // 2, t % 2, cols], cy[:, t, cols], ACT.Square)\
                                .then_inc(sq_ready, 1)
                    elif (step, i) == ("ln", 1):
                        act.wait_ge(aq_scaled, (AG + 1) * (l + 1))
                        root(c0, T2, CONV)
                    elif (step, i) == ("ln", 2):
                        for t in range(4):
                            E.need(ln_rows)
                            C.do(nc.scalar.activation(cy[:, t, cols], cy[:, t, cols], ACT.Silu,
                                                      bias=v_("conv_ln_b_2", l, t), scale=v_("conv_ln_w_2", l, t)))
                    elif (step, i) == ("ln", 3):
                        C.settle()
                        for t in range(4):
                            nc.scalar.activation(y2_hi[:, t, cols], cy[:, t, cols], ACT.Copy).then_inc(y_hi_done, 1)
                    elif step == "mscore":
                        for t in range(4):
                            E.need(m_score)
                            nc.scalar.activation(s_sb[:, t, cols], X[t % 2][:, cols], ACT.Copy).then_inc(m_score_out, 1)
                    elif step == "em":
                        h, d = i
                        E.need(em_in)
                        if d:
                            act.wait_ge(m_taken, 2 * (l * MH + h) + 1)
                        nc.scalar.activation(em[:, cols], X[4][:, cols], ACT.Exp, scale=-1.0).then_inc(em_out, 1)
                    elif step == "warg":
                        h, d, n = i
                        E.need(w_arg)
                        a, b = hull(spans(d, ORDER[d][n], c0)[0])
                        w = wgt[:, (8 * (l * MH + h) + 4 * d + n) % 3, a:b]
                        nc.scalar.activation(w, w, ACT.Exp, scale=-1.0).then_inc(w_exp, 1)
                    elif step == "hsq":
                        E.need(head_done)
                        for j in range(2):
                            nc.scalar.activation(s_sb[:, j, cols], hacc[:, j, cols], ACT.Square).then_inc(sq_ready, 1)
                        root(c0, T2, MD)
                    elif step == "hout":
                        for j in range(2):
                            E.need(y_rows)
                            nc.scalar.activation(y2_hi[:, 2 * i + j, cols], hacc[:, j, cols], ACT.Copy)\
                                .then_inc(y_hi_done, 1)
                    outs[step, i] = E.seen.get(tile_done.name, 0)
                act.wait_ge(tile_done, outs["gate", (2, KD - 1)])
                for f in range(KD):
                    E.need(merged_rows)
                    nc.scalar.activation(h_hi[:, f, cols], mix[:, f, cols], ACT.Copy).then_inc(merged_hi, 1)
                take_update(c0, T2, True)
                root(c0, T2, D)
                split_shifted(1, l, c0)
                E.need(up_zero)
                first = c0 // SEQ
                for half in range(2):
                    n0 = NFF * l + FF_HALF * half
                    for t in range(FF_HALF + 2):
                        if t < FF_HALF:
                            if t >= 2:
                                act.wait_ge(fc_rows, n0 + t - 1)
                            for j in range(2):
                                take(up[:, t % 2, j, first:2, 1:SEQ + 1], c0, T2)
                        if 1 <= t <= FF_HALF:
                            E.need(fc_rows)
                            g = fc[:, (t - 1) % 2, 1, cols]
                            nc.scalar.activation(g, g, ACT.Silu).then_inc(fc_gate, 1)
                        if t >= 2:
                            E.need(ff2_rows)
                            nc.scalar.activation(hid2_hi[:, t - 2, cols], fh[:, t % 2, cols], ACT.Copy).then_inc(ff2_hi, 1)
                    take_update(c0, T2, half == 1 and l < DEPTH - 1)

        @block.vector
        def _(dve):
            E = Expect(dve)
            C = Chain(dve, dve_chain)
            V = nc.vector
            MUL, ADD, SUB = ALU.mult, ALU.add, ALU.subtract

            def inverse_root(c0, c1):
                E.need(std_ready)
                C.do(V.reciprocal(sd[:, c0:c1], sd[:, c0:c1]))
                C.settle()

            def norm1(name, l):
                c0, c1 = LAT
                inverse_root(c0, c1)
                for k in range(KD + 2):
                    if k < KD:
                        V.scalar_tensor_tensor(work[:, k, c0:c1], xs[:, k, c0:c1], v_(name, l, k), sd[:, c0:c1],
                                               MUL, MUL).then_inc(norm_rows, 1)
                    if k >= 2:
                        E.need(hi_done)
                        V.tensor_tensor(h_lo[:, k - 2, c0:c1], work[:, k - 2, c0:c1], h_hi[:, k - 2, c0:c1], SUB)\
                            .then_inc(h_ready, 1)

            def add_normed(name, l):
                c0, c1 = LAT
                inverse_root(c0, c1)
                written = []
                for k in range(KD + 1):
                    if k < KD:
                        written.append(C.do(V.scalar_tensor_tensor(work[:, k, c0:c1], mix[:, k, c0:c1], v_(name, l, k),
                                                                   sd[:, c0:c1], MUL, MUL)))
                    if k:
                        C.settle(written[k - 1])
                        V.tensor_tensor(xs[:, k - 1, c0:c1], xs[:, k - 1, c0:c1], work[:, k - 1, c0:c1], ADD)\
                            .then_inc(x_ready, 1)

            V.memset(eps[:, :], EPS).then_inc(eps_ready, 1)

            def rotation_angles():
                C.do(V.tensor_copy(ang[:, :], pos_i[:, :]))
                C.settle()
                C.do(V.tensor_scalar(ang[:, :], ang[:, :], c_("inv_freq"), None, MUL))
                C.settle()
                ROUND = 1.5 * 2.0 ** 23
                T1 = 6.28125
                T2_ = 0.0019350051879882812
                T3 = 2 * np.pi - T1 - T2_
                for dst, quarter in ((ang2, 0.25), (ang, 0.0)):
                    C.do(V.tensor_scalar(turns[:, :], ang[:, :], float(1 / (2 * np.pi)), quarter, MUL, ADD))
                    C.settle()
                    C.do(V.tensor_scalar(turns[:, :], turns[:, :], ROUND, ROUND, ADD, SUB))
                    C.settle()
                    src = ang
                    for part in (T1, T2_, T3):
                        C.do(V.scalar_tensor_tensor(dst[:, :], turns[:, :], -float(part), src[:, :], MUL, ADD))
                        C.settle()
                        src = dst
                    if quarter:
                        C.do(V.tensor_scalar(dst[:, :], dst[:, :], float(np.pi / 2), None, ADD))
                        C.settle()
                    last = V.tensor_scalar(dst[:, :], dst[:, :], 3.1415925, -3.1415925, ALU.min, ALU.max)
                    if quarter:
                        C.do(last)
                last.then_inc(trig_args, 1)

            summed = {}

            def add_modulation(l, step):
                unit = l * ADA_LAYER + step
                k = step % KD
                dve.wait_ge(ada_loaded[unit % ADA_SLOTS], 16 * (unit // ADA_SLOTS + 1))
                if k == 0 and unit >= 2 * KD:
                    dve.wait_ge(ada_summed, unit // KD - 1)
                for s in range(2):
                    acc, c = ada_acc[step // KD % 2][s], silu_c[:, k, s:s + 1]
                    if k == 0:
                        last = V.tensor_scalar(acc, ada_raw[unit % ADA_SLOTS], c, None, MUL)
                    else:
                        C.settle(summed[0]) if s == 0 else dve.wait_ge(ada_used, unit)
                        last = V.scalar_tensor_tensor(acc, ada_raw[unit % ADA_SLOTS], c, acc, MUL, ADD)
                    if s == 0:
                        summed[0] = C.do(last)
                last.then_inc(ada_used, 1)


            def modulation(l):
                dve.wait_ge(ada_summed, MODS * (l + 1))
                V.tensor_tensor(mod[:, l, :, :], X[2][:, 0:2 * MODS * KD].rearrange("p (i s) -> p i s", s=2),
                                v_("ada_b_2", l, 0, MODS * KD).unsqueeze(2).to_broadcast([P, MODS * KD, 2]), ADD)\
                    .then_inc(mod_ready, 1)

            dve.wait_ge(x_loaded, 16)
            dve.wait_ge(vec_loaded, 16)
            c0, c1 = LAT
            for l in range(DEPTH):
                if l:
                    dve.wait_ge(x_ready, 2 * KD * l)
                norm1("norm_mix_pre", l)
                if l:
                    modulation(l - 1)
                both = [P, 2, SEQ]
                outs = {}

                def pairs(level):
                    return gmask[:, level, :].unsqueeze(1).unsqueeze(1).to_broadcast([P, 2, 2, P])

                def blocks_of(bank):
                    return bank[:, :].rearrange("p (h j n) -> p h j n", h=2, j=2)

                def head_norm(o, i, name):
                    inverse_root(0, T2)
                    for h in (2 * i, 2 * i + 1):
                        C.do(V.scalar_tensor_tensor(o[:, h, :], o[:, h, :], v_(name, l, h),
                                                    sd[:, h % 2 * SEQ:(h % 2 + 1) * SEQ], MUL, MUL))
                    C.settle()
                    for h in (2 * i, 2 * i + 1):
                        gate = (silu_r if o is o_ret else silu_g)[:, h, :]
                        V.tensor_tensor(o[:, h, :], o[:, h, :], gate, MUL).then_inc(y_rows, 1)

                def head_low(o, i, first):
                    for h in (2 * i, 2 * i + 1):
                        E.need(y_hi_done)
                        last = V.tensor_tensor(y1_lo[:, first + h, :], o[:, h, :], y1_hi[:, first + h, :], SUB)
                    if i:
                        last.then_inc(y_ready, 1)

                for step, i in MIX1:
                    if step in ("g", "r", "rv", "gv", "c", "rg", "gr"):
                        n = {"g": 5, "r": 2, "rv": 2, "gv": 2, "c": 3, "rg": RH, "gr": GH}[step]
                        outs[step] = outs[step, i] = E.later(tile_out, n)
                    elif step == "diag":
                        dve.wait_ge(tables_loaded, 16 * 3)
                        C.do(V.memset(g_acc[:, :, :, :], 0.0))
                        C.settle()
                        E.need(lev_done)
                        for odd in range(2):
                            last = V.copy_predicated(g_acc[:, odd::2, 0::2, :], pairs(len(GLA_LEVELS)),
                                                     blocks_of(X[1 + odd]))
                        last.then_inc(lev_taken, 1)
                        dve.wait_ge(lev_taken, N_LEV * l + 1)
                        if l == 0:
                            dve.wait_ge(cst_loaded, 16)
                            rotation_angles()
                    elif step == "rot":
                        dve.wait_ge(tile_out, outs["r", i])
                        if l == 0 and i == 0:
                            E.need(trig_done)
                        C.do(V.tensor_tensor(rqk[:, i, :, :], rq_raw[:, i, :, :],
                                             cos1[:, :].unsqueeze(1).to_broadcast(both), MUL))
                        E.need(rot_done)
                        C.settle()
                        C.do(V.tensor_tensor(rq_raw[:, i, :, :], X[0][:, :].rearrange("p (a n) -> p a n", a=2),
                                             sin1[:, :].unsqueeze(1).to_broadcast(both), MUL))
                        C.settle()
                        V.tensor_tensor(rqk[:, i, :, :], rqk[:, i, :, :], rq_raw[:, i, :, :], ADD).then_inc(qk_ready, 1)
                    elif step == "score":
                        E.need(score_done)
                        if i or l:
                            E.need(ret_o_done)
                        V.tensor_tensor(ret_a[:, :], X[3][:, 0:3 * P], dec[:, i, :], MUL).then_inc(ret_a_ready, 1)
                    elif step == "gates":
                        E.need(logit_out)
                        E.need(logit_ln)
                        C.do(V.tensor_scalar(logit[:, :, :], logit[:, :, :], 0.0, None, ALU.min))
                        C.settle()
                        C.do(V.tensor_tensor(logit[:, :, :], logit[:, :, :], gdec[:, :, :], SUB))
                        C.do(V.memset(k_dec[:, 0, :], 1.0))
                        C.settle()
                        for j in range(2):
                            C.do(V.tensor_tensor_scan(g_cum[:, j, :], k_dec[:, 0, :], logit[:, j, :], 0.0, MUL, ADD))
                        C.settle()
                    elif step == "diff":
                        m = ([P] + GLA_LEVELS)[i]
                        blocks = g_cum[:, :, :].rearrange("p a (b t) -> p (a b) t", t=2 * m)
                        middle = blocks[:, :, m - 1:m].to_broadcast([P, 2 * SEQ // (2 * m), 2 * m])
                        V.tensor_tensor(gdec[:, :, :].rearrange("p a (b t) -> p (a b) t", t=2 * m), blocks, middle, SUB)\
                            .then_inc(lev_diff, 1)
                    elif step == "rows":
                        E.need(lev_exp)
                        C.do(V.tensor_tensor(q_dec[:, :, :], gqk[:, 0, :, :], gdec[:, :, :], MUL))
                        V.tensor_tensor(k_dec[:, :, :], gqk[:, 1, :, :], gdec[:, :, :], MUL).then_inc(lev_rows, 1)
                        C.settle()
                        dve.wait_ge(lev_rows, (N_LEV - 1) * l + i + 1)
                    elif step == "take":
                        E.need(lev_done)
                        for odd in range(2):
                            if i == 0:
                                last = V.tensor_copy(g_acc[:, odd::2, 1, :],
                                                     X[1 + odd][:, 0:2 * P].rearrange("p (h n) -> p h n", n=P))
                            else:
                                last = V.copy_predicated(g_acc[:, odd::2, 0::2, :], pairs(i - 1), blocks_of(X[1 + odd]))
                        last.then_inc(lev_taken, 1)
                        dve.wait_ge(lev_taken, N_LEV * l + i + 2)
                    elif step == "conv":
                        if i == 0:
                            C.do(V.memset(zrow[:, 0:2], 0.0))
                        dve.wait_ge(tile_out, outs["c", i])
                        u, g, b = (conv_in[:, i % 2, j, :] for j in range(3))
                        C.do(V.tensor_tensor(zrow[:, 2:], u, g, MUL))
                        C.settle()
                        y = conv_y[:, i % 2, :]
                        C.do(V.tensor_scalar(y, zrow[:, 0:SEQ], v_("conv_w", l, i), None, MUL))
                        for j in (1, 2):
                            C.settle()
                            C.do(V.scalar_tensor_tensor(y, zrow[:, j:j + SEQ], v_("conv_w", l, 4 * j + i), y, MUL, ADD))
                        C.settle()
                        C.do(V.tensor_tensor(y, y, b, MUL))
                        C.settle()
                        V.tensor_copy(y1_hi[:, i, :], y).then_inc(conv_used, 1)
                        dve.wait_ge(conv_used, 4 * l + i + 1)
                        last = V.tensor_tensor(y1_lo[:, i, :], y, y1_hi[:, i, :], SUB)
                        if i < 3:
                            C.do(last)
                        else:
                            last.then_inc(y_ready, 1)
                    elif step == "mean":
                        for j in range(2):
                            E.need(mean_done)
                            two = o_ret[:, 2 * j:2 * j + 2, :]
                            V.scalar_tensor_tensor(two, X[3 * j][:, :].rearrange("p (a n) -> p a n", a=2), -1.0 / RD, two,
                                                   MUL, ADD).then_inc(centred, 1)
                        due = E.seen[mean_done.name]
                        dve.wait_ge(centred, due)
                    elif step == "norm":
                        dve.wait_ge(tile_out, outs["rg"])
                        head_norm(o_ret, i, "ret_gn_w")
                    elif step == "split":
                        head_low(o_ret, i, 4)
                dve.wait_ge(silu_c_ready, 1)

                def merged_low(f):
                    E.need(merged_hi)
                    V.tensor_tensor(y1_lo[:, f, :], mix[:, f, SEQ:T2], y1_hi[:, f, :], SUB).then_inc(merged_ready, 1)

                for b in range(3):
                    for f in range(KD):
                        E.need(tile_out, 2)
                        g, y, p = gate1[:, f % 2, :], branch1[:, f % 2, :], prod1[:, f % 2, :]
                        if b == 0:
                            V.scalar_tensor_tensor(mix[:, f, SEQ:T2], g, 1.0, y, ADD, MUL).then_inc(merge_used, 1)
                            if f == 0:
                                head_low(o_ret, 1, 4)
                            if f in (1, 3):
                                head_norm(o_gla, f // 2, "gla_gn_w")
                            elif f in (2, 4):
                                head_low(o_gla, f // 2 - 1, 8)
                        else:
                            V.scalar_tensor_tensor(p, g, 1.0, y, ADD, MUL).then_inc(merge_used, 1)
                            dve.wait_ge(merge_used, 3 * KD * l + KD * b + f + 1)
                            last = V.tensor_tensor(mix[:, f, SEQ:T2], mix[:, f, SEQ:T2], p, ADD)
                            if b == 2:
                                last.then_inc(merged_rows, 1)
                                if f:
                                    merged_low(f - 1)
                            else:
                                written = C.do(last)
                        for step in ADA_AT[KD * b + f]:
                            add_modulation(l, step)
                        if b == 1:
                            C.settle(written)
                merged_low(KD - 1)
                E.need(tile_out, KD)
                add_normed("norm_mix_post", l)
                dve.wait_ge(x_ready, KD * (2 * l + 1))
                norm1("norm_ffn_pre", l)
                for t in range(NFF):
                    E.need(tile_out, 2)
                    if t >= 2:
                        dve.wait_ge(ff_ready, NFF * l + t - 1)
                    V.tensor_tensor(ff_p[:, t % 2, :], ff_g[:, t % 2, :], ff_u[:, t % 2, :], MUL).then_inc(ff_rows, 1)
                    if t:
                        dve.wait_ge(ff_hi, NFF * l + t)
                        V.tensor_tensor(hid_lo[:, t - 1, :], ff_p[:, (t - 1) % 2, :], hid_hi[:, t - 1, :], SUB)\
                            .then_inc(ff_ready, 1)
                    for step in ADA_AT[3 * KD + t]:
                        add_modulation(l, step)
                dve.wait_ge(ff_hi, NFF * (l + 1))
                V.tensor_tensor(hid_lo[:, NFF - 1, :], ff_p[:, (NFF - 1) % 2, :], hid_hi[:, NFF - 1, :], SUB)\
                    .then_inc(ff_ready, 1)
                E.need(tile_out, KD)
                add_normed("norm_ffn_post", l)
            modulation(DEPTH - 1)
            dve.wait_ge(mod_ready, DEPTH)

            def norm2(n, l, c0):
                inverse_root(c0, T2)
                streams = [(i, slice(i * SEQ, (i + 1) * SEQ)) for i in range(c0 // SEQ, 2)]
                for k in range(KD + 2):
                    if k < KD:
                        for i, part in streams:
                            last = V.scalar_tensor_tensor(work[:, k, part], xs[:, k, part], gain[:, n, k, i:i + 1],
                                                          sd[:, part], MUL, MUL)
                        last.then_inc(norm_rows, 1)
                    if k >= 2:
                        E.need(hi_done)
                        for i, part in streams:
                            last = V.scalar_tensor_tensor(h_lo[:, k - 2, part], work[:, k - 2, part],
                                                          mod[:, l, 3 * n * KD + k - 2, i:i + 1], h_hi[:, k - 2, part],
                                                          ADD, SUB)
                        last.then_inc(h_ready, 1)

            def add_gated(part_of_mod, l, c0, signal):
                for f in range(KD):
                    E.need(tile_out)
                    for i in range(c0 // SEQ, 2):
                        part = slice(i * SEQ, (i + 1) * SEQ)
                        last = V.scalar_tensor_tensor(xs[:, f, part], mix[:, f, part],
                                                      mod[:, l, part_of_mod * KD + f, i:i + 1], xs[:, f, part], MUL, ADD)
                        if not signal:
                            C.do(last)
                    if signal:
                        last.then_inc(x_ready, 1)
                if not signal:
                    C.settle()
                else:
                    updates["x"] += KD
                    dve.wait_ge(x_ready, updates["x"])

            for l in range(DEPTH):
                C.do(V.tensor_scalar(half_b[:, l, :], v_("branch_gate_b_2", l, 0, 3 * KD), 0.5, None, MUL))
                last = V.tensor_scalar(half_w[:, l, :], v_("mlstm_norm_w_2", l, 0, KD), 0.5, None, MUL)
                if l < DEPTH - 1:
                    C.do(last)
            last.then_inc(half_ready, 1)
            dve.wait_ge(half_ready, 1)
            dve.wait_ge(ctx_loaded, 16)
            updates = {"x": 2 * KD * DEPTH}
            dve.wait_ge(x_ready, updates["x"])
            tapped = {}
            for l in range(DEPTH):
                c0 = 0 if l < DEPTH - 1 else SEQ
                cols = slice(c0, T2)
                first, ns = c0 // SEQ, 2 - c0 // SEQ
                for n in range(2):
                    C.do(V.scalar_tensor_tensor(gain[:, n, :, :], mod[:, l, (3 * n + 1) * KD:(3 * n + 2) * KD, :], 1.0,
                                                v_(("norm1_w_2", "norm2_w_2")[n], l, 0, KD).unsqueeze(2)
                                                .to_broadcast([P, KD, 2]), ADD, MUL))
                norm2(0, l, 0)
                if l:
                    dve.wait_ge(merge2_used, 3 * KD * l)
                C.do(V.memset(z2[:, :, :, :], 0.0))
                C.settle()

                def by_stream(rows):
                    return rows.rearrange("p (s n) -> p s n", n=SEQ)

                steps, before = att_steps(l), att_before(l)
                outs = {}
                COUNT = {"c": 2, "q": 1, "k": 1, "v": 1, "mg": 1, "mq": 2, "mk": 2, "mv": 4, "mo": 2, "gate": 1, "branch": 1}
                for step, i in mixer2(l):
                    if step in COUNT:
                        outs[step, i] = E.later(tile_out, COUNT[step])
                    elif step == "glu":
                        for j in range(2):
                            dve.wait_ge(tile_out, outs["c", i + j])
                            V.scalar_tensor_tensor(z2[:, j, first:2, PAD:PAD + SEQ], by_stream(cin[:, j, 1, cols]), 1.0,
                                                   by_stream(cin[:, j, 0, cols]), ADD, MUL).then_inc(cin_used, 1)
                        dve.wait_ge(cin_used, 4 * l + i + 2)
                    elif step == "taps":
                        pair, t0, t1 = i
                        for tap in range(t0, t1):
                            for j in range(2):
                                y = by_stream(cy[:, pair + j, cols])
                                z = z2[:, j, first:2, tap:tap + SEQ]
                                w = v_("conv_dw_w_2", l, 4 * tap + pair + j)
                                if tap == 0:
                                    C.do(V.tensor_scalar(y, z, w, v_("conv_dw_b_2", l, pair + j), MUL, ADD))
                                else:
                                    C.settle(tapped[j])
                                    C.do(V.scalar_tensor_tensor(y, z, w, y, MUL, ADD))
                                tapped[j] = C.n
                        if t1 == CONV_K:
                            C.settle()
                            if pair:
                                dve.sem_inc(cy_ready, 1)
                    elif step == "qscale":
                        a = c0 if i < AG else 0
                        inverse_root(a, T2)
                        V.scalar_tensor_tensor(aq[:, i, a:T2], aq[:, i, a:T2],
                                               v_("q_norm_w_2" if i < AG else "k_norm_w_2", l), sd[:, a:T2], MUL, MUL)\
                            .then_inc(aq_scaled, 1)
                    elif step == "qrot":
                        x = aq[:, i, SEQ:T2]
                        E.need(aq_rot)
                        dve.wait_ge(aq_scaled, (AG + 1) * l + i + 1)
                        C.do(V.tensor_tensor(a_rot[:, :], X[i % 2][:, 0:SEQ], c_("sin_ax"), MUL))
                        C.do(V.tensor_tensor(x, x, c_("cos_ax"), MUL))
                        C.settle()
                        V.tensor_tensor(x, x, a_rot[:, :], ADD).then_inc(aq_ready, 1)
                        dve.wait_ge(aq_ready, (AG + 1) * l + i + 1)
                    elif step == "gturn":
                        E.need(mg_turned)
                        V.tensor_tensor(pre[:, :, :], X[3][:, 0:64].rearrange("p (t g) -> p t g", g=16),
                                        v_("mlstm_gate_b_2", l, 0, 16).unsqueeze(1).to_broadcast([P, 4, 16]), ADD)\
                            .then_inc(pre_ready, 1)
                    elif step == "glsg":
                        E.need(lsg_ln)
                        dve.wait_ge(pre_ready, l + 1)
                        V.scalar_tensor_tensor(lsg[:, :, :], pre[:, :, :], 0.0, lsg[:, :, :], ALU.min, SUB)\
                            .then_inc(lsg_ready, 1)
                    elif step == "gsum":
                        E.need(fsum_done)
                        sums = X[4][:, 0:4 * 2 * MH].rearrange("p (t d h) -> p t d h", t=4, d=2)
                        C.do(V.tensor_copy(fsum[:, :, :, :], sums))
                        for d in range(2):
                            last = V.tensor_tensor(gcol[:, :, d, :], pre[:, :, 8 * d:8 * d + MH],
                                                   sums[:, :, d, :], SUB)
                        last.then_inc(gcol_ready, 1)
                    elif step == "rows":
                        E.need(rows_turned)
                        for d in range(2):
                            C.do(V.tensor_copy(g_row[:, d, :], X[2 + d][0:MH, :]))
                        C.settle()
                        C.do(V.tensor_tensor_scan(mx_row[:, 0, :], g_row[:, 0, :], g_row[:, 0, :], M_INIT,
                                                  ALU.max, ALU.max))
                        back = slice(SEQ - 1, None, -1)
                        C.do(V.tensor_tensor_scan(mx_row[:, 1, back], g_row[:, 1, back], g_row[:, 1, back], M_INIT,
                                                  ALU.max, ALU.max))
                        C.settle()
                        back = slice(T2 - 1, SEQ - 1, -1)
                        C.do(V.tensor_tensor_scan(mx_row[:, 1, back], g_row[:, 1, back], g_row[:, 1, back],
                                                  mx_row[:, 1, 0:1], ALU.max, ALU.max))
                        C.settle()
                        for d in range(2):
                            last = V.tensor_tensor(g_row[:, d, :], mx_row[:, d, :], X[4 * d][0:MH, :], ADD)
                            if d == 0:
                                C.do(last)
                        last.then_inc(rows_ready, 1)
                    elif step == "att":
                        if 1 <= i <= len(steps):
                            keys, b = steps[i - 1][3], (i - 1) % 2
                            E.need(a_exp)
                            C.do(V.reciprocal(a_stat[:, b, 3:4], a_stat[:, b, 2:3]))
                            C.settle()
                            V.tensor_scalar(p_sb[:, b, 0:keys], p_sb[:, b, 0:keys], a_stat[:, b, 3:4], None, MUL)\
                                .then_inc(a_prob, 1)
                        if i < len(steps):
                            keys, b = steps[i][3], i % 2
                            E.need(a_score)
                            C.do(V.reduce_max(a_stat[:, b, 0:1], X[b][:, 0:keys], AX_X))
                            C.settle()
                            V.tensor_scalar(a_stat[:, b, 1:2], a_stat[:, b, 0:1], -AD ** -0.5, None, MUL).then_inc(a_neg, 1)
                        if i >= 2 and steps[i - 2][2] == 1:
                            q, j, _, _ = steps[i - 2]
                            E.need(a_o_hi)
                            V.tensor_tensor(y2_lo[:, 4 + j, q * P:(q + 1) * P], X[4][:, 0:P],
                                            y2_hi[:, 4 + j, q * P:(q + 1) * P], SUB).then_inc(a_o_out, 1)
                    elif (step, i) == ("ln", 0):
                        E.need(mean_done)
                        for t in range(4):
                            last = V.scalar_tensor_tensor(cy[:, t, cols], STAT[:, cols], -1.0 / CONV, cy[:, t, cols],
                                                          MUL, ADD)
                        last.then_inc(centred, 1)
                        dve.wait_ge(centred, 2 * DEPTH + l + 1)
                    elif (step, i) == ("ln", 2):
                        inverse_root(c0, T2)
                        for t in range(4):
                            V.tensor_tensor(cy[:, t, cols], cy[:, t, cols], sd[:, cols], MUL).then_inc(ln_rows, 1)
                    elif (step, i) == ("ln", 3):
                        for t in range(4):
                            E.need(y_hi_done)
                            last = V.tensor_tensor(y2_lo[:, t, cols], cy[:, t, cols], y2_hi[:, t, cols], SUB)
                        last.then_inc(y_ready, 1)
                    elif step == "merge":
                        b, f = i
                        dve.wait_ge(tile_out, outs["branch", i])
                        g, y = gate_rows(b, f)[:, cols], branch_sb[:, f % 2, cols]
                        if b == 0:
                            V.scalar_tensor_tensor(mix[:, f, cols], g, 1.0, y, ADD, MUL).then_inc(merge2_used, 1)
                            continue
                        n = C.do(V.scalar_tensor_tensor(y, g, 1.0, y, ADD, MUL))
                        C.settle(n)
                        dve.wait_ge(merge2_used, KD * (3 * l + b - 1) + f + 1)
                        V.tensor_tensor(mix[:, f, cols], mix[:, f, cols], y, ADD).then_inc(merge2_used, 1)
                        if b == 2:
                            dve.wait_ge(merge2_used, KD * (3 * l + b) + f + 1)
                            dve.sem_inc(merged_rows, 1)
                    elif step == "warg":
                        h, d, n = i
                        if n == 0:
                            E.need(mx_done)
                        t, m = ORDER[d][n], 8 * (l * MH + h) + 4 * d + n
                        a, b = hull(spans(d, t, c0)[0])
                        if m >= 3:
                            dve.wait_ge(m_acc, m - 2)
                        V.tensor_scalar(wgt[:, m % 3, a:b], X[2][:, a:b], gcol[:, t, d, h:h + 1], 0.0, SUB, ALU.max)\
                            .then_inc(w_arg, 1)
                    elif step == "wmul":
                        h, d, n = i
                        n_head = l * MH + h
                        t, m = ORDER[d][n], 8 * n_head + 4 * d + n
                        ranges, own = spans(d, t, c0)
                        a, b = hull(ranges)
                        w = wgt[:, m % 3, :]
                        if n == 0 and d == 0:
                            dve.wait_ge(m_score_out, 4 * n_head + 4)
                        E.need(w_exp)
                        last = V.tensor_tensor(w[:, a:b], w[:, a:b], s_sb[:, t, a:b], MUL)
                        if own is not None:
                            C.do(last)
                            C.settle()
                            last = V.tensor_tensor(w[:, own:own + P], w[:, own:own + P],
                                                   c_("upto" if d == 0 else "from"), MUL)
                        last.then_inc(w_ready, 1)
                    elif step == "taken":
                        h, d = i
                        n_head = l * MH + h
                        dve.wait_ge(m_acc, 8 * n_head + 4 * d + 4)
                        E.need(em_out)
                        C.do(V.tensor_tensor(em[:, cols], X[3][:, cols], em[:, cols], ALU.max))
                        C.settle()
                        C.do(V.scalar_tensor_tensor(em[:, cols], X[3][:, cols], -1.0, em[:, cols], MUL, ALU.max))
                        C.settle()
                        C.do(V.reciprocal(em[:, cols], em[:, cols]))
                        C.settle()
                        for j in range(2):
                            last = V.tensor_tensor(wgt[:, j, cols] if d else hacc[:, j, cols], X[j][:, cols], em[:, cols], MUL)
                            if j == 0:
                                C.do(last)
                        last.then_inc(m_taken, 1)
                        if d:
                            dve.wait_ge(m_taken, 2 * n_head + 2)
                            C.settle()
                            for j in range(2):
                                last = V.tensor_tensor(hacc[:, j, cols], hacc[:, j, cols], wgt[:, j, cols], ADD)
                            last.then_inc(head_done, 1)
                    elif step == "hout":
                        dve.wait_ge(tile_out, outs["mo", i])
                        inverse_root(c0, T2)
                        dve.wait_ge(head_done, l * MH + i + 1)
                        for j in range(2):
                            C.do(V.scalar_tensor_tensor(hacc[:, j, cols], hacc[:, j, cols],
                                                        half_w[:, l, 2 * i + j:2 * i + j + 1], sd[:, cols], MUL, MUL))
                        C.settle()
                        for j in range(2):
                            V.scalar_tensor_tensor(hacc[:, j, cols], smo[:, j, cols], 1.0, hacc[:, j, cols], ADD, MUL)\
                                .then_inc(y_rows, 1)
                        for j in range(2):
                            E.need(y_hi_done)
                            last = V.tensor_tensor(y2_lo[:, 2 * i + j, cols], hacc[:, j, cols], y2_hi[:, 2 * i + j, cols], SUB)
                            if j == 0 or i < MH - 1:
                                C.do(last)
                            else:
                                last.then_inc(y_ready, 1)
                for f in range(KD):
                    E.need(merged_hi)
                    V.tensor_tensor(h_lo[:, f, cols], mix[:, f, cols], h_hi[:, f, cols], SUB).then_inc(merged_ready, 1)
                add_gated(2, l, c0, True)
                norm2(1, l, c0)
                dve.wait_ge(h_ready, KD * (DEPTH * 2 + 2 * l + 2))
                V.memset(up[:, :, :, :, :], 0.0).then_inc(up_zero, 1)
                for half in range(2):
                    n0 = NFF * l + FF_HALF * half
                    for t in range(FF_HALF + 2):
                        if t < FF_HALF:
                            E.need(tile_out, 2)
                            b = t % 2
                            if t >= 2:
                                dve.wait_ge(ff2_rows, n0 + t - 1)
                            for tap in range(3):
                                for j in range(2):
                                    y = by_stream(fc[:, b, j, cols])
                                    z = up[:, b, j, first:2, tap:tap + SEQ]
                                    at = j * NFF + half * FF_HALF + t
                                    w = v_("ffn_conv_w_2", l, 2 * NFF * tap + at)
                                    if tap == 0:
                                        C.do(V.tensor_scalar(y, z, w, v_("ffn_conv_b_2", l, at), MUL, ADD))
                                        continue
                                    last = V.scalar_tensor_tensor(y, z, w, y, MUL, ADD)
                                    if tap == 1 or j == 0:
                                        C.do(last)
                                if tap < 2:
                                    C.settle()
                            last.then_inc(fc_rows, 1)
                        if 1 <= t <= FF_HALF:
                            b = (t - 1) % 2
                            E.need(fc_gate)
                            C.settle()
                            if t >= 3:
                                dve.wait_ge(ff2_ready, n0 + t - 2)
                            V.tensor_tensor(fh[:, b, cols], fc[:, b, 0, cols], fc[:, b, 1, cols], MUL).then_inc(ff2_rows, 1)
                        if t >= 2:
                            E.need(ff2_hi)
                            V.tensor_tensor(hid2_lo[:, t - 2, cols], fh[:, t % 2, cols], hid2_hi[:, t - 2, cols], SUB)\
                                .then_inc(ff2_ready, 1)
                    add_gated(5, l, c0, half == 1)


def kernel(**inputs):
    import concourse.bacc as bacc
    from concourse.bass_utils import run_bass_kernel_spmd

    inputs = {k: np.asarray(v) for k, v in inputs.items()}
    cst, decay, masks = constants()

    def rows(a):
        return np.ascontiguousarray(a.T.reshape(KD, P, SEQ).transpose(1, 0, 2))

    arrays = {
        "stream": pack_weights(inputs),
        "vectors": pack_vectors(inputs),
        "consts": cst,
        "decay": decay,
        "gla_masks": masks,
        "positions": np.ascontiguousarray(np.broadcast_to(inputs["positions"].astype(np.int32), (P, SEQ))),
        "x_rows": rows(inputs["x"][0]),
        "ctx_rows": rows(inputs["ctx_2"][0]),
    }
    nc = bacc.Bacc("TRN2", target_bir_lowering=False, num_devices=1)
    args = [nc.dram_tensor(n, a.shape, mybir.dt.from_np(a.dtype), kind="ExternalInput").ap()
            for n, a in arrays.items()]
    out = nc.dram_tensor("out_rows", (P, KD, SEQ), F32, kind="ExternalOutput").ap()
    mixer_stack_kernel(nc, *args, out)
    got = run_bass_kernel_spmd(nc, [arrays], core_ids=[0]).results[0]["out_rows"]
    return np.ascontiguousarray(got.transpose(1, 0, 2).reshape(D, SEQ).T)[None]
```
